# Optimizing a Trainium2 kernel written in Bass

```python
import math
import jax, jax.numpy as jnp
from jax import lax
import numpy as np

D_MODEL = 1024
BATCH = 1
SEQ = 512
DEPTH = 2

EPS = 1e-6
D_FF = 4 * D_MODEL
CONV_CH = D_MODEL // 2
CONV_WIDTH = 31
ATTN_HEAD_DIM = 64
ATTN_HEADS = (D_MODEL // 2) // ATTN_HEAD_DIM
ATTN_WIDTH = ATTN_HEADS * ATTN_HEAD_DIM
MOBA_BLOCK = 256
MOBA_TOP_K = 3
MOBA_Q_CHUNK = 32
AB_IN_WIDTH = 2 * CONV_CH + 3 * ATTN_WIDTH
AB_OUT_WIDTH = CONV_CH + ATTN_WIDTH
LRU_WIDTH = D_MODEL
LRU_HEADS = 8
LRU_BLOCK = LRU_WIDTH // LRU_HEADS
LRU_CONV_WIDTH = 4
LRU_C = 8.0
N_EVEN = (DEPTH + 1) // 2
N_ODD = DEPTH // 2


def rmsnorm(x, g):
    xf = x.astype(jnp.float32)
    y = xf * lax.rsqrt(jnp.mean(xf * xf, axis=-1, keepdims=True) + EPS)
    return (y * g.astype(jnp.float32)).astype(x.dtype)

def layernorm(x, g, b):
    xf = x.astype(jnp.float32)
    mu = jnp.mean(xf, axis=-1, keepdims=True)
    var = jnp.mean(jnp.square(xf - mu), axis=-1, keepdims=True)
    y = (xf - mu) * lax.rsqrt(var + EPS)
    return (y * g.astype(jnp.float32) + b.astype(jnp.float32)).astype(x.dtype)

def causal_depthwise_conv(x, w):
    width, ch = w.shape
    return lax.conv_general_dilated(
        x, w[:, None, :].astype(x.dtype), window_strides=(1,),
        padding=[(width - 1, 0)], dimension_numbers=("NWC", "WIO", "NWC"),
        feature_group_count=ch)

def alibi_slopes(n_heads):
    return 2.0 ** (-8.0 * jnp.arange(1, n_heads + 1, dtype=jnp.float32) / n_heads)

def conformer_conv(u_val, u_gate, conv_w, ln_g, ln_b):
    z = u_val * jax.nn.sigmoid(u_gate)
    z = causal_depthwise_conv(z, conv_w)
    z = layernorm(z, ln_g, ln_b)
    return jax.nn.silu(z)

def moba_attention(q, k, v):
    b, s, h, dh = q.shape
    nb = -(-s // MOBA_BLOCK)
    sp = nb * MOBA_BLOCK
    pad = sp - s
    q, k, v = [jnp.pad(t.transpose(0, 2, 1, 3), ((0, 0), (0, 0), (0, pad), (0, 0)))
               for t in (q, k, v)]
    slopes = alibi_slopes(h)[None, :, None, None]
    scale = dh ** -0.5
    n_past = min(MOBA_TOP_K, nb - 1)
    offs = jnp.arange(MOBA_BLOCK)
    kb = k.reshape(b, h, nb, MOBA_BLOCK, dh)
    vb = v.reshape(b, h, nb, MOBA_BLOCK, dh)
    bi = jnp.arange(b)[:, None, None, None]
    hi = jnp.arange(h)[None, :, None, None]

    if n_past > 0:
        kbar = jnp.mean(kb.astype(jnp.float32), axis=3)
        gate = jnp.einsum("bhsd,bhnd->bhsn", q.astype(jnp.float32), kbar)
        qblk = jnp.arange(sp) // MOBA_BLOCK
        past = jnp.arange(nb)[None, :] < qblk[:, None]
        gate = jnp.where(past, gate, -jnp.inf)
        top_val, top_idx = lax.top_k(gate, n_past)
        top_ok = jnp.isfinite(top_val)

    def chunk(c):
        start = c * MOBA_Q_CHUNK
        t = start + jnp.arange(MOBA_Q_CHUNK)
        qc = lax.dynamic_slice_in_dim(q, start, MOBA_Q_CHUNK, axis=2)
        own0 = (start // MOBA_BLOCK) * MOBA_BLOCK
        k_own = lax.dynamic_slice_in_dim(k, own0, MOBA_BLOCK, axis=2)
        v_own = lax.dynamic_slice_in_dim(v, own0, MOBA_BLOCK, axis=2)
        dist_own = (t[:, None] - (own0 + offs)[None, :]).astype(jnp.float32)
        l_own = (jnp.einsum("bhqd,bhkd->bhqk", qc, k_own).astype(jnp.float32) * scale
                 - slopes * dist_own)
        l_own = jnp.where(dist_own >= 0, l_own, -jnp.inf)
        if n_past > 0:
            idx = lax.dynamic_slice_in_dim(top_idx, start, MOBA_Q_CHUNK, axis=2)
            ok = lax.dynamic_slice_in_dim(top_ok, start, MOBA_Q_CHUNK, axis=2)
            k_sel = kb[bi, hi, idx]
            v_sel = vb[bi, hi, idx]
            pos = idx[..., None] * MOBA_BLOCK + offs
            dist = (t[None, None, :, None, None] - pos).astype(jnp.float32)
            l_sel = (jnp.einsum("bhqd,bhqnkd->bhqnk", qc, k_sel).astype(jnp.float32) * scale
                     - slopes[..., None] * dist)
            l_sel = jnp.where(ok[..., None], l_sel, -jnp.inf)
            n_sel = n_past * MOBA_BLOCK
            logits = jnp.concatenate(
                [l_sel.reshape(b, h, MOBA_Q_CHUNK, n_sel), l_own], axis=-1)
            p = jax.nn.softmax(logits, axis=-1).astype(v.dtype)
            p_sel = p[..., :n_sel].reshape(b, h, MOBA_Q_CHUNK, n_past, MOBA_BLOCK)
            p_own = p[..., n_sel:]
            o = (jnp.einsum("bhqnk,bhqnkd->bhqd", p_sel, v_sel)
                 + jnp.einsum("bhqk,bhkd->bhqd", p_own, v_own))
        else:
            p_own = jax.nn.softmax(l_own, axis=-1).astype(v.dtype)
            o = jnp.einsum("bhqk,bhkd->bhqd", p_own, v_own)
        return o

    out = lax.map(chunk, jnp.arange(sp // MOBA_Q_CHUNK))
    out = out.transpose(1, 2, 0, 3, 4).reshape(b, h, sp, dh)[:, :, :s]
    return out.transpose(0, 2, 1, 3)

def rg_lru(x, w_r, b_r, w_i, b_i, lam):
    b, s, w = x.shape
    xb = x.reshape(b, s, LRU_HEADS, LRU_BLOCK)
    r = jax.nn.sigmoid(jnp.einsum("bshi,hij->bshj", xb, w_r) + b_r).reshape(b, s, w)
    i = jax.nn.sigmoid(jnp.einsum("bshi,hij->bshj", xb, w_i) + b_i).reshape(b, s, w)
    log_a = -LRU_C * r.astype(jnp.float32) * jax.nn.softplus(-lam.astype(jnp.float32))
    a = jnp.exp(log_a)
    mult = jnp.sqrt(-jnp.expm1(2.0 * log_a))
    bx = mult * (i * x).astype(jnp.float32)

    def combine(e1, e2):
        a1, b1 = e1
        a2, b2 = e2
        return a1 * a2, a2 * b1 + b2

    _, hseq = lax.associative_scan(combine, (a, bx), axis=1)
    return hseq.astype(x.dtype)

def mixer_ab(h, w_in, conv_w, ln_g, ln_b, w_out):
    b, s, _ = h.shape
    u = h @ w_in
    u_val, u_gate, q, k, v = jnp.split(
        u, np.cumsum([CONV_CH, CONV_CH, ATTN_WIDTH, ATTN_WIDTH]).tolist(), axis=-1)
    ya = conformer_conv(u_val, u_gate, conv_w, ln_g, ln_b)
    shp = (b, s, ATTN_HEADS, ATTN_HEAD_DIM)
    yb = moba_attention(q.reshape(shp), k.reshape(shp), v.reshape(shp)).reshape(b, s, ATTN_WIDTH)
    return jnp.concatenate([ya, yb], axis=-1) @ w_out

def mixer_c(h, w_in, conv_w, conv_b, w_r, b_r, w_i, b_i, lam, w_out):
    u = h @ w_in
    gate, xr = jnp.split(u, 2, axis=-1)
    xr = causal_depthwise_conv(xr, conv_w) + conv_b
    y = rg_lru(xr, w_r, b_r, w_i, b_i, lam) * jax.nn.gelu(gate)
    return y @ w_out

def sq_relu_mlp(h, w_up, w_down):
    return jnp.square(jax.nn.relu(h @ w_up)) @ w_down

def first_inputs(seed: int = 0) -> dict:
    key = jax.random.key(seed)
    ks = iter(jax.random.split(key, 32))
    f32 = jnp.float32

    def nrm(shape, fan_in):
        return jax.random.normal(next(ks), shape, f32) * (fan_in ** -0.5)

    def gain(shape):
        return 1.0 + 0.02 * jax.random.normal(next(ks), shape, f32)

    def bias(shape):
        return 0.01 * jax.random.normal(next(ks), shape, f32)

    x = jax.random.normal(next(ks), (BATCH, SEQ, D_MODEL), f32)
    a_c = jax.random.uniform(next(ks), (N_ODD, LRU_WIDTH), f32, 0.9, 0.999)
    a_base = a_c ** (1.0 / LRU_C)
    lam = jnp.log(a_base) - jnp.log1p(-a_base)
    return {
        "x": x,
        "mix_norm": gain((DEPTH, D_MODEL)),
        "mlp_norm": gain((DEPTH, D_MODEL)),
        "w_up": nrm((DEPTH, D_MODEL, D_FF), D_MODEL),
        "w_down": nrm((DEPTH, D_FF, D_MODEL), D_FF),
        "ab_w_in": nrm((N_EVEN, D_MODEL, AB_IN_WIDTH), D_MODEL),
        "ab_conv_w": nrm((N_EVEN, CONV_WIDTH, CONV_CH), CONV_WIDTH),
        "ab_ln_g": gain((N_EVEN, CONV_CH)),
        "ab_ln_b": bias((N_EVEN, CONV_CH)),
        "ab_w_out": nrm((N_EVEN, AB_OUT_WIDTH, D_MODEL), AB_OUT_WIDTH),
        "c_w_in": nrm((N_ODD, D_MODEL, 2 * LRU_WIDTH), D_MODEL),
        "c_conv_w": nrm((N_ODD, LRU_CONV_WIDTH, LRU_WIDTH), LRU_CONV_WIDTH),
        "c_conv_b": bias((N_ODD, LRU_WIDTH)),
        "c_w_r": nrm((N_ODD, LRU_HEADS, LRU_BLOCK, LRU_BLOCK), LRU_BLOCK),
        "c_b_r": bias((N_ODD, LRU_HEADS, LRU_BLOCK)),
        "c_w_i": nrm((N_ODD, LRU_HEADS, LRU_BLOCK, LRU_BLOCK), LRU_BLOCK),
        "c_b_i": bias((N_ODD, LRU_HEADS, LRU_BLOCK)),
        "c_lambda": lam,
        "c_w_out": nrm((N_ODD, LRU_WIDTH, D_MODEL), LRU_WIDTH),
        "final_norm": gain((D_MODEL,)),
    }

def first_block(x, mix_norm, mlp_norm, w_up, w_down, ab_w_in, ab_conv_w, ab_ln_g, ab_ln_b,
              ab_w_out, c_w_in, c_conv_w, c_conv_b, c_w_r, c_b_r, c_w_i, c_b_i, c_lambda,
              c_w_out, final_norm):
    for layer in range(DEPTH):
        j = layer // 2
        h = rmsnorm(x, mix_norm[layer])
        if layer % 2 == 0:
            y = mixer_ab(h, ab_w_in[j], ab_conv_w[j], ab_ln_g[j], ab_ln_b[j], ab_w_out[j])
        else:
            y = mixer_c(h, c_w_in[j], c_conv_w[j], c_conv_b[j], c_w_r[j], c_b_r[j],
                        c_w_i[j], c_b_i[j], c_lambda[j], c_w_out[j])
        x = x + y
        x = x + sq_relu_mlp(rmsnorm(x, mlp_norm[layer]), w_up[layer], w_down[layer])
    return rmsnorm(x, final_norm)


CHUNK = 64
N_META = 16
ROPE_THETA = 10000.0
A_HEADS = 4
A_DK = 128
A_DV = 128
A_CONV = 4
B_HEADS = 4
B_DH = 128
IDX_HEADS = 8
IDX_DIM = 64
TOPK_MAX = 256
TOPK_DIV = 4
Q_BLOCK = 64
D_FF_2 = 2816
FFN_CONV = 3

A_WIDTH = A_HEADS * A_DV
B_WIDTH = B_HEADS * B_DH
IN_SPLITS = (A_HEADS * A_DK, A_HEADS * A_DK, A_WIDTH, A_WIDTH, A_HEADS, A_HEADS,
             B_WIDTH, B_DH, B_DH, IDX_HEADS * IDX_DIM, IDX_DIM, IDX_HEADS)
IN_COLS = sum(IN_SPLITS)
SPLIT_POINTS = tuple(int(c) for c in np.cumsum(IN_SPLITS)[:-1])


def rms_norm(x, g):
    xf = x.astype(jnp.float32)
    y = xf * lax.rsqrt(jnp.mean(xf * xf, axis=-1, keepdims=True) + EPS)
    return (y * g.astype(jnp.float32)).astype(x.dtype)

def l2_norm(x):
    xf = x.astype(jnp.float32)
    return xf * lax.rsqrt(jnp.sum(xf * xf, axis=-1, keepdims=True) + EPS)

def rope_tables(T, dim):
    inv_freq = 1.0 / (ROPE_THETA ** (jnp.arange(0, dim, 2, dtype=jnp.float32) / dim))
    ang = jnp.arange(T, dtype=jnp.float32)[:, None] * inv_freq[None, :]
    return jnp.cos(ang), jnp.sin(ang)

def apply_rope(x, cos, sin):
    xf = x.astype(jnp.float32)
    x1, x2 = jnp.split(xf, 2, axis=-1)
    c, s = cos[:, None, :], sin[:, None, :]
    return jnp.concatenate([x1 * c - x2 * s, x2 * c + x1 * s], axis=-1).astype(x.dtype)

def causal_dwconv(x, w):
    width = w.shape[0]
    T = x.shape[1]
    xp = jnp.pad(x, ((0, 0), (width - 1, 0), (0, 0)))
    out = xp[:, 0:T] * w[0]
    for i in range(1, width):
        out = out + xp[:, i:i + T] * w[i]
    return out

def gated_deltanet(q, k, v, z, a, b, conv_w, a_log, dt_bias, norm_g):
    f32 = jnp.float32
    Bsz, T, _ = q.shape
    qkv = jax.nn.silu(causal_dwconv(jnp.concatenate([q, k, v], axis=-1), conv_w))
    q, k, v = jnp.split(qkv, [A_HEADS * A_DK, 2 * A_HEADS * A_DK], axis=-1)
    q = l2_norm(q.reshape(Bsz, T, A_HEADS, A_DK)) * (A_DK ** -0.5)
    k = l2_norm(k.reshape(Bsz, T, A_HEADS, A_DK))
    v = v.reshape(Bsz, T, A_HEADS, A_DV).astype(f32)
    g = -jnp.exp(a_log.astype(f32)) * jax.nn.softplus(a.astype(f32) + dt_bias.astype(f32))
    beta = jax.nn.sigmoid(b.astype(f32))
    pad = (-T) % CHUNK
    Tp = T + pad
    N = Tp // CHUNK

    def chunks(t):
        t = jnp.pad(t, ((0, 0), (pad, 0)) + ((0, 0),) * (t.ndim - 2))
        t = t.reshape((Bsz, N, CHUNK) + t.shape[2:])
        return jnp.moveaxis(t, 3, 1)

    qc, kc, vc, gch, bc = chunks(q), chunks(k), chunks(v), chunks(g), chunks(beta)
    gcum = jnp.cumsum(gch, axis=-1)
    pos = jnp.arange(CHUNK)
    incl = pos[:, None] >= pos[None, :]
    strict = pos[:, None] > pos[None, :]
    decay = jnp.exp(jnp.where(incl, gcum[..., :, None] - gcum[..., None, :], -jnp.inf))
    kk = jnp.einsum('bhncd,bhnsd->bhncs', kc, kc)
    m = jnp.where(strict, bc[..., None] * kk * decay, 0.0)
    lhs = m + jnp.eye(CHUNK, dtype=f32)
    rhs = jnp.concatenate([vc * bc[..., None], kc * (bc * jnp.exp(gcum))[..., None]], axis=-1)
    sol = lax.linalg.triangular_solve(lhs, rhs, left_side=True, lower=True, unit_diagonal=True)
    u, w = sol[..., :A_DV], sol[..., A_DV:]
    qk = jnp.einsum('bhncd,bhnsd->bhncs', qc, kc) * decay

    def step(S, inp):
        q_c, k_c, u_c, w_c, g_c, qk_c = inp
        v_new = u_c - jnp.einsum('bhcd,bhde->bhce', w_c, S)
        o = (jnp.einsum('bhcd,bhde->bhce', q_c * jnp.exp(g_c)[..., None], S)
             + jnp.einsum('bhcs,bhse->bhce', qk_c, v_new))
        g_last = g_c[..., -1]
        S = (S * jnp.exp(g_last)[..., None, None]
             + jnp.einsum('bhcd,bhce->bhde', k_c * jnp.exp(g_last[..., None] - g_c)[..., None], v_new))
        return S, o

    xs = tuple(jnp.moveaxis(t, 2, 0) for t in (qc, kc, u, w, gcum, qk))
    S0 = jnp.zeros((Bsz, A_HEADS, A_DK, A_DV), f32)
    _, o = lax.scan(step, S0, xs)
    o = jnp.transpose(o, (1, 0, 3, 2, 4)).reshape(Bsz, Tp, A_HEADS, A_DV)[:, pad:]
    o = rms_norm(o, norm_g) * jax.nn.silu(z.reshape(Bsz, T, A_HEADS, A_DV).astype(f32))
    return o.reshape(Bsz, T, A_WIDTH).astype(z.dtype)

def dsa_attention(q, k, v, iq, ik, iw, q_norm, k_norm, kidx_norm, cos_a, sin_a, cos_i, sin_i):
    f32 = jnp.float32
    Bsz, T, _ = q.shape
    S = T - N_META
    topk = min(TOPK_MAX, S // TOPK_DIV)
    q = apply_rope(rms_norm(q.reshape(Bsz, T, B_HEADS, B_DH), q_norm), cos_a, sin_a)
    k = apply_rope(rms_norm(k.reshape(Bsz, T, 1, B_DH), k_norm), cos_a, sin_a)[:, :, 0]
    iq = apply_rope(iq.reshape(Bsz, T, IDX_HEADS, IDX_DIM), cos_i, sin_i)
    ik = apply_rope(rms_norm(ik.reshape(Bsz, T, 1, IDX_DIM), kidx_norm), cos_i, sin_i)[:, :, 0]
    iw = iw * (IDX_HEADS ** -0.5 * IDX_DIM ** -0.5)
    scale = B_DH ** -0.5

    q_m, k_m, v_m = q[:, :N_META], k[:, :N_META], v[:, :N_META]
    s_mm = jnp.einsum('bqhd,bkd->bhqk', q_m, k_m).astype(f32) * scale
    o_meta = jnp.einsum('bhqk,bkd->bqhd', jax.nn.softmax(s_mm, axis=-1).astype(v.dtype), v_m)

    nb = S // Q_BLOCK
    q_r = q[:, N_META:].reshape(Bsz, nb, Q_BLOCK, B_HEADS, B_DH).swapaxes(0, 1)
    iq_r = iq[:, N_META:].reshape(Bsz, nb, Q_BLOCK, IDX_HEADS, IDX_DIM).swapaxes(0, 1)
    iw_r = iw[:, N_META:].reshape(Bsz, nb, Q_BLOCK, IDX_HEADS).swapaxes(0, 1)
    ik_r = ik[:, N_META:]
    kv_r = jnp.concatenate([k[:, N_META:], v[:, N_META:]], axis=-1)
    key_pos = jnp.arange(S)

    def one_block(args):
        j, qb, iqb, iwb = args
        q_pos = j * Q_BLOCK + jnp.arange(Q_BLOCK)
        limit = (q_pos // CHUNK + 1) * CHUNK
        valid = key_pos[None, :] < limit[:, None]
        logit_i = jnp.einsum('bqhd,bsd->bhqs', iqb, ik_r)
        score = jnp.einsum('bhqs,bqh->bqs', jax.nn.relu(logit_i), iwb).astype(f32)
        score = jnp.where(valid[None], score, -jnp.inf)
        _, sel = lax.top_k(score, topk)
        sel_valid = sel < limit[None, :, None]
        kv_sel = jax.vmap(lambda arr, ix: arr[ix])(kv_r, sel)
        k_sel, v_sel = kv_sel[..., :B_DH], kv_sel[..., B_DH:]
        s_meta = jnp.einsum('bqhd,bmd->bhqm', qb, k_m).astype(f32)
        s_sel = jnp.einsum('bqhd,bqkd->bhqk', qb, k_sel).astype(f32)
        s_sel = jnp.where(sel_valid[:, None], s_sel, -jnp.inf)
        p = jax.nn.softmax(jnp.concatenate([s_meta, s_sel], axis=-1) * scale, axis=-1).astype(v.dtype)
        return (jnp.einsum('bhqm,bmd->bqhd', p[..., :N_META], v_m)
                + jnp.einsum('bhqk,bqkd->bqhd', p[..., N_META:], v_sel))

    o_r = lax.map(one_block, (jnp.arange(nb), q_r, iq_r, iw_r))
    o_r = o_r.swapaxes(0, 1).reshape(Bsz, S, B_HEADS, B_DH)
    return jnp.concatenate([o_meta, o_r], axis=1).reshape(Bsz, T, B_WIDTH)

def hybrid_mixer(n, w_in, conv_a, a_log, dt_bias, a_out_norm, q_norm, k_norm, kidx_norm,
                 w_branch_a, w_branch_b, w_gate, b_gate, w_out, cos_a, sin_a, cos_i, sin_i):
    Bsz, T, D = n.shape
    proj = n @ w_in
    aq, ak, av, az, aa, ab, bq, bk, bv, iq, ik, iw = jnp.split(proj, SPLIT_POINTS, axis=-1)
    o_a = gated_deltanet(aq, ak, av, az, aa, ab, conv_a, a_log, dt_bias, a_out_norm)
    o_b = dsa_attention(bq, bk, bv, iq, ik, iw, q_norm, k_norm, kidx_norm, cos_a, sin_a, cos_i, sin_i)
    gates = jax.nn.sigmoid(n @ w_gate + b_gate).reshape(Bsz, T, 2, D)
    y = gates[:, :, 0] * (o_a @ w_branch_a) + gates[:, :, 1] * (o_b @ w_branch_b)
    return y @ w_out

def conv_gated_mlp(n, w_up, conv_w, w_down):
    gate, up = jnp.split(n @ w_up, 2, axis=-1)
    gate = causal_dwconv(gate, conv_w)
    return (jax.nn.silu(gate) * up) @ w_down

def second_inputs(seed: int = 0) -> dict:
    key = jax.random.key(seed)
    ks = jax.random.split(key, 24)
    L, D = DEPTH, D_MODEL
    f32 = jnp.float32

    def nrm(k, shape, scale):
        return jax.random.normal(k, shape, f32) * scale

    def gain(k, shape):
        return 1.0 + nrm(k, shape, 0.02)

    a_init = jax.random.uniform(ks[5], (L, A_HEADS), f32, 1.0, 16.0)
    dt = jnp.exp(jax.random.uniform(ks[6], (L, A_HEADS), f32, math.log(1e-3), math.log(1e-1)))
    return {
        "x": nrm(ks[0], (BATCH, SEQ, D), 1.0),
        "meta_tokens": nrm(ks[1], (N_META, D), 0.5),
        "norm_mix": gain(ks[2], (L, D)),
        "w_in": nrm(ks[3], (L, D, IN_COLS), D ** -0.5),
        "conv_a": nrm(ks[4], (L, A_CONV, 2 * A_HEADS * A_DK + A_WIDTH), 0.5),
        "a_log": jnp.log(a_init),
        "dt_bias": dt + jnp.log(-jnp.expm1(-dt)),
        "a_out_norm": gain(ks[7], (L, A_DV)),
        "q_norm": gain(ks[8], (L, B_DH)),
        "k_norm": gain(ks[9], (L, B_DH)),
        "kidx_norm": gain(ks[10], (L, IDX_DIM)),
        "w_branch_a": nrm(ks[11], (L, A_WIDTH, D), A_WIDTH ** -0.5),
        "w_branch_b": nrm(ks[12], (L, B_WIDTH, D), B_WIDTH ** -0.5),
        "w_gate": nrm(ks[13], (L, D, 2 * D), D ** -0.5),
        "b_gate": nrm(ks[14], (L, 2 * D), 0.1),
        "w_out": nrm(ks[15], (L, D, D), D ** -0.5),
        "norm_ffn": gain(ks[16], (L, D)),
        "w_up": nrm(ks[17], (L, D, 2 * D_FF_2), D ** -0.5),
        "conv_ffn": nrm(ks[18], (L, FFN_CONV, D_FF_2), 0.5),
        "w_down": nrm(ks[19], (L, D_FF_2, D), D_FF_2 ** -0.5),
    }

def second_block(x, meta_tokens, norm_mix, w_in, conv_a, a_log, dt_bias, a_out_norm, q_norm, k_norm,
              kidx_norm, w_branch_a, w_branch_b, w_gate, b_gate, w_out, norm_ffn, w_up, conv_ffn,
              w_down) -> jnp.ndarray:
    Bsz = x.shape[0]
    T = N_META + x.shape[1]
    cos_a, sin_a = rope_tables(T, B_DH)
    cos_i, sin_i = rope_tables(T, IDX_DIM)
    meta = jnp.broadcast_to(meta_tokens.astype(x.dtype)[None], (Bsz, N_META, x.shape[2]))
    h = jnp.concatenate([meta, x], axis=1)
    for l in range(DEPTH):
        n = rms_norm(h, norm_mix[l])
        h = h + hybrid_mixer(n, w_in[l], conv_a[l], a_log[l], dt_bias[l], a_out_norm[l], q_norm[l],
                             k_norm[l], kidx_norm[l], w_branch_a[l], w_branch_b[l], w_gate[l], b_gate[l],
                             w_out[l], cos_a, sin_a, cos_i, sin_i).astype(h.dtype)
        n = rms_norm(h, norm_ffn[l])
        h = h + conv_gated_mlp(n, w_up[l], conv_ffn[l], w_down[l]).astype(h.dtype)
    return h[:, N_META:]


def setup_inputs(seed=0):
    out = dict(first_inputs(seed))
    for name, value in second_inputs(seed + 1).items():
        if name != "x":
            out[name + "_2"] = value
    return out


def reference(
    x, mix_norm, mlp_norm, w_up, w_down, ab_w_in, ab_conv_w, ab_ln_g, ab_ln_b, ab_w_out, c_w_in,
    c_conv_w, c_conv_b, c_w_r, c_b_r, c_w_i, c_b_i, c_lambda, c_w_out, final_norm,
    meta_tokens_2, norm_mix_2, w_in_2, conv_a_2, a_log_2, dt_bias_2, a_out_norm_2, q_norm_2,
    k_norm_2, kidx_norm_2, w_branch_a_2, w_branch_b_2, w_gate_2, b_gate_2, w_out_2, norm_ffn_2,
    w_up_2, conv_ffn_2, w_down_2,
):
    x = first_block(
        x, mix_norm, mlp_norm, w_up, w_down, ab_w_in, ab_conv_w, ab_ln_g, ab_ln_b, ab_w_out,
        c_w_in, c_conv_w, c_conv_b, c_w_r, c_b_r, c_w_i, c_b_i, c_lambda, c_w_out, final_norm,
    )
    return second_block(
        x, meta_tokens_2, norm_mix_2, w_in_2, conv_a_2, a_log_2, dt_bias_2, a_out_norm_2,
        q_norm_2, k_norm_2, kidx_norm_2, w_branch_a_2, w_branch_b_2, w_gate_2, b_gate_2,
        w_out_2, norm_ffn_2, w_up_2, conv_ffn_2, w_down_2,
    )


_drawn_inputs = setup_inputs


def setup_inputs(seed=0):
    import zlib

    import numpy as np

    out = dict(_drawn_inputs(seed))
    spreads = {}
    factors = {'ab_ln_g': 3.021,
     'ab_ln_b': 5.101,
     'c_b_r': 8.0,
     'c_b_i': 8.0,
     'a_out_norm_2': 5.944,
     'q_norm_2': 8.0,
     'k_norm_2': 8.0,
     'kidx_norm_2': 5.868,
     'norm_ffn_2': 2.877}
    for name, (base, spread) in spreads.items():
        noise = np.random.default_rng([zlib.crc32(name.encode()), seed]).standard_normal(out[name].shape)
        drawn = base * np.exp(spread * noise) if base else spread * noise
        out[name] = __import__('jax').numpy.asarray(drawn.astype(out[name].dtype))
    for name, factor in factors.items():
        out[name] = (out[name] * factor).astype(out[name].dtype)
    return out
```

```python
import math
from contextlib import ExitStack

import concourse.bass as bass
from concourse import mybir

F32 = mybir.dt.float32
F32R = mybir.dt.float32r
ALU = mybir.AluOpType
ACT = mybir.ActivationFunctionType
AX = mybir.AxisListType

P = 128
D = 1024
KT = D // P
SEQ = 512
META = 16
T = SEQ + META
HALF = T // 2
EPS = 1e-6
BIG = 1e30

CONV_CH = 512
CONV_W = 31
HEADS = 8
DH = 64
AB_IN = 2560
LRU_HEADS = 8
LRU_W = 4
FF = 4096
QUARTERS = FF // D

A_HEADS = 4
B_HEADS = 4
IDX_HEADS = 8
FF2 = 2816
FT2 = FF2 // P
SPLITS = (512, 512, 512, 512, 4, 4, 512, 128, 128, 512, 64, 8)
AQ, AK, AV, AZ, AA, AB_, BQ, BK, BV, IQ, IK, IW = (sum(SPLITS[:n]) for n in range(12))
TOPK = 128
CHUNK = 64
UNITS = 5

TOP_GATES = 4
UNIT_JOBS = A_HEADS + KT - TOP_GATES
BRANCHES = 24 + UNIT_JOBS + TOP_GATES

RAW_SLOTS = 4
W_SLOTS = 4
AHEAD = 3


def mlp_order():
    order = [("up", 0)]
    for q in range(QUARTERS):
        if q + 1 < QUARTERS:
            order.append(("up", q + 1))
        order.append(("down", q))
    return order


FFN_THIRDS = [(0, 8), (8, 16), (16, FT2)]
FFN_ORDER = [("up", 0), ("up", 1), ("down", 0), ("up", 2), ("down", 1), ("down", 2)]


STAGES = ["mix0", "mlp0", "mix1", "mlp1", "final", "layer0", "layer1"]


def weight_plan():
    plan = []

    def column(name, layer, col, rows=range(KT)):
        plan.append((name, layer, [(P * r, col, P) for r in rows]))

    def mixer0():
        for i in range(4):
            column("ab_w_in", 0, CONV_CH + P * i)
            column("ab_w_in", 0, P * i)
        for m in range(8, 20):
            column("ab_w_in", 0, P * m)
        for m in range(KT):
            column("ab_w_out", 0, P * m)

    def mixer1():
        for m in range(KT):
            column("c_w_in", 0, D + P * m)
        for m in range(KT):
            column("c_w_in", 0, P * m)
        for m in range(KT):
            column("c_w_out", 0, P * m)

    def mlp(layer):
        for what, q in mlp_order():
            for m in range(KT):
                if what == "up":
                    column("w_up", layer, D * q + P * m)
                else:
                    column("w_down", layer, P * m, range(KT * q, KT * q + KT))

    def block2(layer):
        plan.append(("w_in_2", layer, [(P * r, "ab_iw", 16) for r in range(KT)]))
        plan.append(("w_in_2", layer, [(P * r, "ik_twice", P) for r in range(KT)]))
        for c in (IQ, BQ):
            for i in range(4):
                column("w_in_2", layer, c + P * i)
        column("w_in_2", layer, BK)
        column("w_in_2", layer, BV)
        for h in range(A_HEADS):
            for c in (AK, AQ, AV):
                column("w_in_2", layer, c + P * h)
        for m in range(TOP_GATES):
            column("w_gate_2", layer, P * m)
        for h in range(A_HEADS):
            column("w_in_2", layer, AZ + P * h)
        for m in range(TOP_GATES, KT):
            column("w_gate_2", layer, P * m)
        for m in range(KT):
            column("w_gate_2", layer, D + P * m)
            plan.append(("w_branch_2", layer, [(P * r, P * m, P) for r in range(KT)]))
        for m in range(KT):
            column("w_out_2", layer, P * m)
        for what, g in FFN_ORDER:
            a, b = FFN_THIRDS[g]
            if what == "up":
                for i in range(a, b):
                    column("w_up_2", layer, P * i)
                    column("w_up_2", layer, FF2 + P * i)
            else:
                for m in range(KT):
                    column("w_down_2", layer, P * m, range(a, b))

    make = {"mix0": mixer0, "mix1": mixer1, "mlp0": lambda: mlp(0), "mlp1": lambda: mlp(1),
            "final": lambda: None, "layer0": lambda: block2(0), "layer1": lambda: block2(1)}
    starts = {}
    for stage in STAGES:
        starts[stage] = len(plan)
        make[stage]()
    return plan, starts


PAD = 4
LEVELS = 6
TILES4 = 4 * T * 4
SEL_AT = [0]
for _j in range(4):
    SEL_AT.append(SEL_AT[-1] + META + P * (_j + 1))
MARK = -3e38


class Counts:

    def __init__(self):
        self.seen = {}
        self.latest = None

    def made(self, sem):
        self.seen[sem.name] = self.seen.get(sem.name, 0) + 1
        self.latest = (sem, self.seen[sem.name])
        return 1

    def mine(self):
        return self.latest

    def next(self, sem, n=1):
        self.seen[sem.name] = self.seen.get(sem.name, 0) + n
        return self.seen[sem.name]

    def at(self, sem):
        return self.seen.get(sem.name, 0)


class Area:

    def __init__(self, nc, start, end):
        self.nc, self.at, self.end = nc, start, end

    def take(self, name, shape, dtype=F32):
        size = 4 * math.prod(shape[1:])
        at = self.at
        self.at = at + -(-size // 32) * 32
        assert self.at <= self.end, (name, self.at, self.end)
        return self.nc.alloc_sbuf_tensor_at(name, shape, dtype, offset=at)


VEC1 = [("mix_norm", 16), ("mlp_norm", 16), ("final_norm", 8), ("ab_conv_w", 4 * CONV_W),
        ("ab_ln_g", 4), ("ab_ln_b", 4), ("c_conv_w", KT * LRU_W), ("c_conv_b", 8),
        ("c_b_r", 8), ("c_b_i", 8), ("c_lambda", 8)]
VEC2 = [("norm_mix_2", 8), ("norm_ffn_2", 8), ("conv_a_2", 48), ("a_log_2", 4), ("dt_bias_2", 4),
        ("a_out_norm_2", 1), ("q_norm_2", 1), ("k_norm_2", 1), ("kidx_norm_2", 1),
        ("b_gate_2", 16), ("conv_ffn_2", 66)]
CONST1 = [("ident", P), ("ones", P)]
CONST2 = [("cos_a", T), ("sin_a", T), ("cos_i", T), ("sin_i", T), ("turn_a", P), ("turn_i", P),
          ("until", P), ("same", P), ("strict", P), ("ahead", P)] + [(f"join_{n}", P) for n in range(LEVELS)] + [("rows", 64), ("is_meta", 8)]


def columns(table):
    out, at = {}, 0
    for name, n in table:
        out[name] = (at, at + n)
        at += n
    return out, at


V1, NV1 = columns(VEC1)
V2, NV2 = columns(VEC2)
C1, NC1 = columns(CONST1)
C2, NC2 = columns(CONST2)


def fill_blocks(u, n):
    level = (LEVELS - 1) * u + n - 1
    job, third = divmod(level, 3)
    return job, third, ((1, 2), (1, 2), (1, 1))[third] if job < UNIT_JOBS else (0, 0)


def build(nc, stream, xt, vec1, vec2, const1, const2, dist, lru_w, meta, saved_x, out):
    plan, starts = weight_plan()
    pieces = len(plan)
    base = -(-nc.sbuf_base // 64) * 64
    fixed = Area(nc, base, nc.sbuf_usable_end)
    x = fixed.take("x", [P, KT, T])
    nh = fixed.take("n_hi", [P, KT, T], F32R)
    nl = fixed.take("n_lo", [P, KT, T], F32R)
    raw = fixed.take("w_raw", [P, RAW_SLOTS, KT * P])
    wh = fixed.take("w_hi", [P, W_SLOTS, KT * P], F32R)
    wl = fixed.take("w_lo", [P, W_SLOTS, KT * P], F32R)
    scale = fixed.take("norm_scale", [P, T])
    ssq = fixed.take("square_sum", [P, T])
    sqb = fixed.take("squares", [P, 2, T])
    ubp = fixed.take("unit_a", [P, 2, T + PAD])
    ub = ubp[:, :, PAD:]
    sb_ = fixed.take("unit_b", [P, 2, T])
    rt = fixed.take("root", [P, T])
    v1 = fixed.take("vec1", [P, NV1])
    v2 = fixed.take("vec2", [P, 2, NV2])
    c1 = fixed.take("const1", [P, NC1])
    ident = c1[:, C1["ident"][0]:C1["ident"][1]]
    ones = c1[:, C1["ones"][0]:C1["ones"][1]]

    def const(name):
        return c2[:, C2[name][0]:C2[name][1]]

    def vec2_(layer, name, n=0, count=1):
        return v2[:, layer, V2[name][0] + n:V2[name][0] + n + count]

    def vec(name, n=0):
        return v1[:, V1[name][0] + n:V1[name][0] + n + 1]

    eps = fixed.take("eps", [P, 8])
    area = fixed.at
    end = nc.sbuf_usable_end // 64 * 64 - 4 * NC2 - 64
    c2 = Area(nc, end, nc.sbuf_usable_end).take("const2", [P, NC2])
    mlp = Area(nc, area, end)
    hid_hi = mlp.take("hidden_hi", [P, 2, KT, T], F32R)
    hid_lo = mlp.take("hidden_lo", [P, 2, KT, T], F32R)

    m0 = Area(nc, area, end)
    distance = m0.take("distance", [P, SEQ])[:, :]
    zpad = m0.take("z_padded", [P, 4, CONV_W - 1 + SEQ])
    cv = m0.take("conv_out", [P, 4, SEQ])
    qs = m0.take("queries", [P, 4, SEQ])
    ks = m0.take("keys", [P, 4, SEQ])
    vs = m0.take("values", [P, 4, SEQ])
    vt = m0.take("values_by_token", [P, 4, SEQ])
    bias = m0.take("alibi", [P, 2, SEQ])
    sm = m0.take("softmax", [P, 2, SEQ])
    pt = m0.take("probs_t", [P, 2, SEQ])
    small = m0.take("row_values", [P, 8, 2])

    m1 = Area(nc, area, end)
    gb = m1.take("gate", [P, KT, SEQ])
    xc = m1.take("lru_in", [P, KT, SEQ])
    rb = m1.take("lru_a", [P, KT, SEQ])
    tb = m1.take("lru_b", [P, KT, SEQ])
    lw = m1.take("lru_weights", [P, 2 * LRU_HEADS, P])
    c8 = m1.take("lru_rate", [P, 6, KT])

    A = area
    dq = Area(nc, A, end).take("delta_q", [P, A_HEADS, T])
    dz = Area(nc, A + TILES4, end).take("delta_z", [P, A_HEADS, T])
    dk = Area(nc, A + 2 * TILES4, end).take("delta_k", [P, A_HEADS, T])
    dv = Area(nc, A + 3 * TILES4, end).take("delta_v", [P, A_HEADS, T])
    W = A + 4 * TILES4
    iq = Area(nc, W, end).take("index_q", [P, 4, T])
    pb = Area(nc, W, end).take("probs", [P, 4, T])
    bq = Area(nc, W + TILES4, end).take("attn_q", [P, 4, T])
    ob = Area(nc, W + 2 * TILES4, end).take("attn_out", [P, 4, T])
    score = Area(nc, W + 2 * TILES4, end).take("index_score", [P, 3, SEQ])
    rest = Area(nc, W + 3 * TILES4, end)
    ik = rest.take("index_k", [P, T])
    bk = rest.take("attn_k", [P, T])
    bv = rest.take("attn_v", [P, T])
    selb = rest.take("select_bias", [P, SEL_AT[4]])
    vtok = rest.take("attn_v_by_token", [P, UNITS, P])
    rest.at = W + 3 * TILES4 + 7 * 4 * A_HEADS * P
    abt = rest.take("rates", [P, UNITS, 16])
    gt = rest.take("gates_by_token", [P, 10, UNITS * A_HEADS])
    rtok = rest.take("scale_by_token", [P, 8])
    best = rest.take("best8", [P, 3, 8])
    row4 = rest.take("row_values2", [P, 4, 4])
    lo_part = Area(nc, W, W + 2 * TILES4)
    hi_part = Area(nc, W + 3 * TILES4, end)
    names = ["decay_t", "exp_g_row", "qk_t", "q_g", "m_t", "c_t", "inv", "inv_t"]
    dt, egr, qkt, qg, mt, ct, xi, xit = (lo_part.take(n, [P, A_HEADS, P]) for n in names)
    names = ["p1", "k_beta_g", "k_g", "v_beta", "w_t", "v_new", "state"]
    p1, kbg, kg, vb, nwt, vn, state = (hi_part.take(n, [P, A_HEADS, P]) for n in names)
    assert hi_part.at <= W + 3 * TILES4 + 7 * 2048
    oh = Area(nc, A + 2 * TILES4, end).take("out_hi", [P, KT, T], F32R)
    ol = Area(nc, W, end).take("out_lo", [P, KT, T], F32R)
    yh = Area(nc, A, end).take("mixed_hi", [P, KT, T], F32R)
    yl = Area(nc, W + 2 * TILES4, end).take("mixed_lo", [P, KT, T], F32R)

    acc = nc.alloc_psum_tensor("acc", [P, 4, 512], F32)
    aux = nc.alloc_psum_tensor("aux", [P, 4, 512], F32)

    def sem(name):
        return nc.alloc_semaphore(name)

    landed = [sem(f"w_landed_{n}") for n in range(RAW_SLOTS)]
    loaded = sem("tables_landed")
    lru_landed = sem("lru_weights_landed")
    stored = sem("output_stored")
    w_hi, w_lo, w_used = sem("w_hi_ready"), sem("w_lo_ready"), sem("w_piece_used")
    taken = sem("acc_taken")
    act_seq, dve_seq = sem("act_steps"), sem("dve_steps")
    sq_ready, sq_added, ss_full, root_ready = sem("square_ready"), sem("square_added"), sem("square_sum_full"), sem("root_ready")
    n_hi, n_ready = sem("n_hi_ready"), sem("n_ready")
    h_sq, h_hi, h_ready = sem("hidden_ready"), sem("hidden_hi_ready"), sem("hidden_lo_ready")
    sig_ready = sem("sigmoid_ready")
    pad_clear = sem("pads_clear")
    conv_ready = sem("conv_ready")
    mean_full, cent_ready, var_full, ln_root = sem("mean_full"), sem("centred"), sem("variance_full"), sem("ln_root")
    ln_sq = sem("ln_square")
    ln_scaled, ln_act, ln_out, y_hi, y_ready = sem("ln_scaled"), sem("ln_affine"), sem("ln_out"), sem("y_hi_ready"), sem("y_ready")
    vt_full, vt_copied = sem("v_turned"), sem("v_copied")
    s_full, s_shift, s_exp, p_ready = sem("scores_full"), sem("scores_shifted"), sem("scores_exp"), sem("probs_ready")
    pt_full, pt_ready, o_full = sem("probs_turned"), sem("probs_t_ready"), sem("attn_out_full")
    xc_ready, ri_full, ri_sig, tanh_ready = sem("lru_conv_ready"), sem("lru_gates_full"), sem("lru_sigmoid"), sem("lru_tanh")
    g_ready, gsig_ready = sem("gelu_inner"), sem("gelu_sigmoid")
    xc_gated, x_final = sem("lru_input_gated"), sem("x_final")
    a_ready, m_ready, mult_ready, yc_ready = sem("lru_decay"), sem("lru_square"), sem("lru_mult"), sem("lru_out")
    rate_in, rate_ready = sem("lru_rate_exp"), sem("lru_rate_ready")

    scale_ready, rtok_full = sem("norm_scale_ready"), sem("token_scale_full")
    dsq_ready, dsq_used, dsum_full = sem("head_square_ready"), sem("head_square_used"), sem("head_sums_full")
    droot_ready, dinv_ready, gained = sem("head_roots_ready"), sem("head_scales_ready"), sem("gained")
    raw_ready = sem("projected")
    rot_full, rope_done = sem("turned_full"), sem("rope_done")
    is_full, irelu, iscore = sem("index_logits_full"), sem("index_relu"), sem("index_added")
    vtok_full, vtok_ready = sem("v_tokens_full"), sem("v_tokens_ready")
    bs_full, bshift, bexp, bp_ready = sem("dsa_scores_full"), sem("dsa_shifted"), sem("dsa_exp"), sem("dsa_probs")
    bt_full, bt_ready, bo_full, bo_ready = sem("dsa_turned"), sem("dsa_probs_t"), sem("dsa_out_full"), sem("dsa_out_taken")
    csig, silu_in, silu_out = sem("silu_sigmoid"), sem("silu_in"), sem("silu_out")
    abe_in, abe_out = sem("rates_in"), sem("rates_exp")
    g_in, gcol_full = sem("decay_logs"), sem("decay_sums")
    lbc_full, lnormed = sem("l2_scale_full"), sem("l2_normed")
    ugb_full, udt, udt_exp, ukq_full = sem("row_values_full"), sem("decay_diff"), sem("decay_exp"), sem("products_full")
    egr_ready = sem("exp_g_row_ready")
    ux_ready, ux_full, ux_copied = sem("join0_ready"), sem("join0_turned"), sem("join0_copied")
    utok_full, utok_ready, uq_ready = sem("tokens_full"), sem("tokens_scaled"), sem("query_side_ready")
    uct_ready, up1_full, up1_ready = sem("join_block_ready"), sem("join_half_full"), sem("join_half_ready")
    uz_full, uinv_ready, uw_full, uw_ready = sem("join_full"), sem("join_done"), sem("w_full"), sem("w_ready")
    uv_full, uv_ready, uso_full, us_ready, uo_done = sem("v_new_full"), sem("v_new_ready"), sem("step_full"), sem("state_ready"), sem("step_out_taken")
    onorm_ready, o_in, oz_ready, o_hi, o_ready = sem("out_normed"), sem("out_in"), sem("out_gated"), sem("out_hi_ready"), sem("out_lo_ready")
    gate_sig, mix_ready, mix_hi, mix_lo = sem("gate_sigmoid"), sem("mixed"), sem("mixed_hi"), sem("mixed_lo")
    meta_landed = sem("meta_landed")
    x_saved, gate_kept = sem("x_saved"), sem("first_gate_ready")
    x_back = [sem(f"x_back_{m}") for m in range(KT)]

    def first(u):
        return META + P * (u - 1) if u else 0

    def wide(a):
        return a.rearrange("p (s t) -> p s t", s=2)

    ROW = slice(META, T)

    def pieces_of(p):
        return len(plan[p][2])

    def pair_of(p):
        for l in range(2):
            first_job = starts.get(f"layer{l}", pieces) + 24 + TOP_GATES
            if first_job <= p < first_job + UNIT_JOBS:
                return 0
        return p % 2

    block = nc.Block()
    block.__enter__()

    @block.sync
    def _(sp):
        c = Counts()
        sp.dma_start(c1[:, :], const1).then_inc(loaded, 16)
        sp.dma_start(v1[:, :], vec1).then_inc(loaded, 16)
        sp.dma_start(x[:, :, ROW], xt.rearrange("(k p) t -> p k t", p=P)).then_inc(loaded, 16)
        sp.dma_start(distance, dist).then_inc(loaded, 16)
        if "layer0" in STAGES:
            sp.dma_start(x[:, :, 0:META], meta.rearrange("(k p) t -> p k t", p=P)).then_inc(meta_landed, 16)
            sp.dma_start(v2[:, :, :], vec2).then_inc(meta_landed, 16)
            sp.dma_start(c2[:, :], const2).then_inc(meta_landed, 16)

        def save_x(l):
            norms = 4 + 2 * l if "mix0" in STAGES else 2 * l
            sp.wait_ge(n_ready, KT * (norms + 1))
            sp.dma_start(saved_x.rearrange("(k p) t -> p k t", p=P), x[:, :, :]).then_inc(x_saved, 16)
            sp.wait_ge(x_saved, 16 * (l + 1))

        def restore_x(l, m):
            sp.wait_ge(mix_ready, KT * l + m + 1)
            sp.dma_start(x[:, m, :], saved_x[P * m:P * m + P, :]).then_inc(x_back[m], 16)

        also = {}
        for l in range(2):
            if f"layer{l}" in starts:
                first_piece = starts[f"layer{l}"]
                also[first_piece + RAW_SLOTS] = (save_x, l)
                for m in range(KT):
                    also[first_piece + BRANCHES + 2 * m + 7] = (restore_x, l, m)

        for p in range(pieces):
            if p >= RAW_SLOTS:
                sp.wait_ge(w_lo, p - RAW_SLOTS + 1)
            n = pieces_of(p)
            sp.dma_start(raw[:, p % RAW_SLOTS, 0:n * P], stream[p, :, 0:n * P])\
                .then_inc(landed[p % RAW_SLOTS], 16)
            if p in also:
                also[p][0](*also[p][1:])
            if p == starts.get("mix1", -9) + 3:
                sp.wait_ge(taken, starts["mix1"])
                sp.dma_start(lw[:, :, :], lru_w).then_inc(lru_landed, 16)
        for k in range(KT):
            if STAGES[-1] == "final":
                sp.wait_ge(x_final, k + 1)
            else:
                sp.wait_ge(taken, pieces - KT + k + 1)
            sp.dma_start(out[P * k:P * k + P, :], x[:, k, ROW]).then_inc(stored, 16)
        sp.wait_ge(stored, 16 * KT)

    @block.gpsimd
    def _(pool):
        for p in range(pieces):
            n = pieces_of(p) * P
            pool.wait_ge(w_hi, p + 1)
            pool.tensor_tensor(wl[:, p % W_SLOTS, 0:n], raw[:, p % RAW_SLOTS, 0:n],
                               wh[:, p % W_SLOTS, 0:n].bitcast(F32), ALU.subtract).then_inc(w_lo, 1)

    @block.tensor
    def _(pe):
        c = Counts()
        at = {"piece": 0, "both": False, "block": 0}

        def product(job, hi, lo, cols, wait=None):
            p = at["piece"]
            pe.wait_ge(w_lo, p + 1)
            one = cols == SEQ
            slots = 4 if one else 2
            if job >= slots:
                pe.wait_ge(taken, job if at["both"] else job - slots + 1)
            at["both"] = False
            n, last = pieces_of(p), None
            for b in range(n):
                if wait is not None:
                    pe.wait_ge(wait, c.next(wait))
                for i, (w, v) in enumerate(((wh, hi), (wh, lo), (wl, hi))):
                    for s in range(1 if one else 2):
                        o = acc[:, job % 4, :] if one else acc[:, 2 * pair_of(job) + s, 0:HALF]
                        r = v[:, b, ROW] if one else v[:, b, HALF * s:HALF * s + HALF]
                        last = pe.matmul(o, w[:, p % W_SLOTS, P * b:P * b + P], r,
                                         start=(b == 0 and i == 0), stop=(b == n - 1 and i == 2))
            last.then_inc(w_used, 1)
            at["piece"] = p + 1

        def square_sum(cols):
            pe.wait_ge(sq_added, c.next(sq_added, KT))
            if cols == SEQ:
                pe.matmul(aux[:, 0, :], ones, ssq[:, ROW], start=True, stop=True).then_inc(ss_full, 1)
            else:
                pe.matmul(aux[:, 0, 0:HALF], ones, ssq[:, 0:HALF], start=True, stop=True)
                pe.matmul(aux[:, 1, 0:HALF], ones, ssq[:, HALF:T], start=True, stop=True)\
                    .then_inc(ss_full, 1)

        def jobs(n, cols=SEQ, fresh=False, hi=nh, lo=nl):
            for i in range(n):
                product(at["piece"], hi, lo, cols, n_ready if fresh and i == 0 else None)

        def mixer0():
            square_sum(SEQ)
            jobs(20, fresh=True)
            pe.wait_ge(root_ready, c.next(root_ready))
            pe.wait_ge(conv_ready, c.next(conv_ready, 4))
            for i in range(4):
                mm = pe.matmul(aux[:, 1, :], ones, cv[:, i, :], start=(i == 0), stop=(i == 3))
            mm.then_inc(mean_full, 1)
            pe.wait_ge(taken, at["piece"])
            for a in range(4):
                if a >= 2:
                    pe.wait_ge(vt_copied, a - 1)
                for i in range(4):
                    mm = pe.transpose(aux[:, 2 + a % 2, P * i:P * i + P], vs[:, i, P * a:P * a + P], ident)
                mm.then_inc(vt_full, 1)
            for i in range(4):
                pe.wait_ge(ln_sq, c.next(ln_sq))
                mm = pe.matmul(aux[:, 0, :], ones, zpad[:, i, 0:SEQ], start=(i == 0), stop=(i == 3))
            mm.then_inc(var_full, 1)
            pe.wait_ge(vt_copied, c.next(vt_copied, 4))
            pe.wait_ge(ln_root, c.next(ln_root))

            def turn(u):
                h, i = divmod(u, 4)
                pe.wait_ge(p_ready, u + 1)
                if u >= 2:
                    pe.wait_ge(pt_ready, u - 1)
                for b in range(i + 1):
                    mm = pe.transpose(aux[:, 2 + u % 2, P * b:P * b + P], sm[:, u % 2, P * b:P * b + P], ident)
                mm.then_inc(pt_full, 1)

            def values(u):
                h, i = divmod(u, 4)
                po, pair = DH * (h % 2), h // 2
                pe.wait_ge(pt_ready, u + 1)
                if pair >= 2:
                    pe.wait_ge(y_ready, 4 + pair - 1)
                for b in range(i + 1):
                    mm = pe.matmul(acc[po:po + DH, pair % 2, P * i:P * i + P],
                                   vt[:, b, DH * h:DH * h + DH], pt[:, u % 2, P * b:P * b + P],
                                   start=(b == 0), stop=(b == i))
                mm.then_inc(o_full, 1)

            for u in range(4 * HEADS + 2):
                if u < 4 * HEADS:
                    h, i = divmod(u, 4)
                    po, w = DH * (h % 2), P * (i + 1)
                    if u >= 2:
                        pe.wait_ge(s_shift, u - 1)
                    pe.matmul(aux[:, u % 2, 0:w], qs[po:po + DH, h // 2, P * i:P * i + P],
                              ks[po:po + DH, h // 2, 0:w], start=True, stop=True).then_inc(s_full, 1)
                if 1 <= u <= 4 * HEADS:
                    turn(u - 1)
                if u >= 2:
                    values(u - 2)
            pe.wait_ge(y_ready, c.next(y_ready, 8))
            jobs(KT)

        def mixer1():
            square_sum(SEQ)
            jobs(KT, fresh=True)
            pe.wait_ge(root_ready, c.next(root_ready))
            pe.wait_ge(lru_landed, 16)
            for h in range(KT):
                jobs(1)
                pe.wait_ge(xc_ready, h + 1)
                if h >= 2:
                    pe.wait_ge(ri_sig, h - 1)
                for g in range(2):
                    mm = pe.matmul(aux[:, 2 * (h % 2) + g, :], lw[:, LRU_HEADS * g + h, :], xc[:, h, :],
                                   start=True, stop=True)
                mm.then_inc(ri_full, 1)
            pe.wait_ge(ri_sig, KT)
            pe.wait_ge(y_ready, c.next(y_ready, KT))
            jobs(KT)

        def mlp1():
            square_sum(SEQ)
            made = 0
            for n, (what, q) in enumerate(mlp_order()):
                if what == "up":
                    jobs(KT, fresh=(n == 0))
                    if n == 0:
                        pe.wait_ge(root_ready, c.next(root_ready))
                else:
                    pe.wait_ge(h_ready, c.next(h_ready, KT))
                    jobs(KT, hi=hid_hi[:, q % 2], lo=hid_lo[:, q % 2])

        def rows_sum(n, count, which):
            pe.wait_ge(dsq_ready, c.next(dsq_ready))
            for s in range(2):
                mm = pe.matmul(aux[0:8, s, 0:HALF], const("rows")[:, 8 * n:8 * n + 8],
                               sqb[:, which % 2, HALF * s:HALF * s + HALF], start=(n == 0), stop=(n == count - 1))
            mm.then_inc(dsq_used if n < count - 1 else dsum_full, 1)

        def spread(n, pair):
            for s in range(2):
                mm = pe.matmul(aux[:, 2 * pair + s, 0:HALF], ident[0:8, n:n + 1].to_broadcast([8, P]),
                               rt[0:8, HALF * s:HALF * s + HALF], start=True, stop=True)
            return mm

        def layer(l):
            square_sum(T)
            pe.wait_ge(n_ready, c.next(n_ready, KT))
            p = at["piece"]
            pe.wait_ge(w_lo, p + 1)
            if p:
                pe.wait_ge(taken, p)
            for u in range(UNITS):
                for b in range(KT):
                    for i, (w, v) in enumerate(((wh, nh), (wh, nl), (wl, nh))):
                        mm = pe.matmul(acc[:, 2 * (p % 2), 16 * u:16 * u + 16], v[:, b, first(u):first(u) + P],
                                       w[:, p % W_SLOTS, P * b:P * b + 16],
                                       start=(b == 0 and i == 0), stop=(b == KT - 1 and i == 2))
            mm.then_inc(w_used, 1)
            at["piece"] = p + 1
            jobs(1, T)
            pe.wait_ge(root_ready, c.next(root_ready))
            pe.wait_ge(scale_ready, c.at(root_ready))
            for u in range(UNITS):
                mm = pe.matmul(aux[:, 2, u:u + 1], scale[0:1, first(u):first(u) + P], ones[0:1, 0:1],
                               start=True, stop=True)
            mm.then_inc(rtok_full, 1)
            jobs(10, T)
            for n in range(6):
                rows_sum(n, 6, n)
            jobs(2, T)
            pe.wait_ge(dinv_ready, c.next(dinv_ready))
            pe.wait_ge(gained, c.next(gained, 6))
            tiles = [(ik[:, :], "turn_i", 0)] + [(iq[:, i, :], "turn_i", None) for i in range(4)] \
                + [(bq[:, i, :], "turn_a", 1 + i) for i in range(4)] + [(bk[:, :], "turn_a", 5)]
            for n, (t, turn, row) in enumerate(tiles):
                if n:
                    pe.wait_ge(rope_done, c.next(rope_done))
                for s in range(2):
                    mm = pe.matmul(aux[:, s, 0:HALF], const(turn), t[:, HALF * s:HALF * s + HALF],
                                   start=True, stop=True)
                if row is not None:
                    mm = spread(row, 1)
                mm.then_inc(rot_full, 1)
                jobs(1, T)
            pe.wait_ge(rope_done, c.next(rope_done))
            n = 0
            base = c.at(irelu)
            for j in range(1, 4):
                for h in range(IDX_HEADS):
                    if n >= 4:
                        pe.wait_ge(irelu, base + n - 3)
                    po, w = 64 * (h % 2), P * (j + 1)
                    pe.matmul(aux[:, n % 4, 0:w], iq[po:po + 64, h // 2, META + P * j:META + P * j + P],
                              ik[po:po + 64, META:META + w], start=True, stop=True).then_inc(is_full, 1)
                    n += 1
            pe.wait_ge(irelu, c.next(irelu, n))
            for u in range(UNITS):
                mm = pe.transpose(aux[:, u // 4, P * (u % 4):P * (u % 4) + P], bv[:, first(u):first(u) + P], ident)
            mm.then_inc(vtok_full, 1)
            pe.wait_ge(vtok_ready, c.next(vtok_ready))
            for n in range(8):
                rows_sum(n, 8, n)
            jobs(1, T)
            pe.wait_ge(dinv_ready, c.next(dinv_ready))
            base = c.at(lnormed)
            for n in range(8):
                if n >= 2:
                    pe.wait_ge(lnormed, base + n - 1)
                spread(n, n % 2).then_inc(lbc_full, 1)
                if n in (1, 3, 5):
                    jobs(1, T)
            pe.wait_ge(lnormed, c.next(lnormed, 8))
            pe.wait_ge(g_in, c.next(g_in))
            pe.matmul(aux[:, 0, 0:20], const("until"), gt[:, 1, :], start=True, stop=True)
            pe.matmul(aux[:, 0, 32:52], const("same"), gt[:, 1, :], start=True, stop=True).then_inc(gcol_full, 1)
            pe.wait_ge(g_in, c.next(g_in))
            pe.wait_ge(taken, at["piece"])
            attention()
            for u in range(UNITS):
                unit(u)
            pe.wait_ge(us_ready, c.next(us_ready))
            for n in range(4):
                rows_sum(n, 4, n)
            pe.wait_ge(dinv_ready, c.next(dinv_ready))
            base = c.at(onorm_ready)
            for n in range(4):
                if n >= 2:
                    pe.wait_ge(onorm_ready, base + n - 1)
                spread(n, n % 2).then_inc(lbc_full, 1)
            pe.wait_ge(onorm_ready, c.next(onorm_ready, 4))
            pe.wait_ge(o_ready, c.next(o_ready, 8))
            for m in range(KT):
                jobs(1, T)
                branch()
            pe.wait_ge(mix_lo, c.next(mix_lo, KT))
            jobs(KT, T, hi=yh, lo=yl)
            square_sum(T)
            for n, (what, g) in enumerate(FFN_ORDER):
                a, b = FFN_THIRDS[g]
                if what == "up":
                    jobs(2 * (b - a), T, fresh=(n == 0))
                    if n == 0:
                        pe.wait_ge(root_ready, c.next(root_ready))
                else:
                    pe.wait_ge(h_ready, c.next(h_ready, b - a))
                    jobs(KT, T, hi=hid_hi[:, g % 2], lo=hid_lo[:, g % 2])

        def branch():
            p = at["piece"]
            pe.wait_ge(w_lo, p + 1)
            pe.wait_ge(taken, p)
            for g in range(2):
                for b in range(4 * g, 4 * g + 4):
                    for i, (w, v) in enumerate(((wh, oh), (wh, ol), (wl, oh))):
                        for s in range(2):
                            mm = pe.matmul(acc[:, 2 * g + s, 0:HALF], w[:, p % W_SLOTS, P * b:P * b + P],
                                           v[:, b, HALF * s:HALF * s + HALF],
                                           start=(b == 4 * g and i == 0), stop=(b == 4 * g + 3 and i == 2))
            mm.then_inc(w_used, 1)
            at["piece"] = p + 1
            at["both"] = True

        def fill(blocks):
            p = at["piece"]
            if blocks and at["block"] == 0:
                pe.wait_ge(w_lo, p + 1)
                pe.wait_ge(taken, p)
            for _ in range(blocks):
                b = at["block"]
                for i, (w, v) in enumerate(((wh, nh), (wh, nl), (wl, nh))):
                    for s in range(2):
                        mm = pe.matmul(acc[:, s, 0:HALF], w[:, p % W_SLOTS, P * b:P * b + P],
                                       v[:, b, HALF * s:HALF * s + HALF],
                                       start=(b == 0 and i == 0), stop=(b == KT - 1 and i == 2))
                at["block"] = b + 1
            if at["block"] == KT:
                mm.then_inc(w_used, 1)
                at.update(piece=p + 1, block=0, both=True)

        def heads(bank, make):
            for h in range(A_HEADS):
                mm = make(bank[:, P * h:P * h + P], h)
            return mm

        def mm_(out, lhs, rhs, start=True, stop=True):
            return pe.matmul(out, lhs, rhs, start=start, stop=stop)

        def unit(u):
            cs = slice(first(u), first(u) + P)
            heads(aux[:, 0, :], lambda o, h: mm_(o, gt[:, 1, 4 * u + h:4 * u + h + 1].to_broadcast([P, P]), const("until")))
            heads(aux[:, 1, :], lambda o, h: mm_(o, gt[:, 0, 4 * u + h:4 * u + h + 1].to_broadcast([P, P]), ident))\
                .then_inc(ugb_full, 1)
            heads(aux[:, 2, :], lambda o, h: mm_(o, dk[:, h, cs], dk[:, h, cs]))
            heads(aux[:, 3, :], lambda o, h: mm_(o, dk[:, h, cs], dq[:, h, cs])).then_inc(ukq_full, 1)
            heads(acc[:, 2, :], lambda o, h: pe.transpose(o, dk[:, h, cs], ident))
            heads(acc[:, 3, :], lambda o, h: pe.transpose(o, dv[:, h, cs], ident)).then_inc(utok_full, 1)
            pe.wait_ge(ux_ready, c.next(ux_ready))
            heads(aux[:, 0, :], lambda o, h: pe.transpose(o, xit[:, h, :], ident)).then_inc(ux_full, 1)
            pe.wait_ge(ux_copied, c.next(ux_copied))
            for n in range(1, LEVELS):
                pe.wait_ge(uct_ready, c.next(uct_ready))
                heads(aux[:, 0, :], lambda o, h: mm_(o, ct[:, h, :], xi[:, h, :])).then_inc(up1_full, 1)
                fill(fill_blocks(u, n)[2][0])
                pe.wait_ge(up1_ready, c.next(up1_ready))
                mm = heads(aux[:, 2, :], lambda o, h: mm_(o, p1[:, h, :], xit[:, h, :]))
                if n < LEVELS - 1:
                    mm = heads(aux[:, 1, :], lambda o, h: mm_(o, xit[:, h, :], p1[:, h, :]))
                mm.then_inc(uz_full, 1)
                fill(fill_blocks(u, n)[2][1])
                pe.wait_ge(uinv_ready, c.next(uinv_ready))
            pe.wait_ge(utok_ready, c.next(utok_ready))
            heads(acc[:, 2, :], lambda o, h: mm_(o, kbg[:, h, :], xit[:, h, :])).then_inc(uw_full, 1)
            pe.wait_ge(uw_ready, c.next(uw_ready))
            pe.wait_ge(uq_ready, c.next(uq_ready))
            for cc in range(1 if u == 0 else 2):
                r = slice(64 * cc, 64 * cc + 64)
                pe.wait_ge(us_ready, c.next(us_ready))
                for h in range(A_HEADS):
                    o = aux[r, 0, P * h:P * h + P]
                    mm_(o, xit[:, h, r], vb[:, h, :], True, False)
                    mm = mm_(o, nwt[:, h, r], state[:, h, :], False, True)
                mm.then_inc(uv_full, 1)
                pe.wait_ge(uv_ready, c.next(uv_ready))
                for h in range(A_HEADS):
                    o = aux[:, 3, P * h + 64 * cc:P * h + 64 * cc + 64]
                    mm_(o, state[:, h, :], qg[:, h, r], True, False)
                    mm_(o, vn[r, h, :], qkt[r, h, r], False, True)
                    mm = mm_(aux[:, 1, P * h:P * h + P], kg[r, h, :], vn[r, h, :])
                mm.then_inc(uso_full, 1)
            pe.wait_ge(uo_done, c.next(uo_done))

        def attention():
            n, t = 0, 0
            shifted, turned, outs = c.at(bshift), c.at(bt_ready), c.at(bo_ready)
            for j in range(4):
                w = META + P * (j + 1)
                for h in range(B_HEADS):
                    if n >= 2:
                        pe.wait_ge(bshift, shifted + n - 1)
                    for s in range(2):
                        mm = pe.matmul(aux[:, 2 * (h % 2) + s, 0:w // 2], bq[:, h, META + P * j:META + P * j + P],
                                       bk[:, s * (w // 2):(s + 1) * (w // 2)], start=True, stop=True)
                    mm.then_inc(bs_full, 1)
                    n += 1
                pe.wait_ge(bp_ready, c.next(bp_ready, 4))
                for b in range(j + 3):
                    if b < j + 2:
                        rows = P if b else META
                        if t + b >= 2:
                            pe.wait_ge(bt_ready, turned + t + b - 1)
                        for h in range(B_HEADS):
                            mm = pe.transpose(acc[0:rows, (t + b) % 2, P * h:P * h + P],
                                              pb[:, h, first(b):first(b) + rows], ident)
                        mm.then_inc(bt_full, 1)
                    if b == 0:
                        if j >= 2:
                            pe.wait_ge(bo_ready, outs + j - 1)
                        continue
                    v, rows = b - 1, P if b > 1 else META
                    pe.wait_ge(bt_ready, turned + t + v + 1)
                    mm = pe.matmul(acc[:, 2 + j % 2, :], vtok[0:rows, v, :], sb_[0:rows, (t + v) % 2, 0:512],
                                   start=(v == 0), stop=(v == j + 1))
                t += j + 2
                mm.then_inc(bo_full, 1)
            pe.wait_ge(bshift, c.next(bshift, n))
            for h in range(B_HEADS):
                mm = pe.matmul(aux[0:META, 0, META * h:META * h + META], bq[:, h, 0:META], bk[:, 0:META],
                               start=True, stop=True)
            mm.then_inc(bs_full, 1)
            pe.wait_ge(bp_ready, c.next(bp_ready))
            c.next(bshift)
            c.next(bt_ready, t)
            pe.wait_ge(bt_ready, c.at(bt_ready))
            for h in range(B_HEADS):
                mm = pe.transpose(acc[0:META, 0, META * h:META * h + META], pb[0:META, h, 0:META], ident[0:META, 0:META])
            mm.then_inc(bt_full, 1)
            pe.wait_ge(bt_ready, c.next(bt_ready))
            pe.wait_ge(bo_ready, c.next(bo_ready, 4))
            pe.matmul(acc[:, 2, 0:4 * META], vtok[0:META, 0, :], sb_[0:META, 0, 0:4 * META],
                      start=True, stop=True).then_inc(bo_full, 1)
            pe.wait_ge(bo_ready, c.next(bo_ready))

        for stage in STAGES:
            if stage == "mix0":
                mixer0()
            if stage == "mix1":
                mixer1()
            if stage in ("mlp0", "mlp1"):
                mlp1()
            if stage == "final":
                square_sum(SEQ)
                pe.wait_ge(root_ready, c.next(root_ready))
            if stage in ("layer0", "layer1"):
                layer(int(stage[-1]))

    @block.scalar
    def _(act):
        c = Counts()
        at = {"piece": 0, "split": 0}

        def split(p):
            while at["split"] <= min(p, pieces - 1):
                q = at["split"]
                act.wait_ge(landed[q % RAW_SLOTS], 16 * (q // RAW_SLOTS + 1))
                if q >= W_SLOTS:
                    act.wait_ge(w_used, q - W_SLOTS + 1)
                n = pieces_of(q) * P
                act.activation(wh[:, q % W_SLOTS, 0:n], raw[:, q % RAW_SLOTS, 0:n], ACT.Copy)\
                    .then_inc(w_hi, 1)
                at["split"] = q + 1

        def job():
            p = at["piece"]
            split(p + AHEAD)
            at["piece"] = p + 1
            return p

        def norm(gains, cols, first=False, after=None):
            split(at["piece"] + AHEAD)
            s = ROW if cols == SEQ else slice(0, T)
            if at["piece"]:
                act.wait_ge(w_used, at["piece"])
            for k in range(KT):
                if after is not None:
                    act.wait_ge(after, c.next(after))
                elif not first:
                    act.wait_ge(taken, at["piece"] - KT + k + 1)
                if k >= 2:
                    act.wait_ge(sq_added, c.at(sq_added) + k - 1)
                act.activation(sqb[:, k % 2, s], x[:, k, s], ACT.Square).then_inc(sq_ready, c.made(sq_ready))
                if gains is not None:
                    act.activation(nh[:, k, s], x[:, k, s], ACT.Copy, scale=gains(k)).then_inc(n_hi, c.made(n_hi))
            c.next(sq_added, KT)
            root(cols)

        def root(cols):
            act.wait_ge(ss_full, c.next(ss_full))
            if cols == SEQ:
                act.activation(rt[:, ROW], aux[:, 0, :], ACT.Sqrt, scale=1.0 / D, bias=eps[:, 0:1])\
                    .then_inc(root_ready, c.made(root_ready))
            else:
                act.activation(rt[:, :].rearrange("p (s t) -> p s t", s=2), aux[:, 0:2, 0:HALF], ACT.Sqrt,
                               scale=1.0 / D, bias=eps[:, 0:1]).then_inc(root_ready, c.made(root_ready))

        def mixer0():
            norm(lambda k: vec("mix_norm", k), SEQ, first=True)
            for i in range(4):
                p = job()
                act.wait_ge(taken, p + 1)
                act.activation(sb_[:, i % 2, 0:SEQ], ub[:, i % 2, 0:SEQ], ACT.Sigmoid)\
                    .then_inc(sig_ready, c.made(sig_ready))
                job()
            for _ in range(12):
                job()
            for a in range(4):
                act.wait_ge(vt_full, c.next(vt_full))
                act.activation(vt[:, a, :], aux[:, 2 + a % 2, :], ACT.Copy).then_inc(vt_copied, c.made(vt_copied))
            for i in range(4):
                act.wait_ge(cent_ready, c.next(cent_ready))
                act.activation(zpad[:, i, 0:SEQ], cv[:, i, :], ACT.Square).then_inc(ln_sq, c.made(ln_sq))
            act.wait_ge(var_full, c.next(var_full))
            act.activation(rt[:, 0:SEQ], aux[:, 0, :], ACT.Sqrt, scale=1.0 / CONV_CH, bias=eps[:, 0:1])\
                .then_inc(ln_root, c.made(ln_root))
            for i in range(4):
                act.wait_ge(ln_scaled, c.next(ln_scaled))
                act.activation(zpad[:, i, 0:SEQ], cv[:, i, :], ACT.Identity, scale=vec("ab_ln_g", i),
                               bias=vec("ab_ln_b", i)).then_inc(act_seq, c.made(act_seq))
                act.activation(cv[:, i, :], cv[:, i, :], ACT.Sigmoid, scale=vec("ab_ln_g", i),
                               bias=vec("ab_ln_b", i)).then_inc(ln_act, c.made(ln_act))
            for i in range(4):
                act.wait_ge(ln_out, c.next(ln_out))
                act.activation(nh[:, i, ROW], zpad[:, i, 0:SEQ], ACT.Copy).then_inc(y_hi, c.made(y_hi))

            def copy_probs(u):
                act.wait_ge(pt_full, u + 1)
                if u >= 2:
                    act.wait_ge(o_full, u - 1)
                w = P * (u % 4 + 1)
                act.activation(pt[:, u % 2, 0:w], aux[:, 2 + u % 2, 0:w], ACT.Copy).then_inc(pt_ready, c.made(pt_ready))

            def heads_out(pair):
                act.wait_ge(o_full, 8 * pair + 8)
                act.activation(nh[:, 4 + pair, ROW], acc[:, pair % 2, :], ACT.Copy).then_inc(y_hi, c.made(y_hi))

            for u in range(4 * HEADS + 3):
                if u < 4 * HEADS:
                    act.wait_ge(s_shift, u + 1)
                    w, b = P * (u % 4 + 1), u % 2
                    act.activation(sm[:, b, 0:w], sm[:, b, 0:w], ACT.Exp, bias=small[:, 1, b:b + 1],
                                   accum_out=small[:, 2, b:b + 1]).then_inc(s_exp, c.made(s_exp))
                if 1 <= u <= 4 * HEADS:
                    copy_probs(u - 1)
                if u >= 3 and (u - 3) % 8 == 7:
                    heads_out((u - 3) // 8)
            for _ in range(KT):
                job()

        def mixer1():
            act.wait_ge(rate_in, 1)
            act.activation(c8[:, 1, :], c8[:, 0, :], ACT.Exp, scale=-1.0).then_inc(rate_ready, c.made(rate_ready))
            norm(lambda k: vec("mix_norm", 8 + k), SEQ)
            for _ in range(KT):
                job()
            act.wait_ge(rate_in, 2)
            for h in range(KT):
                job()
                act.wait_ge(g_ready, c.next(g_ready))
                act.activation(sb_[:, h % 2, 0:SEQ], sb_[:, h % 2, 0:SEQ], ACT.Sigmoid,
                               scale=2.0 * math.sqrt(2.0 / math.pi)).then_inc(gsig_ready, c.made(gsig_ready))
                act.wait_ge(ri_full, c.next(ri_full))
                act.activation(rb[:, h, :], aux[:, 2 * (h % 2), :], ACT.Sigmoid, bias=vec("c_b_r", h))\
                    .then_inc(act_seq, c.made(act_seq))
                done = c.mine()
                if h >= 2:
                    act.wait_ge(xc_gated, h - 1)
                act.activation(ub[:, h % 2, 0:SEQ], aux[:, 2 * (h % 2) + 1, :], ACT.Sigmoid, bias=vec("c_b_i", h))\
                    .then_inc(ri_sig, c.made(ri_sig))
                act.wait_ge(*done)
                act.activation(tb[:, h, :], rb[:, h, :], ACT.Tanh, scale=c8[:, 2, h:h + 1])\
                    .then_inc(tanh_ready, c.made(tanh_ready))
            for h in range(KT):
                act.activation(rb[:, h, :], rb[:, h, :], ACT.Exp, scale=c8[:, 3, h:h + 1])\
                    .then_inc(a_ready, c.made(a_ready))
            for h in range(KT):
                act.wait_ge(m_ready, c.next(m_ready))
                act.activation(tb[:, h, :], tb[:, h, :], ACT.Sqrt).then_inc(mult_ready, c.made(mult_ready))
            act.wait_ge(w_used, at["piece"])
            for h in range(KT):
                act.wait_ge(yc_ready, c.next(yc_ready))
                act.activation(nh[:, h, ROW], xc[:, h, :], ACT.Copy).then_inc(y_hi, c.made(y_hi))
            for _ in range(KT):
                job()

        def mlp1(layer):
            norm(lambda k: vec("mlp_norm", 8 * layer + k), SEQ)
            for what, q in mlp_order():
                for m in range(KT):
                    p = job()
                    if what == "up":
                        act.wait_ge(h_sq, c.next(h_sq))
                        act.activation(hid_hi[:, q % 2, m, ROW], sb_[:, m % 2, 0:SEQ], ACT.Copy)\
                            .then_inc(h_hi, c.made(h_hi))

        def square_rows(tiles, gains=None):
            base = c.at(dsq_used)
            for n, (t, ready) in enumerate(tiles):
                if ready is not None:
                    act.wait_ge(*ready)
                if n >= 2:
                    act.wait_ge(dsq_used, base + n - 1)
                act.activation(sqb[:, n % 2, :], t, ACT.Square).then_inc(dsq_ready, c.made(dsq_ready))
                if gains is not None:
                    act.activation(t, t, ACT.Copy, scale=gains[n]).then_inc(gained, c.made(gained))
            c.next(dsq_used, len(tiles) - 1)

        def row_roots(factor):
            act.wait_ge(dsum_full, c.next(dsum_full))
            act.activation(wide(rt[0:8, :]), aux[0:8, 0:2, 0:HALF], ACT.Sqrt, scale=factor, bias=eps[0:8, 0:1])\
                .then_inc(droot_ready, c.made(droot_ready))

        def layer(l):
            def vec(name, n=0, count=1):
                return vec2_(l, name, n, count)

            def gate_tile(m, p):
                act.wait_ge(taken, p + 1)
                act.activation(x[:, m, :], x[:, m, :], ACT.Sigmoid, bias=vec("b_gate_2", m))\
                    .then_inc(gate_kept, c.made(gate_kept))

            if l == 0:
                act.wait_ge(meta_landed, 48)
            norm(lambda k: vec("norm_mix_2", k), T, after=x_final if l == 0 else None)
            p0 = at["piece"]
            for _ in range(12):
                job()
            tiles = [(ik[:, :], (taken, p0 + 2))] + [(bq[:, i, :], (taken, p0 + 7 + i)) for i in range(4)] \
                + [(bk[:, :], (taken, p0 + 11))]
            square_rows(tiles, [vec("kidx_norm_2")] + [vec("q_norm_2")] * 4 + [vec("k_norm_2")])
            row_roots(1.0 / P)
            act.wait_ge(abe_in, c.next(abe_in))
            act.activation(gt[:, 4, :], gt[:, 3, :], ACT.Exp, scale=-1.0).then_inc(act_seq, c.made(act_seq))
            act.activation(gt[:, 9, 0:4], vec("a_log_2", 0, 4), ACT.Exp).then_inc(act_seq, c.made(act_seq))
            act.activation(gt[:, 0, :].rearrange("p (u h) -> p u h", h=4), abt[:, :, 4:8], ACT.Sigmoid)\
                .then_inc(abe_out, c.made(abe_out))
            for n in range(12):
                job()
                t = ((dk, dq, dv)[n % 3])[:, n // 3, :]
                act.wait_ge(silu_in, c.next(silu_in))
                if n >= 2:
                    act.wait_ge(silu_out, c.at(silu_out) + n - 1)
                act.activation(sb_[:, n % 2, :], t, ACT.Sigmoid).then_inc(csig, c.made(csig))
            n = 0
            base = c.at(iscore)
            for j in range(1, 4):
                for h in range(IDX_HEADS):
                    w = P * (j + 1)
                    act.wait_ge(is_full, c.next(is_full))
                    if n >= 2:
                        act.wait_ge(iscore, base + n - 1)
                    act.activation(sqb[:, n % 2, 0:w], aux[:, n % 4, 0:w], ACT.Relu).then_inc(irelu, c.made(irelu))
                    n += 1
            c.next(iscore, n)
            c.next(silu_out, 12)
            act.wait_ge(vtok_full, c.next(vtok_full))
            act.activation(vtok[:, 0:4, :], aux[:, 0, :].rearrange("p (u d) -> p u d", u=4), ACT.Copy)\
                .then_inc(act_seq, c.made(act_seq))
            act.activation(vtok[:, 4, :], aux[:, 1, 0:P], ACT.Copy).then_inc(vtok_ready, c.made(vtok_ready))
            act.wait_ge(silu_out, c.at(silu_out))
            act.wait_ge(iscore, c.at(iscore))
            square_rows([(dq[:, h, :], None) for h in range(4)] + [(dk[:, h, :], None) for h in range(4)])
            row_roots(1.0)
            for m in range(TOP_GATES):
                gate_tile(m, job())
            act.wait_ge(abe_in, c.next(abe_in))
            act.activation(gt[:, 5, :], gt[:, 3, :], ACT.Exp).then_inc(act_seq, c.made(act_seq))
            act.activation(gt[:, 6, :], gt[:, 4, :], ACT.Exp).then_inc(abe_out, c.made(abe_out))
            attention()
            for u in range(UNITS):
                unit(u, gate_tile)
            c.next(silu_out, A_HEADS)
            c.next(uo_done, UNITS)
            square_rows([(dq[:, h, :], (uo_done, c.at(uo_done))) for h in range(4)])
            row_roots(1.0 / P)
            for h in range(4):
                act.wait_ge(oz_ready, c.next(oz_ready))
                act.activation(oh[:, h, :], dq[:, h, :], ACT.Copy).then_inc(o_hi, c.made(o_hi))
            for h in range(4):
                act.activation(oh[:, 4 + h, :], ob[:, h, :], ACT.Copy).then_inc(o_hi, c.made(o_hi))
            for m in range(KT):
                p = job()
                act.wait_ge(taken, p + 1)
                act.activation(sb_[:, m % 2, :], ub[:, m % 2, :], ACT.Sigmoid, bias=vec("b_gate_2", KT + m))\
                    .then_inc(gate_sig, c.made(gate_sig))
                job()
                act.wait_ge(mix_ready, c.next(mix_ready))
                act.activation(yh[:, m, :], sqb[:, 0, :], ACT.Copy).then_inc(mix_hi, c.made(mix_hi))
            for _ in range(KT):
                job()
            norm(lambda k: vec("norm_ffn_2", k), T)
            for what, g in FFN_ORDER:
                a, b = FFN_THIRDS[g]
                if what == "down":
                    for _ in range(KT):
                        job()
                    continue
                for i in range(a, b):
                    job()
                    act.wait_ge(silu_in, c.next(silu_in))
                    act.activation(sqb[:, i % 2, :], sb_[:, i % 2, :], ACT.Sigmoid).then_inc(csig, c.made(csig))
                    job()
                    act.wait_ge(h_sq, c.next(h_sq))
                    act.activation(hid_hi[:, g % 2, i - a, :], sb_[:, i % 2, :], ACT.Copy).then_inc(h_hi, c.made(h_hi))

        def flat(t):
            return t[:, :, :].rearrange("p h i -> p (h i)")

        def fill_sigmoid(f, gate_tile):
            p = at["filled"] + f
            if f >= A_HEADS:
                gate_tile(TOP_GATES + f - A_HEADS, p)
                return
            act.wait_ge(taken, p + 1)
            if f >= 2:
                act.wait_ge(silu_out, c.at(silu_out) + f - 1)
            act.activation(sb_[:, f % 2, :], dz[:, f, :], ACT.Sigmoid).then_inc(csig, c.made(csig))

        def unit(u, gate_tile):
            act.wait_ge(ugb_full, c.next(ugb_full))
            act.activation(flat(egr), aux[:, 0, :], ACT.Exp).then_inc(egr_ready, c.made(egr_ready))
            act.wait_ge(udt, c.next(udt))
            act.activation(flat(dt), flat(dt), ACT.Exp).then_inc(udt_exp, c.made(udt_exp))
            act.wait_ge(ux_full, c.next(ux_full))
            act.activation(flat(xi), aux[:, 0, :], ACT.Copy).then_inc(ux_copied, c.made(ux_copied))
            for n in range(1, LEVELS):
                f, third, _ = fill_blocks(u, n)
                if third == 0 and f < UNIT_JOBS:
                    p = job()
                    if f == 0:
                        at["filled"] = p
                act.wait_ge(up1_full, c.next(up1_full))
                act.activation(flat(p1), aux[:, 0, :], ACT.Copy).then_inc(up1_ready, c.made(up1_ready))
                if third == 0 and f > 0:
                    fill_sigmoid(f - 1, gate_tile)
            act.wait_ge(uw_full, c.next(uw_full))
            act.activation(flat(nwt), acc[:, 2, :], ACT.Copy, scale=-1.0).then_inc(uw_ready, c.made(uw_ready))
            for cc in range(1 if u == 0 else 2):
                r = slice(64 * cc, 64 * cc + 64)
                act.wait_ge(uv_full, c.next(uv_full))
                act.activation(vn[r, :, :].rearrange("p h i -> p (h i)"), aux[r, 0, :], ACT.Copy)\
                    .then_inc(uv_ready, c.made(uv_ready))

        def attention():
            t = 0
            for j in range(4):
                w = META + P * (j + 1)
                for h in range(B_HEADS):
                    act.wait_ge(bshift, c.next(bshift))
                    act.activation(pb[:, h, 0:w], pb[:, h, 0:w], ACT.Exp, scale=P ** -0.5, bias=row4[:, 1, h:h + 1],
                                   accum_out=row4[:, 2, h:h + 1]).then_inc(bexp, c.made(bexp))
                for b in range(j + 2):
                    rows = P if b else META
                    act.wait_ge(bt_full, c.next(bt_full))
                    act.activation(sb_[0:rows, t % 2, 0:512], acc[0:rows, t % 2, :], ACT.Copy)\
                        .then_inc(bt_ready, c.made(bt_ready))
                    t += 1
                act.wait_ge(bo_full, c.next(bo_full))
                act.activation(ob[:, :, META + P * j:META + P * j + P],
                               acc[:, 2 + j % 2, :].rearrange("p (h q) -> p h q", h=4), ACT.Copy)\
                    .then_inc(bo_ready, c.made(bo_ready))
            act.wait_ge(bshift, c.next(bshift))
            act.activation(pb[0:META, :, 0:META], pb[0:META, :, 0:META], ACT.Exp, scale=P ** -0.5)\
                .then_inc(bexp, c.made(bexp))
            act.wait_ge(bt_full, c.next(bt_full))
            act.activation(sb_[0:META, 0, 0:4 * META], acc[0:META, 0, 0:4 * META], ACT.Copy)\
                .then_inc(bt_ready, c.made(bt_ready))
            act.wait_ge(bo_full, c.next(bo_full))
            act.activation(ob[:, :, 0:META], acc[:, 2, 0:4 * META].rearrange("p (h q) -> p h q", h=4), ACT.Copy)\
                .then_inc(bo_ready, c.made(bo_ready))

        act.wait_ge(loaded, 64)
        act.wait_ge(pad_clear, 1)
        for stage in STAGES:
            if stage == "mix0":
                mixer0()
            if stage == "mix1":
                mixer1()
            if stage in ("mlp0", "mlp1"):
                mlp1(int(stage[-1]))
            if stage == "final":
                norm(None, SEQ)
            if stage in ("layer0", "layer1"):
                layer(int(stage[-1]))

    @block.vector
    def _(dve):
        c = Counts()
        at = {"piece": 0}

        def step(i):
            i.then_inc(dve_seq, c.made(dve_seq))
            return c.mine()

        def full():
            p = at["piece"]
            dve.wait_ge(w_used, p + 1)
            at["piece"] = p + 1
            return acc[:, p % 4, :] if p < starts.get("layer0", pieces) else acc[:, 2 * pair_of(p):2 * pair_of(p) + 2, 0:HALF]

        def norm(gains, cols):
            s = ROW if cols == SEQ else slice(0, T)
            for k in range(KT):
                dve.wait_ge(sq_ready, c.next(sq_ready))
                if k == 0:
                    dve.tensor_copy(ssq[:, s], sqb[:, 0, s]).then_inc(sq_added, c.made(sq_added))
                else:
                    dve.wait_ge(sq_added, c.at(sq_added))
                    dve.tensor_tensor(ssq[:, s], ssq[:, s], sqb[:, k % 2, s], ALU.add)\
                        .then_inc(sq_added, c.made(sq_added))
                if gains is not None:
                    dve.wait_ge(n_hi, c.next(n_hi))
                    dve.scalar_tensor_tensor(nl[:, k, s], x[:, k, s], gains(k), nh[:, k, s].bitcast(F32),
                                             ALU.mult, ALU.subtract).then_inc(n_ready, c.made(n_ready))
            dve.wait_ge(root_ready, c.next(root_ready))
            dve.reciprocal(scale[:, s], rt[:, s]).then_inc(scale_ready, c.made(scale_ready))
            dve.wait_ge(*c.mine())

        def mixer0():
            norm(lambda k: vec("mix_norm", k), SEQ)
            for i in range(4):
                a = full()
                if i >= 2:
                    dve.wait_ge(sig_ready, i - 1)
                dve.tensor_tensor(ub[:, i % 2, 0:SEQ], a, scale[:, ROW], ALU.mult).then_inc(taken, c.made(taken))
                a = full()
                dve.tensor_tensor(cv[:, i, :], a, scale[:, ROW], ALU.mult).then_inc(taken, c.made(taken))
                mine = c.mine()
                dve.wait_ge(sig_ready, i + 1)
                dve.wait_ge(*mine)
                dve.tensor_tensor(zpad[:, i, CONV_W - 1:], cv[:, i, :], sb_[:, i % 2, 0:SEQ], ALU.mult)\
                    .then_inc(dve_seq, c.made(dve_seq))
            c.next(sig_ready, 4)
            latest = [c.mine()] * 4
            taps = [(j, i) for j in range(CONV_W) for i in range(4)]

            def convolve(n):
                for _ in range(min(n, len(taps))):
                    j, i = taps.pop(0)
                    dve.wait_ge(*latest[i])
                    w = vec("ab_conv_w", CONV_W * i + j)
                    if j == 0:
                        t = dve.tensor_scalar(cv[:, i, :], zpad[:, i, 0:SEQ], w, None, ALU.mult)
                    else:
                        t = dve.scalar_tensor_tensor(cv[:, i, :], zpad[:, i, j:j + SEQ], w, cv[:, i, :],
                                                     ALU.mult, ALU.add)
                    if j < CONV_W - 1:
                        latest[i] = step(t)
                    else:
                        t.then_inc(conv_ready, c.made(conv_ready))

            for n in range(12):
                a = full()
                if n < 4:
                    dve.scalar_tensor_tensor(qs[:, n, :], a, DH ** -0.5, scale[:, ROW], ALU.mult, ALU.mult)\
                        .then_inc(taken, c.made(taken))
                else:
                    dve.tensor_tensor((ks if n < 8 else vs)[:, n % 4, :], a, scale[:, ROW], ALU.mult)\
                        .then_inc(taken, c.made(taken))
                convolve(8)
            convolve(len(taps))
            dve.wait_ge(mean_full, c.next(mean_full))
            for i in range(4):
                dve.scalar_tensor_tensor(cv[:, i, :], aux[:, 1, :], -1.0 / CONV_CH, cv[:, i, :], ALU.mult, ALU.add)\
                    .then_inc(cent_ready, c.made(cent_ready))
            dve.wait_ge(ln_root, c.next(ln_root))
            dve.wait_ge(*step(dve.reciprocal(ub[:, 0, 0:SEQ], rt[:, 0:SEQ])))
            for i in range(4):
                dve.tensor_tensor(cv[:, i, :], cv[:, i, :], ub[:, 0, 0:SEQ], ALU.mult)\
                    .then_inc(ln_scaled, c.made(ln_scaled))
            for i in range(4):
                dve.wait_ge(ln_act, c.next(ln_act))
                dve.tensor_tensor(zpad[:, i, 0:SEQ], zpad[:, i, 0:SEQ], cv[:, i, :], ALU.mult)\
                    .then_inc(ln_out, c.made(ln_out))
            for i in range(4):
                dve.wait_ge(y_hi, c.next(y_hi))
                dve.tensor_tensor(nl[:, i, ROW], zpad[:, i, 0:SEQ], nh[:, i, ROW].bitcast(F32), ALU.subtract)\
                    .then_inc(y_ready, c.made(y_ready))

            def normalise(u):
                dve.wait_ge(s_exp, u + 1)
                w, b = P * (u % 4 + 1), u % 2
                dve.wait_ge(*step(dve.reciprocal(small[:, 3, b:b + 1], small[:, 2, b:b + 1])))
                dve.tensor_scalar(sm[:, b, 0:w], sm[:, b, 0:w], small[:, 3, b:b + 1], None, ALU.mult)\
                    .then_inc(p_ready, c.made(p_ready))

            def heads_low(pair):
                dve.wait_ge(y_hi, c.next(y_hi))
                dve.tensor_tensor(nl[:, 4 + pair, ROW], acc[:, pair % 2, :], nh[:, 4 + pair, ROW].bitcast(F32),
                                  ALU.subtract).then_inc(y_ready, c.made(y_ready))

            for u in range(4 * HEADS + 4):
                if u < 4 * HEADS:
                    h, i = divmod(u, 4)
                    w, b = P * (i + 1), u % 2
                    if i == 0:
                        dve.wait_ge(*step(dve.tensor_scalar(bias[:, h % 2, :], distance,
                                                            2.0 ** (-8.0 * (h + 1) / HEADS), None, ALU.mult)))
                    dve.wait_ge(s_full, u + 1)
                    if u >= 2:
                        dve.wait_ge(pt_full, u - 1)
                    dve.wait_ge(*step(dve.tensor_tensor_reduce(
                        sm[:, b, 0:w], aux[:, b, 0:w], bias[:, h % 2, SEQ - w:SEQ], 1.0, -3e38,
                        ALU.add, ALU.max, small[:, 0, b:b + 1])))
                    dve.tensor_scalar(small[:, 1, b:b + 1], small[:, 0, b:b + 1], -1.0, None, ALU.mult)\
                        .then_inc(s_shift, c.made(s_shift))
                if 1 <= u <= 4 * HEADS:
                    normalise(u - 1)
                if u >= 4 and (u - 4) % 8 == 7:
                    heads_low((u - 4) // 8)
            add_to_x()

        written = {}

        def add_to_x(cols=SEQ, back=0):
            for m in range(KT):
                a = full()
                if back:
                    dve.wait_ge(x_back[m], 16 * back)
                if m in written:
                    dve.wait_ge(*written[m])
                xm = x[:, m, ROW] if cols == SEQ else wide(x[:, m, :])
                dve.tensor_tensor(xm, xm, a, ALU.add).then_inc(taken, c.made(taken))
                written[m] = c.mine()

        def log1p(e, tmp, sum_):
            d, s, s2 = tmp
            dve.wait_ge(*step(dve.tensor_scalar(d, e, 2.0, None, ALU.add)))
            dve.wait_ge(*step(dve.reciprocal(d, d)))
            dve.wait_ge(*step(dve.tensor_tensor(s, e, d, ALU.mult)))
            dve.wait_ge(*step(dve.tensor_tensor(s2, s, s, ALU.mult)))
            dve.wait_ge(*step(dve.tensor_scalar(sum_, s2, 1.0 / 17.0, None, ALU.mult)))
            for n in (15, 13, 11, 9, 7, 5, 3):
                dve.wait_ge(*step(dve.scalar_tensor_tensor(sum_, sum_, 1.0 / n, s2, ALU.add, ALU.mult)))
            dve.wait_ge(*step(dve.scalar_tensor_tensor(sum_, sum_, 1.0, s, ALU.add, ALU.mult)))
            dve.wait_ge(*step(dve.tensor_scalar(sum_, sum_, 2.0, None, ALU.mult)))

        def mixer1():
            lam = v1[:, V1["c_lambda"][0]:V1["c_lambda"][1]]
            dve.wait_ge(*step(dve.tensor_scalar(c8[:, 2, :], lam, -1.0, 0.0, ALU.mult, ALU.max)))
            dve.wait_ge(*step(dve.tensor_scalar(c8[:, 0, :], lam, -1.0, None, ALU.mult)))
            dve.tensor_tensor(c8[:, 0, :], c8[:, 0, :], lam, ALU.max).then_inc(rate_in, c.made(rate_in))
            dve.wait_ge(rate_ready, c.next(rate_ready))
            log1p(c8[:, 1, :], (c8[:, 3, :], c8[:, 4, :], c8[:, 5, :]), c8[:, 0, :])
            dve.wait_ge(*step(dve.tensor_tensor(c8[:, 2, :], c8[:, 2, :], c8[:, 0, :], ALU.add)))
            dve.wait_ge(*step(dve.tensor_scalar(c8[:, 2, :], c8[:, 2, :], 8.0, None, ALU.mult)))
            dve.tensor_scalar(c8[:, 3, :], c8[:, 2, :], -1.0, None, ALU.mult).then_inc(rate_in, c.made(rate_in))
            norm(lambda k: vec("mix_norm", 8 + k), SEQ)
            for h in range(KT):
                a = full()
                dve.tensor_tensor(ub[:, h % 2, 0:SEQ], a, scale[:, ROW], ALU.mult).then_inc(taken, c.made(taken))
                for j in range(LRU_W):
                    w = vec("c_conv_w", LRU_W * h + j)
                    src = ubp[:, h % 2, PAD - LRU_W + 1 + j:PAD - LRU_W + 1 + j + SEQ]
                    dve.wait_ge(*c.mine())
                    if j == 0:
                        step(dve.tensor_scalar(xc[:, h, :], src, w, vec("c_conv_b", h),
                                               ALU.mult, ALU.add))
                    else:
                        t = dve.scalar_tensor_tensor(xc[:, h, :], src, w, xc[:, h, :],
                                                     ALU.mult, ALU.add)
                        t.then_inc(xc_ready if j == LRU_W - 1 else dve_seq,
                                   c.made(xc_ready if j == LRU_W - 1 else dve_seq))
            for h in range(KT):
                a = full()
                s = sb_[:, h % 2, 0:SEQ]
                dve.tensor_tensor(gb[:, h, :], a, scale[:, ROW], ALU.mult).then_inc(taken, c.made(taken))
                dve.wait_ge(*c.mine())
                dve.wait_ge(*step(dve.tensor_tensor(s, gb[:, h, :], gb[:, h, :], ALU.mult)))
                dve.wait_ge(*step(dve.tensor_scalar(s, s, 0.044715, 1.0, ALU.mult, ALU.add)))
                dve.tensor_tensor(s, s, gb[:, h, :], ALU.mult).then_inc(g_ready, c.made(g_ready))
                dve.wait_ge(ri_sig, c.next(ri_sig))
                dve.tensor_tensor(xc[:, h, :], xc[:, h, :], ub[:, h % 2, 0:SEQ], ALU.mult)\
                    .then_inc(xc_gated, c.made(xc_gated))
                dve.wait_ge(gsig_ready, c.next(gsig_ready))
                step(dve.tensor_tensor(gb[:, h, :], gb[:, h, :], s, ALU.mult))
            for h in range(KT):
                dve.wait_ge(a_ready, c.next(a_ready))
                dve.wait_ge(*step(dve.tensor_tensor(ub[:, h % 2, 0:SEQ], rb[:, h, :], rb[:, h, :], ALU.mult)))
                dve.scalar_tensor_tensor(tb[:, h, :], ub[:, h % 2, 0:SEQ], 1.0, tb[:, h, :], ALU.add, ALU.mult)\
                    .then_inc(m_ready, c.made(m_ready))
            for h in range(KT):
                dve.wait_ge(mult_ready, c.next(mult_ready))
                dve.wait_ge(*step(dve.tensor_tensor(xc[:, h, :], xc[:, h, :], tb[:, h, :], ALU.mult)))
                dve.wait_ge(*step(dve.tensor_tensor_scan(tb[:, h, :], rb[:, h, :], xc[:, h, :], 0.0,
                                                         ALU.mult, ALU.add)))
                dve.tensor_tensor(xc[:, h, :], tb[:, h, :], gb[:, h, :], ALU.mult).then_inc(yc_ready, c.made(yc_ready))
            for h in range(KT):
                dve.wait_ge(y_hi, c.next(y_hi))
                dve.tensor_tensor(nl[:, h, ROW], xc[:, h, :], nh[:, h, ROW].bitcast(F32), ALU.subtract)\
                    .then_inc(y_ready, c.made(y_ready))
            add_to_x()

        def mlp1(layer):
            norm(lambda k: vec("mlp_norm", 8 * layer + k), SEQ)
            waiting = []

            def low():
                q, m = waiting.pop(0)
                dve.wait_ge(h_hi, c.next(h_hi))
                dve.tensor_tensor(hid_lo[:, q % 2, m, ROW], sb_[:, m % 2, 0:SEQ],
                                  hid_hi[:, q % 2, m, ROW].bitcast(F32), ALU.subtract)\
                    .then_inc(h_ready, c.made(h_ready))

            for what, q in mlp_order():
                if what == "down":
                    add_to_x()
                    continue
                for m in range(KT):
                    a = full()
                    u = ub[:, m % 2, 0:SEQ]
                    dve.scalar_tensor_tensor(u, a, 0.0, scale[:, ROW], ALU.max, ALU.mult)\
                        .then_inc(taken, c.made(taken))
                    if waiting:
                        low()
                    dve.wait_ge(taken, c.at(taken))
                    dve.tensor_tensor(sb_[:, m % 2, 0:SEQ], u, u, ALU.mult).then_inc(h_sq, c.made(h_sq))
                    waiting.append((q, m))
                low()

        def row_scales():
            dve.wait_ge(droot_ready, c.next(droot_ready))
            dve.reciprocal(rt[0:8, :], rt[0:8, :]).then_inc(dinv_ready, c.made(dinv_ready))

        def layer(l):
            def vec(name, n=0, count=1):
                return vec2_(l, name, n, count)

            norm(lambda k: vec("norm_mix_2", k), T)
            wscale = wide(scale[:, :])
            p0 = at["piece"]
            full()
            dve.wait_ge(rtok_full, c.next(rtok_full))
            dve.wait_ge(*step(dve.tensor_copy(rtok[:, 0:UNITS], aux[:, 2, 0:UNITS])))
            for u in range(UNITS):
                i = dve.tensor_scalar(abt[:, u, :], acc[:, 2 * (p0 % 2), 16 * u:16 * u + 16], rtok[:, u:u + 1],
                                      None, ALU.mult)
                i.then_inc(taken if u == UNITS - 1 else dve_seq, c.made(taken if u == UNITS - 1 else dve_seq))
            for t in [ik[:, :]] + [iq[:, i, :] for i in range(4)] + [bq[:, i, :] for i in range(4)] \
                    + [bk[:, :], bv[:, :]]:
                a = full()
                dve.tensor_tensor(wide(t), a, wscale, ALU.mult).then_inc(taken, c.made(taken))
            dve.wait_ge(*c.mine())
            step(dve.tensor_scalar(abt[:, :, 8:16], abt[:, :, 8:16], (IDX_HEADS * 64) ** -0.5, None, ALU.mult))

            def by_unit(n):
                return gt[:, n, :].rearrange("p (u h) -> p u h", h=4)

            def all_units(a):
                return a.rearrange("p (o h) -> p o h", o=1).to_broadcast([P, UNITS, 4])

            dve.wait_ge(*step(dve.tensor_tensor(by_unit(2), abt[:, :, 0:4], all_units(vec("dt_bias_2", 0, 4)), ALU.add)))
            dve.wait_ge(*step(dve.tensor_scalar(gt[:, 3, :], gt[:, 2, :], -1.0, None, ALU.mult)))
            dve.tensor_tensor(gt[:, 3, :], gt[:, 3, :], gt[:, 2, :], ALU.max).then_inc(abe_in, c.made(abe_in))
            row_scales()
            dve.wait_ge(abe_out, c.next(abe_out))
            log1p(gt[:, 4, :], (gt[:, 5, :], gt[:, 6, :], gt[:, 7, :]), gt[:, 8, :])
            dve.wait_ge(*step(dve.scalar_tensor_tensor(gt[:, 2, :], gt[:, 2, :], 0.0, gt[:, 8, :], ALU.max, ALU.add)))
            dve.wait_ge(*step(dve.scalar_tensor_tensor(by_unit(1), by_unit(2), -1.0, all_units(gt[:, 9, 0:4]),
                                                       ALU.mult, ALU.mult)))
            is_meta = const("is_meta")[:, 0:1]
            step(dve.tensor_scalar(gt[:, 1, 0:4], gt[:, 1, 0:4], is_meta, None, ALU.mult))
            dve.tensor_scalar(gt[:, 0, 0:4], gt[:, 0, 0:4], is_meta, None, ALU.mult).then_inc(g_in, c.made(g_in))

            pending = []

            def silu():
                t, b = pending.pop(0)
                dve.wait_ge(csig, c.next(csig))
                dve.tensor_tensor(t, t, sb_[:, b, :], ALU.mult).then_inc(silu_out, c.made(silu_out))

            def delta_tile(n):
                a = full()
                t = ((dk, dq, dv)[n % 3])[:, n // 3, :]
                tile = (4, 0, 8)[n % 3] + n // 3
                dve.tensor_tensor(wide(ub[:, n % 2, :]), a, wscale, ALU.mult).then_inc(taken, c.made(taken))
                for j in range(4):
                    w = vec("conv_a_2", 4 * tile + j)
                    src = ubp[:, n % 2, PAD - 3 + j:PAD - 3 + j + T]
                    dve.wait_ge(*c.mine())
                    if j == 0:
                        step(dve.tensor_scalar(t, src, w, None, ALU.mult))
                    else:
                        s = silu_in if j == 3 else dve_seq
                        dve.scalar_tensor_tensor(t, src, w, t, ALU.mult, ALU.add).then_inc(s, c.made(s))
                pending.append((t, n % 2))
                if len(pending) > 1:
                    silu()

            delta_tile(0)
            delta_tile(1)
            tiles = [(ik[:, :], "i", 0)] + [(iq[:, i, :], "i", None) for i in range(4)] \
                + [(bq[:, i, :], "a", 1 + i) for i in range(4)] + [(bk[:, :], "a", 5)]
            for n, (t, which, row) in enumerate(tiles):
                dve.wait_ge(rot_full, c.next(rot_full))
                step(dve.tensor_tensor(wide(ssq[:, :]), aux[:, 0:2, 0:HALF], wide(const("sin_" + which)), ALU.mult))
                dve.wait_ge(*step(dve.tensor_tensor(t, t, const("cos_" + which), ALU.mult)))
                i = dve.tensor_tensor(t, t, ssq[:, :], ALU.add)
                if row is not None:
                    dve.wait_ge(*step(i))
                    i = dve.tensor_tensor(wide(t), wide(t), aux[:, 2:4, 0:HALF], ALU.mult)
                i.then_inc(rope_done, c.made(rope_done))
                delta_tile(2 + n)
            silu()
            n = 0
            latest = {}
            for j in range(1, 4):
                for h in range(IDX_HEADS):
                    w = P * (j + 1)
                    iw, s = abt[:, j + 1, 8 + h:9 + h], score[:, j - 1, 0:w]
                    dve.wait_ge(irelu, c.next(irelu))
                    if h == 0:
                        dve.tensor_scalar(s, sqb[:, n % 2, 0:w], iw, None, ALU.mult).then_inc(iscore, c.made(iscore))
                    else:
                        dve.wait_ge(iscore, c.at(iscore))
                        dve.scalar_tensor_tensor(s, sqb[:, n % 2, 0:w], iw, s, ALU.mult, ALU.add)\
                            .then_inc(iscore, c.made(iscore))
                    n += 1

            def gate_tile(m):
                a = full()
                dve.tensor_tensor(wide(x[:, m, :]), a, wscale, ALU.mult).then_inc(taken, c.made(taken))

            def l2_scale(n):
                t = dq[:, n, :] if n < 4 else dk[:, n - 4, :]
                dve.wait_ge(lbc_full, c.next(lbc_full))
                b = aux[:, 2 * (n % 2):2 * (n % 2) + 2, 0:HALF]
                dve.scalar_tensor_tensor(wide(t), wide(t), P ** -0.5 if n < 4 else 1.0, b, ALU.mult, ALU.mult)\
                    .then_inc(lnormed, c.made(lnormed))

            def decay_sums():
                dve.wait_ge(gcol_full, c.next(gcol_full))
                dve.wait_ge(*step(dve.tensor_copy(gt[:, 3, :], aux[:, 0, 0:20])))
                dve.tensor_tensor(gt[:, 4, :], aux[:, 0, 32:52], gt[:, 3, :], ALU.subtract).then_inc(g_in, c.made(g_in))
                dve.wait_ge(*c.mine())
                dve.tensor_copy(gt[:, 8, :], gt[:, 4, :]).then_inc(abe_in, c.made(abe_in))

            def between(round_):
                if round_ == 0:
                    dve.wait_ge(x_saved, 16 * (l + 1))
                if round_ == 3:
                    row_scales()
                if round_ in (5, 7, 9, 11):
                    m = (round_ - 5) // 2
                    gate_tile(m)
                    l2_scale(2 * m)
                    l2_scale(2 * m + 1)
                if round_ == 12:
                    decay_sums()

            top_keys(between)
            dve.wait_ge(abe_out, c.next(abe_out))
            dve.wait_ge(*step(dve.tensor_tensor(gt[:, 7, :], gt[:, 0, :], gt[:, 5, :], ALU.mult)))
            attention()
            dve.memset(state[:, :, :], 0.0).then_inc(us_ready, c.made(us_ready))
            filled = []

            def fill_result():
                f = len(filled)
                if f >= A_HEADS:
                    gate_tile(TOP_GATES + f - A_HEADS)
                else:
                    a = full()
                    dve.tensor_tensor(wide(dz[:, f, :]), a, wscale, ALU.mult).then_inc(taken, c.made(taken))
                    pending.append((dz[:, f, :], f % 2))
                filled.append(f)

            for u in range(UNITS):
                unit(u, fill_result, lambda: silu() if pending else None)
            row_scales()
            for h in range(4):
                dve.wait_ge(lbc_full, c.next(lbc_full))
                b = aux[:, 2 * (h % 2):2 * (h % 2) + 2, 0:HALF]
                dve.scalar_tensor_tensor(wide(dq[:, h, :]), wide(dq[:, h, :]), vec("a_out_norm_2"), b,
                                         ALU.mult, ALU.mult).then_inc(onorm_ready, c.made(onorm_ready))
                dve.wait_ge(*c.mine())
                dve.tensor_tensor(dq[:, h, :], dq[:, h, :], dz[:, h, :], ALU.mult).then_inc(oz_ready, c.made(oz_ready))
            for k in range(8):
                dve.wait_ge(o_hi, c.next(o_hi))
                src = dq[:, k, :] if k < 4 else ob[:, k - 4, :]
                dve.tensor_tensor(ol[:, k, :], src, oh[:, k, :].bitcast(F32), ALU.subtract)\
                    .then_inc(o_ready, c.made(o_ready))
            dve.wait_ge(gate_kept, c.next(gate_kept, KT))
            for m in range(KT):
                a = full()
                dve.tensor_tensor(wide(ub[:, m % 2, :]), a, wscale, ALU.mult).then_inc(taken, c.made(taken))
                if m:
                    mixed_low(m - 1)
                full()
                dve.wait_ge(gate_sig, c.next(gate_sig))
                if m:
                    dve.wait_ge(mix_lo, c.at(mix_lo))
                step(dve.tensor_tensor(wide(sqb[:, 0, :]), acc[:, 0:2, 0:HALF], wide(x[:, m, :]), ALU.mult))
                dve.tensor_tensor(wide(sqb[:, 1, :]), acc[:, 2:4, 0:HALF], wide(sb_[:, m % 2, :]), ALU.mult)\
                    .then_inc(taken, c.made(taken))
                dve.wait_ge(*c.mine())
                dve.tensor_tensor(sqb[:, 0, :], sqb[:, 0, :], sqb[:, 1, :], ALU.add)\
                    .then_inc(mix_ready, c.made(mix_ready))
            mixed_low(KT - 1)
            add_to_x(T, l + 1)
            norm(lambda k: vec("norm_ffn_2", k), T)
            waiting = []

            def low():
                g, i, b = waiting.pop(0)
                dve.wait_ge(h_hi, c.next(h_hi))
                dve.tensor_tensor(hid_lo[:, g % 2, i, :], sb_[:, b, :], hid_hi[:, g % 2, i, :].bitcast(F32),
                                  ALU.subtract).then_inc(h_ready, c.made(h_ready))

            for what, g in FFN_ORDER:
                if what == "down":
                    add_to_x(T)
                    continue
                for i in range(*FFN_THIRDS[g]):
                    b = i % 2
                    a = full()
                    dve.tensor_tensor(wide(ub[:, b, :]), a, wscale, ALU.mult).then_inc(taken, c.made(taken))
                    if waiting:
                        low()
                    for j in range(3):
                        w = vec("conv_ffn_2", 3 * i + j)
                        src = ubp[:, b, PAD - 2 + j:PAD - 2 + j + T]
                        dve.wait_ge(*c.mine())
                        if j == 0:
                            step(dve.tensor_scalar(sb_[:, b, :], src, w, None, ALU.mult))
                        else:
                            s = silu_in if j == 2 else dve_seq
                            dve.scalar_tensor_tensor(sb_[:, b, :], src, w, sb_[:, b, :], ALU.mult, ALU.add)\
                                .then_inc(s, c.made(s))
                    a = full()
                    dve.wait_ge(silu_in, c.at(silu_in))
                    dve.tensor_tensor(wide(ub[:, b, :]), a, wscale, ALU.mult).then_inc(taken, c.made(taken))
                    dve.wait_ge(csig, c.next(csig))
                    dve.wait_ge(*step(dve.tensor_tensor(sb_[:, b, :], sb_[:, b, :], sqb[:, b, :], ALU.mult)))
                    dve.tensor_tensor(sb_[:, b, :], sb_[:, b, :], ub[:, b, :], ALU.mult).then_inc(h_sq, c.made(h_sq))
                    waiting.append((g, i - FFN_THIRDS[g][0], b))
                low()

        def mixed_low(m):
            dve.wait_ge(mix_hi, c.next(mix_hi))
            dve.tensor_tensor(yl[:, m, :], sqb[:, 0, :], yh[:, m, :].bitcast(F32), ALU.subtract)\
                .then_inc(mix_lo, c.made(mix_lo))

        def top_keys(between):
            latest = {}
            dve.wait_ge(iscore, c.at(iscore))
            for j in range(1, 4):
                latest[j] = step(dve.memset(score[0:64, j - 1, P * j + 64:P * j + P], -BIG))
            for round_ in range(TOPK // 8):
                between(round_)
                for j in range(1, 4):
                    s = score[:, j - 1, 0:P * (j + 1)]
                    dve.wait_ge(*latest[j])
                    latest[j] = step(dve.max(best[:, j - 1, :], s))
                for j in range(1, 4):
                    s = score[:, j - 1, 0:P * (j + 1)]
                    dve.wait_ge(*latest[j])
                    latest[j] = step(dve.match_replace(s, best[:, j - 1, :], s, MARK))
            for j in range(4):
                o = SEL_AT[j]
                step(dve.memset(selb[:, o:o + META], 0.0))
                if j == 0:
                    step(dve.tensor_copy(selb[:, o + META:SEL_AT[1]], const("ahead")))
                else:
                    dve.wait_ge(*latest[j])
                    step(dve.tensor_scalar(selb[:, o + META:SEL_AT[j + 1]], score[:, j - 1, 0:P * (j + 1)], MARK, -BIG,
                                           ALU.not_equal, ALU.mult))
            dve.wait_ge(*c.mine())

        def per_head(a):
            return a.rearrange("p (o i) -> p o i", o=1).to_broadcast([P, A_HEADS, P])

        def per_token(n, u):
            return gt[:, n, 4 * u:4 * u + 4].rearrange("p (h o) -> p h o", o=1).to_broadcast([P, A_HEADS, P])

        def by_head(bank):
            return bank.rearrange("p (h i) -> p h i", h=A_HEADS)

        def unit(u, fill_result, silu):
            cs = slice(first(u), first(u) + P)
            dve.wait_ge(egr_ready, c.next(egr_ready))
            for h in range(A_HEADS):
                i = dve.tensor_scalar(dt[:, h, :], aux[:, 0, P * h:P * h + P], gt[:, 3, 4 * u + h:4 * u + h + 1], 0.0,
                                      ALU.subtract, ALU.min)
                s = udt if h == A_HEADS - 1 else dve_seq
                i.then_inc(s, c.made(s))
            dve.wait_ge(udt_exp, c.next(udt_exp))
            dve.wait_ge(ukq_full, c.next(ukq_full))
            dve.wait_ge(*step(dve.tensor_tensor(mt[:, :, :], by_head(aux[:, 2, :]), dt[:, :, :], ALU.mult)))
            dve.wait_ge(*step(dve.tensor_tensor(mt[:, :, :], mt[:, :, :], by_head(aux[:, 1, :]), ALU.mult)))
            dve.wait_ge(*step(dve.tensor_tensor(mt[:, :, :], mt[:, :, :], per_head(const("strict")), ALU.mult)))
            dve.wait_ge(*step(dve.tensor_tensor(xit[:, :, :], mt[:, :, :], per_head(const("join_0")), ALU.mult)))
            dve.tensor_tensor(xit[:, :, :], per_head(ident), xit[:, :, :], ALU.subtract).then_inc(ux_ready, c.made(ux_ready))
            dve.wait_ge(utok_full, c.next(utok_full))
            dve.tensor_tensor(ct[:, :, :], mt[:, :, :], per_head(const("join_1")), ALU.mult)\
                .then_inc(uct_ready, c.made(uct_ready))
            step(dve.tensor_tensor(kbg[:, :, :], by_head(acc[:, 2, :]), per_token(7, u), ALU.mult))
            step(dve.tensor_tensor(kg[:, :, :], by_head(acc[:, 2, :]), per_token(6, u), ALU.mult))
            dve.tensor_tensor(vb[:, :, :], by_head(acc[:, 3, :]), per_token(0, u), ALU.mult)\
                .then_inc(utok_ready, c.made(utok_ready))
            dve.wait_ge(*step(dve.tensor_tensor(dt[:, :, :], dt[:, :, :], per_head(const("until")), ALU.mult)))
            step(dve.tensor_tensor(qkt[:, :, :], by_head(aux[:, 3, :]), dt[:, :, :], ALU.mult))
            dve.tensor_tensor(qg[:, :, :], dq[:, :, cs], egr[:, :, :], ALU.mult).then_inc(uq_ready, c.made(uq_ready))
            for n in range(1, LEVELS):
                f, third, _ = fill_blocks(u, n)
                if third == 0 and f > 0:
                    fill_result()
                if third == 1:
                    silu()
                dve.wait_ge(uz_full, c.next(uz_full))
                if n < LEVELS - 1:
                    step(dve.tensor_tensor(xi[:, :, :], xi[:, :, :], by_head(aux[:, 1, :]), ALU.subtract))
                dve.tensor_tensor(xit[:, :, :], xit[:, :, :], by_head(aux[:, 2, :]), ALU.subtract)\
                    .then_inc(uinv_ready, c.made(uinv_ready))
                if n < LEVELS - 1:
                    dve.tensor_tensor(ct[:, :, :], mt[:, :, :], per_head(const(f"join_{n + 1}")), ALU.mult)\
                        .then_inc(uct_ready, c.made(uct_ready))
                dve.wait_ge(*c.mine())
            chunks = 1 if u == 0 else 2
            for cc in range(chunks):
                dve.wait_ge(uso_full, c.next(uso_full))
                for h in range(A_HEADS):
                    i = dve.scalar_tensor_tensor(state[:, h, :], state[:, h, :], egr[:, h, 64 * cc + 63:64 * cc + 64],
                                                 aux[:, 1, P * h:P * h + P], ALU.mult, ALU.add)
                    s = us_ready if h == A_HEADS - 1 else dve_seq
                    i.then_inc(s, c.made(s))
                dve.wait_ge(*c.mine())
            n = P if u else META
            dve.tensor_copy(dq[:, :, first(u):first(u) + n], by_head(aux[:, 3, :])[:, :, 0:n])\
                .then_inc(uo_done, c.made(uo_done))
            dve.wait_ge(*c.mine())

        def attention():
            def shift(j, h):
                w, o = META + P * (j + 1), SEL_AT[j]
                dve.wait_ge(bs_full, c.next(bs_full))
                dve.wait_ge(*step(dve.tensor_tensor_reduce(
                    pb[:, h, 0:w].rearrange("p (s t) -> p s t", s=2), aux[:, 2 * (h % 2):2 * (h % 2) + 2, 0:w // 2],
                    selb[:, o:o + w].rearrange("p (s t) -> p s t", s=2), 1.0, MARK, ALU.add, ALU.max,
                    row4[:, 0, h:h + 1])))
                dve.tensor_scalar(row4[:, 1, h:h + 1], row4[:, 0, h:h + 1], -P ** -0.5, None, ALU.mult)\
                    .then_inc(bshift, c.made(bshift))

            def normalise(j, h):
                w = META + P * (j + 1)
                dve.wait_ge(bexp, c.next(bexp))
                dve.wait_ge(*step(dve.reciprocal(row4[:, 3, h:h + 1], row4[:, 2, h:h + 1])))
                dve.tensor_scalar(pb[:, h, 0:w], pb[:, h, 0:w], row4[:, 3, h:h + 1], None, ALU.mult)\
                    .then_inc(bp_ready, c.made(bp_ready))

            for j in range(4):
                if j:
                    dve.wait_ge(bt_full, c.next(bt_full, j + 1))
                for h in range(B_HEADS):
                    shift(j, h)
                    if h:
                        normalise(j, h - 1)
                normalise(j, B_HEADS - 1)
            dve.wait_ge(bt_full, c.next(bt_full, 5))
            dve.wait_ge(bs_full, c.next(bs_full))
            s = aux[0:META, 0, 0:4 * META].rearrange("p (h k) -> p h k", h=4)
            pm = pb[0:META, :, 0:META]

            def bc(n):
                return row4[0:META, n, :].rearrange("p (h o) -> p h o", o=1).to_broadcast([META, 4, META])

            dve.wait_ge(*step(dve.tensor_reduce(row4[0:META, 0, :], s, AX.X, ALU.max)))
            dve.tensor_tensor(pm, s, bc(0), ALU.subtract).then_inc(bshift, c.made(bshift))
            dve.wait_ge(bexp, c.next(bexp))
            dve.wait_ge(*step(dve.tensor_reduce(row4[0:META, 2, :], pm, AX.X, ALU.add)))
            dve.wait_ge(*step(dve.reciprocal(row4[0:META, 3, :], row4[0:META, 2, :])))
            dve.tensor_tensor(pm, pm, bc(3), ALU.mult).then_inc(bp_ready, c.made(bp_ready))
            c.next(bt_full)

        step(dve.memset(ubp[:, :, 0:PAD], 0.0))
        dve.memset(eps[:, :], EPS).then_inc(dve_seq, c.made(dve_seq))
        dve.memset(zpad[:, :, 0:CONV_W - 1], 0.0).then_inc(pad_clear, c.made(pad_clear))
        dve.wait_ge(*c.mine())
        dve.wait_ge(loaded, 64)
        for stage in STAGES:
            if stage == "mix0":
                mixer0()
            if stage == "mix1":
                mixer1()
            if stage in ("mlp0", "mlp1"):
                mlp1(int(stage[-1]))
            if stage == "final":
                norm(None, SEQ)
                for k in range(KT):
                    dve.scalar_tensor_tensor(x[:, k, ROW], x[:, k, ROW], vec("final_norm", k), scale[:, ROW],
                                             ALU.mult, ALU.mult).then_inc(x_final, c.made(x_final))
            elif stage in ("layer0", "layer1"):
                layer(int(stage[-1]))

    block.__exit__(None, None, None)


def distances(np):
    p = np.arange(P)[:, None]
    s = np.arange(SEQ)[None, :] - (SEQ - P)
    return np.where(s <= p, s - p, -BIG).astype(np.float32)


def tables1(np):
    return np.concatenate([np.eye(P), np.ones((P, P))], axis=1).astype(np.float32)


def tables2(np):
    f32 = np.float32
    p, i = np.arange(P)[:, None], np.arange(P)[None, :]
    parts = {}
    for name, dim in (("a", P), ("i", 64)):
        half = dim // 2
        inv = (f32(1.0) / (f32(10000.0) ** (np.arange(0, dim, 2, dtype=f32) / f32(dim)))).astype(f32)
        angle = (np.arange(T, dtype=f32)[:, None] * inv[None, :]).astype(f32)[:, np.arange(P) % half].T
        parts["cos_" + name], parts["sin_" + name] = np.cos(angle), np.sin(angle)
        low = (i % dim) < half
        parts["turn_" + name] = np.where(low & (p == i + half), -1.0, 0.0) + np.where(~low & (p == i - half), 1.0, 0.0)
    same = p // CHUNK == i // CHUNK
    parts["until"], parts["same"], parts["strict"] = same & (p <= i), same, same & (p < i)
    parts["ahead"] = np.where(i // CHUNK > p // CHUNK, -BIG, 0.0)
    for n in range(LEVELS):
        b = 2 ** n
        parts[f"join_{n}"] = ((i // b) % 2 == 1) & (p // b == i // b - 1)
    parts["rows"] = np.tile((np.arange(64) // 8 == np.arange(64) % 8)[None, :], (P, 1))
    parts["is_meta"] = np.tile(p < META, (1, 8))
    return np.concatenate([parts[name].astype(f32) for name, _ in CONST2], axis=1)


def tile_columns(a):
    return a.reshape(-1, P).T


def kernel(**inputs):
    import numpy as np
    import concourse.bacc as bacc
    from concourse.bass_utils import run_bass_kernel_spmd

    a = {name: np.asarray(v) for name, v in inputs.items()}
    weights = dict(a)
    weights["w_branch_2"] = np.concatenate([a["w_branch_a_2"], a["w_branch_b_2"]], axis=1)

    def piece(name, layer, parts):
        out = np.zeros((P, KT * P), np.float32)
        w = weights[name][layer]
        for b, (r, col, n) in enumerate(parts):
            rows = w[r:r + P]
            if col == "ab_iw":
                out[:, P * b:P * b + 8] = rows[:, AA:AA + 8]
                out[:, P * b + 8:P * b + 16] = rows[:, IW:IW + 8]
            elif col == "ik_twice":
                out[:, P * b:P * b + 64] = rows[:, IK:IK + 64]
                out[:, P * b + 64:P * b + 128] = rows[:, IK:IK + 64]
            else:
                out[:, P * b:P * b + n] = rows[:, col:col + n]
        return out

    plan, _ = weight_plan()
    stream = np.stack([piece(*p) for p in plan])
    v1 = [tile_columns(a["mix_norm"]), tile_columns(a["mlp_norm"]), tile_columns(a["final_norm"]),
          a["ab_conv_w"][0].reshape(CONV_W, 4, P).transpose(2, 1, 0).reshape(P, -1),
          tile_columns(a["ab_ln_g"]), tile_columns(a["ab_ln_b"]),
          a["c_conv_w"][0].reshape(LRU_W, KT, P).transpose(2, 1, 0).reshape(P, -1),
          tile_columns(a["c_conv_b"]), tile_columns(a["c_b_r"]), tile_columns(a["c_b_i"]),
          tile_columns(a["c_lambda"])]
    def by_tile(w, taps):
        return w.reshape(taps, -1, P).transpose(2, 1, 0).reshape(P, -1)

    def all_rows(v):
        return np.repeat(v[None, :], P, axis=0)

    v2 = [np.concatenate([
        tile_columns(a["norm_mix_2"][l]), tile_columns(a["norm_ffn_2"][l]), by_tile(a["conv_a_2"][l], 4),
        all_rows(a["a_log_2"][l]), all_rows(a["dt_bias_2"][l]), tile_columns(a["a_out_norm_2"][l]),
        tile_columns(a["q_norm_2"][l]), tile_columns(a["k_norm_2"][l]),
        np.concatenate([a["kidx_norm_2"][l]] * 2)[:, None],
        tile_columns(a["b_gate_2"][l]), by_tile(a["conv_ffn_2"][l], 3)], axis=1) for l in range(2)]
    arrays = {
        "vec2": np.stack(v2, axis=1), "const2": tables2(np), "dist": distances(np),
        "meta": a["meta_tokens_2"].T,
        "stream": stream,
        "xt": a["x"][0].T,
        "vec1": np.concatenate(v1, axis=1),
        "const1": tables1(np),
        "lru_w": np.concatenate([a["c_w_r"][0], a["c_w_i"][0]]).transpose(1, 0, 2),
    }
    arrays = {f"in_{n}": np.ascontiguousarray(v) for n, v in arrays.items()}
    nc = bacc.Bacc("TRN2", target_bir_lowering=False, num_devices=1)
    dram = {n[3:]: nc.dram_tensor(n, v.shape, mybir.dt.from_np(v.dtype), kind="ExternalInput").ap()
            for n, v in arrays.items()}
    out = nc.dram_tensor("out_dram", (D, SEQ), F32, kind="ExternalOutput").ap()
    saved_x = nc.dram_tensor("saved_x", (D, T), F32, kind="Internal").ap()
    build(nc, out=out, saved_x=saved_x, **dram)
    r = run_bass_kernel_spmd(nc, [arrays], core_ids=[0])
    return r.results[0]["out_dram"].T[None]
```

```python
import math

import concourse.bass as bass
from concourse import mybir

F32 = mybir.dt.float32
F32R = mybir.dt.float32r
ALU = mybir.AluOpType
ACT = mybir.ActivationFunctionType
AX = mybir.AxisListType

P = 128
D = 1024
KT = D // P
SEQ = 512
META = 16
T = SEQ + META
HALF = T // 2
EPS = 1e-6
BIG = 1e30

CONV_CH = 512
CONV_W = 31
HEADS = 8
DH = 64
AB_IN = 2560
LRU_HEADS = 8
LRU_W = 4
FF = 4096
QUARTERS = FF // D

A_HEADS = 4
B_HEADS = 4
IDX_HEADS = 8
FF2 = 2816
FT2 = FF2 // P
SPLITS = (512, 512, 512, 512, 4, 4, 512, 128, 128, 512, 64, 8)
AQ, AK, AV, AZ, AA, AB_, BQ, BK, BV, IQ, IK, IW = (sum(SPLITS[:n]) for n in range(12))
TOPK = 128
CHUNK = 64
UNITS = 5

TOP_GATES = 4
UNIT_JOBS = A_HEADS + KT - TOP_GATES
FILLED = UNIT_JOBS // 2
BRANCHES = 24 + UNIT_JOBS + TOP_GATES

RAW_SLOTS = 4
W_SLOTS = 4
AHEAD = 3


def mlp_order():
    order = [("up", 0)]
    for q in range(QUARTERS):
        if q + 1 < QUARTERS:
            order.append(("up", q + 1))
        order.append(("down", q))
    return order


FFN_THIRDS = [(0, 8), (8, 16), (16, FT2)]
FFN_ORDER = [("up", 0), ("up", 1), ("down", 0), ("up", 2), ("down", 1), ("down", 2)]


STAGES = ["mix0", "mlp0", "mix1", "mlp1", "final", "layer0", "layer1"]


def weight_plan():
    plan = []

    def column(name, layer, col, rows=range(KT)):
        plan.append((name, layer, [(P * r, col, P) for r in rows]))

    def mixer0():
        for i in range(4):
            column("ab_w_in", 0, CONV_CH + P * i)
            column("ab_w_in", 0, P * i)
        for pair in range(4):
            for m in (8, 12, 16):
                column("ab_w_in", 0, P * (m + pair))
        for m in range(KT):
            column("ab_w_out", 0, P * m)

    def mixer1():
        for m in range(KT):
            column("c_w_in", 0, D + P * m)
        for m in range(KT):
            column("c_w_in", 0, P * m)
        for m in range(KT):
            column("c_w_out", 0, P * m)

    def mlp(layer):
        for what, q in mlp_order():
            for m in range(KT):
                if what == "up":
                    column("w_up", layer, D * q + P * m)
                else:
                    column("w_down", layer, P * m, range(KT * q, KT * q + KT))

    def block2(layer):
        plan.append(("w_in_2", layer, [(P * r, "ab_iw", 16) for r in range(KT)]))
        plan.append(("w_in_2", layer, [(P * r, "ik_twice", P) for r in range(KT)]))
        for c in (IQ, BQ):
            for i in range(4):
                column("w_in_2", layer, c + P * i)
        column("w_in_2", layer, BK)
        column("w_in_2", layer, BV)
        for h in range(A_HEADS):
            for c in (AK, AQ, AV):
                column("w_in_2", layer, c + P * h)
        for m in range(TOP_GATES):
            column("w_gate_2", layer, P * m)
        for h in range(A_HEADS):
            column("w_in_2", layer, AZ + P * h)
        for m in range(TOP_GATES, KT):
            column("w_gate_2", layer, P * m)
        column("w_gate_2", layer, D)
        for m in range(KT):
            if m + 1 < KT:
                column("w_gate_2", layer, D + P * (m + 1))
            plan.append(("w_branch_2", layer, [(P * r, P * m, P) for r in range(KT)]))
        for m in range(KT):
            column("w_out_2", layer, P * m)
        for what, g in FFN_ORDER:
            a, b = FFN_THIRDS[g]
            if what == "up":
                for i in range(a, b):
                    column("w_up_2", layer, P * i)
                    column("w_up_2", layer, FF2 + P * i)
            else:
                for m in range(KT):
                    column("w_down_2", layer, P * m, range(a, b))

    make = {"mix0": mixer0, "mix1": mixer1, "mlp0": lambda: mlp(0), "mlp1": lambda: mlp(1),
            "final": lambda: None, "layer0": lambda: block2(0), "layer1": lambda: block2(1)}
    starts = {}
    for stage in STAGES:
        starts[stage] = len(plan)
        make[stage]()
    return plan, starts


PAD = 4
LEVELS = 6
TILES4 = 4 * T * 4
SEL_AT = [0]
for _j in range(4):
    SEL_AT.append(SEL_AT[-1] + META + P * (_j + 1))
MARK = -3e38


class Counts:

    def __init__(self):
        self.seen = {}
        self.latest = None

    def made(self, sem):
        self.seen[sem.name] = self.seen.get(sem.name, 0) + 1
        self.latest = (sem, self.seen[sem.name])
        return 1

    def mine(self):
        return self.latest

    def next(self, sem, n=1):
        self.seen[sem.name] = self.seen.get(sem.name, 0) + n
        return self.seen[sem.name]

    def at(self, sem):
        return self.seen.get(sem.name, 0)


class Area:

    def __init__(self, nc, start, end):
        self.nc, self.at, self.end = nc, start, end

    def take(self, name, shape, dtype=F32):
        size = 4 * math.prod(shape[1:])
        at = self.at
        self.at = at + -(-size // 32) * 32
        assert self.at <= self.end, (name, self.at, self.end)
        return self.nc.alloc_sbuf_tensor_at(name, shape, dtype, offset=at)


VEC1 = [("mix_norm", 16), ("mlp_norm", 16), ("final_norm", 8), ("ab_conv_w", 4 * CONV_W),
        ("ab_ln_g", 4), ("ab_ln_b", 4), ("c_conv_w", KT * LRU_W), ("c_conv_b", 8),
        ("c_b_r", 8), ("c_b_i", 8), ("c_lambda", 8)]
VEC2 = [("norm_mix_2", 8), ("norm_ffn_2", 8), ("conv_a_2", 48), ("a_log_2", 4), ("dt_bias_2", 4),
        ("a_out_norm_2", 1), ("q_norm_2", 1), ("k_norm_2", 1), ("kidx_norm_2", 1),
        ("b_gate_2", 16), ("conv_ffn_2", 66)]
CONST1 = [("ident", P), ("ones", P)]
CONST2 = [("cos_a", T), ("sin_a", T), ("cos_i", T), ("sin_i", T), ("turn_a", P), ("turn_i", P),
          ("until", P), ("same", P), ("ahead", P)] + [(f"join_{n}", P) for n in range(LEVELS)] + [("rows", 64), ("is_meta", 8)]


def columns(table):
    out, at = {}, 0
    for name, n in table:
        out[name] = (at, at + n)
        at += n
    return out, at


V1, NV1 = columns(VEC1)
V2, NV2 = columns(VEC2)
C1, NC1 = columns(CONST1)
C2, NC2 = columns(CONST2)


def build(nc, stream, xt, vec1, vec2, const1, const2, dist, lru_w, meta, saved_x, out):
    plan, starts = weight_plan()
    pieces = len(plan)
    base = -(-nc.sbuf_base // 64) * 64
    fixed = Area(nc, base, nc.sbuf_usable_end)
    x = fixed.take("x", [P, KT, T])
    nh = fixed.take("n_hi", [P, KT, T], F32R)
    nl = fixed.take("n_lo", [P, KT, T], F32R)
    raw = fixed.take("w_raw", [P, RAW_SLOTS, KT * P])
    wh = fixed.take("w_hi", [P, W_SLOTS, KT * P], F32R)
    wl = fixed.take("w_lo", [P, W_SLOTS, KT * P], F32R)
    scale = fixed.take("norm_scale", [P, T])
    ssq = fixed.take("square_sum", [P, T])
    sqb = fixed.take("squares", [P, 2, T])
    ubp = fixed.take("unit_a", [P, 2, T + PAD])
    ub = ubp[:, :, PAD:]
    sb_ = fixed.take("unit_b", [P, 2, T])
    rt = fixed.take("root", [P, T])
    v1 = fixed.take("vec1", [P, NV1])
    v2 = fixed.take("vec2", [P, 2, NV2])
    c1 = fixed.take("const1", [P, NC1])
    ident = c1[:, C1["ident"][0]:C1["ident"][1]]
    ones = c1[:, C1["ones"][0]:C1["ones"][1]]

    def const(name):
        return c2[:, C2[name][0]:C2[name][1]]

    def vec2_(layer, name, n=0, count=1):
        return v2[:, layer, V2[name][0] + n:V2[name][0] + n + count]

    def vec(name, n=0):
        return v1[:, V1[name][0] + n:V1[name][0] + n + 1]

    eps = fixed.take("eps", [P, 8])
    area = fixed.at
    end = nc.sbuf_usable_end // 64 * 64 - 4 * NC2 - 64
    c2 = Area(nc, end, nc.sbuf_usable_end).take("const2", [P, NC2])
    mlp = Area(nc, area, end)
    hid_hi = mlp.take("hidden_hi", [P, 2, KT, T], F32R)
    hid_lo = mlp.take("hidden_lo", [P, 2, KT, T], F32R)

    m0 = Area(nc, area, end)
    distance = m0.take("distance", [P, SEQ])[:, :]
    zpad = m0.take("z_padded", [P, 4, CONV_W - 1 + SEQ])
    cv = m0.take("conv_out", [P, 4, SEQ])
    qs = m0.take("queries", [P, 4, SEQ])
    ks = m0.take("keys", [P, 4, SEQ])
    vs = m0.take("values", [P, 4, SEQ])
    vt = m0.take("values_by_token", [P, 4, SEQ])
    bias = m0.take("alibi", [P, 2, SEQ])
    sm = m0.take("softmax", [P, 4, SEQ])
    pt = m0.take("probs_t", [P, 2, SEQ])
    small = m0.take("row_values", [P, 8, 2])

    m1 = Area(nc, area, end)
    gb = m1.take("gate", [P, KT, SEQ])
    xc = m1.take("lru_in", [P, KT, SEQ])
    rb = m1.take("lru_a", [P, KT, SEQ])
    tb = m1.take("lru_b", [P, KT, SEQ])
    lw = m1.take("lru_weights", [P, 2 * LRU_HEADS, P])
    c8 = m1.take("lru_rate", [P, 6, KT])

    A = area
    dq = Area(nc, A, end).take("delta_q", [P, A_HEADS, T])
    dz = Area(nc, A + TILES4, end).take("delta_z", [P, A_HEADS, T])
    dk = Area(nc, A + 2 * TILES4, end).take("delta_k", [P, A_HEADS, T])
    dv = Area(nc, A + 3 * TILES4, end).take("delta_v", [P, A_HEADS, T])
    W = A + 4 * TILES4
    iq = Area(nc, W, end).take("index_q", [P, 4, T])
    pb = Area(nc, W, end).take("probs", [P, 4, T])
    bq = Area(nc, W + TILES4, end).take("attn_q", [P, 4, T])
    ob = Area(nc, W + 2 * TILES4, end).take("attn_out", [P, 4, T])
    score = Area(nc, W + 2 * TILES4, end).take("index_score", [P, 3, SEQ])
    rest = Area(nc, W + 3 * TILES4, end)
    ik = rest.take("index_k", [P, T])
    bk = rest.take("attn_k", [P, T])
    bv = rest.take("attn_v", [P, T])
    selb = rest.take("select_bias", [P, SEL_AT[4]])
    vtok = rest.take("attn_v_by_token", [P, UNITS, P])
    rest.at = W + 3 * TILES4 + 7 * 4 * A_HEADS * P
    abt = rest.take("rates", [P, UNITS, 16])
    gt = rest.take("gates_by_token", [P, 10, UNITS * A_HEADS])
    best = rest.take("best8", [P, 3, 8])
    row4 = rest.take("row_values2", [P, 4, 4])
    lo_part = Area(nc, W, W + 2 * TILES4)
    hi_part = Area(nc, W + 3 * TILES4, end)
    names = ["decay_t", "exp_g_row", "qk_t", "q_g", "m_t", "c_t", "inv", "inv_t"]
    dt, egr, qkt, qg, mt, ct, xi, xit = (lo_part.take(n, [P, A_HEADS, P]) for n in names)
    names = ["p1", "k_beta_g", "k_g", "v_beta", "w_t", "v_new", "state"]
    p1, kbg, kg, vb, nwt, vn, state = (hi_part.take(n, [P, A_HEADS, P]) for n in names)
    assert hi_part.at <= W + 3 * TILES4 + 7 * 2048
    states = [state, ssq[:, 0:A_HEADS * P].rearrange("p (h i) -> p h i", h=A_HEADS)]

    def state_of(u, cc):
        return states[(2 * u - 1 + cc if u else cc) % 2]

    oh = Area(nc, A + 2 * TILES4, end).take("out_hi", [P, KT, T], F32R)
    ol = Area(nc, W, end).take("out_lo", [P, KT, T], F32R)
    yh = Area(nc, A, end).take("mixed_hi", [P, KT, T], F32R)
    yl = Area(nc, W + 2 * TILES4, end).take("mixed_lo", [P, KT, T], F32R)

    acc = nc.alloc_psum_tensor("acc", [P, 4, 512], F32)
    aux = nc.alloc_psum_tensor("aux", [P, 4, 512], F32)

    def sem(name):
        return nc.alloc_semaphore(name)

    landed = [sem(f"w_landed_{n}") for n in range(RAW_SLOTS)]
    loaded, dist_landed = sem("tables_landed"), sem("distance_landed")
    x_landed = [sem(f"x_landed_{k}") for k in range(KT)]
    lru_landed = sem("lru_weights_landed")
    stored = sem("output_stored")
    w_hi, w_lo, w_used = sem("w_hi_ready"), sem("w_lo_ready"), sem("w_piece_used")
    taken = sem("acc_taken")
    act_seq, dve_seq = sem("act_steps"), sem("dve_steps")
    sq_ready, sq_added, ss_full, root_ready = sem("square_ready"), sem("square_added"), sem("square_sum_full"), sem("root_ready")
    n_hi, n_ready = sem("n_hi_ready"), sem("n_ready")
    h_sq, h_hi, h_ready = sem("hidden_ready"), sem("hidden_hi_ready"), sem("hidden_lo_ready")
    sig_ready = sem("sigmoid_ready")
    pad_clear = sem("pads_clear")
    conv_ready = sem("conv_ready")
    mean_full, cent_ready, var_full, ln_root = sem("mean_full"), sem("centred"), sem("variance_full"), sem("ln_root")
    ln_sq = sem("ln_square")
    ln_scaled, ln_act, ln_out, y_hi, y_ready = sem("ln_scaled"), sem("ln_affine"), sem("ln_out"), sem("y_hi_ready"), sem("y_ready")
    vt_full, vt_copied, o_copied = sem("v_turned"), sem("v_copied"), sem("attn_out_copied")
    s_full, s_shift, s_exp, p_ready = sem("scores_full"), sem("scores_shifted"), sem("scores_exp"), sem("probs_ready")
    pt_full, pt_ready, o_full = sem("probs_turned"), sem("probs_t_ready"), sem("attn_out_full")
    xc_ready, ri_full, ri_sig, tanh_ready = sem("lru_conv_ready"), sem("lru_gates_full"), sem("lru_sigmoid"), sem("lru_tanh")
    g_ready, gsig_ready = sem("gelu_inner"), sem("gelu_sigmoid")
    xc_gated, x_final = sem("lru_input_gated"), sem("x_final")
    a_ready, m_ready, mult_ready, yc_ready = sem("lru_decay"), sem("lru_square"), sem("lru_mult"), sem("lru_out")
    rate_in, rate_ready = sem("lru_rate_exp"), sem("lru_rate_ready")

    scale_ready, rates_full = sem("norm_scale_ready"), sem("rates_full")
    dsq_ready, dsq_used, dsum_full = sem("head_square_ready"), sem("head_square_used"), sem("head_sums_full")
    droot_ready, dinv_ready, gained = sem("head_roots_ready"), sem("head_scales_ready"), sem("gained")
    rot_full, rope_done = sem("turned_full"), sem("rope_done")
    is_full, irelu, iscore = sem("index_logits_full"), sem("index_relu"), sem("index_added")
    vtok_full, vtok_ready = sem("v_tokens_full"), sem("v_tokens_ready")
    bs_full, bshift, bexp, bp_ready = sem("dsa_scores_full"), sem("dsa_shifted"), sem("dsa_exp"), sem("dsa_probs")
    bt_full, bt_ready, bo_full, bo_ready = sem("dsa_turned"), sem("dsa_probs_t"), sem("dsa_out_full"), sem("dsa_out_taken")
    csig, silu_in, silu_out = sem("silu_sigmoid"), sem("silu_in"), sem("silu_out")
    abe_in, abe_out = sem("rates_in"), sem("rates_exp")
    g_in, gcol_full = sem("decay_logs"), sem("decay_sums")
    lbc_full, lnormed = sem("l2_scale_full"), sem("l2_normed")
    ugb_full, udt, udt_exp, ukq_full = sem("row_values_full"), sem("decay_diff"), sem("decay_exp"), sem("products_full")
    egr_ready = sem("exp_g_row_ready")
    ux_ready, ux_full, ux_copied = sem("join0_ready"), sem("join0_turned"), sem("join0_copied")
    utok_full, utok_ready, uq_ready = sem("tokens_full"), sem("tokens_scaled"), sem("query_side_ready")
    uct_ready, up1_full, up1_ready = sem("join_block_ready"), sem("join_half_full"), sem("join_half_ready")
    uxi_full, uxi_ready, uz_full, uinv_ready, uw_full, uw_ready = sem("join_full"), sem("join_x_ready"), sem("join_t_full"), sem("join_done"), sem("w_full"), sem("w_ready")
    uv_full, uv_ready, uso_full, us_ready, uo_done = sem("v_new_full"), sem("v_new_ready"), sem("step_full"), sem("state_ready"), sem("step_out_taken")
    onorm_ready, oz_ready, o_hi, o_ready = sem("out_normed"), sem("out_gated"), sem("out_hi_ready"), sem("out_lo_ready")
    gate_sig, mix_ready, mix_hi, mix_lo = sem("gate_sigmoid"), sem("mixed"), sem("mixed_hi"), sem("mixed_lo")
    meta_landed = sem("meta_landed")
    uout_full = sem("unit_out_full")
    x_saved, gate_kept = sem("x_saved"), sem("first_gate_ready")
    x_back = [sem(f"x_back_{m}") for m in range(KT)]

    def first(u):
        return META + P * (u - 1) if u else 0

    def wide(a):
        return a.rearrange("p (s t) -> p s t", s=2)

    ROW = slice(META, T)

    def pieces_of(p):
        return len(plan[p][2])

    def shares(p):
        return "mix0" in STAGES and 8 <= p < 20

    def bank_of(p):
        return 2 + p % 2 if shares(p) else p % 4

    def pair_of(p):
        for l in range(2):
            first_job = starts.get(f"layer{l}", pieces) + 24 + TOP_GATES
            if first_job <= p < first_job + UNIT_JOBS:
                return 0
            m = p - (first_job + UNIT_JOBS)
            if 0 <= m < 2 * KT:
                return (m + 1) // 2 % 2
        return p % 2

    UNITS_A = 4 * HEADS
    MEAN_AT, CENTRE_AT, VAR_AT, ROOT_AT, INV_AT, SCALE_AT, AFFINE_AT = 23, 24, 25, 26, 27, 28, 29

    block = nc.Block()
    block.__enter__()

    @block.sync
    def _(sp):
        c = Counts()

        def load_piece(p):
            n = pieces_of(p)
            sp.dma_start(raw[:, p % RAW_SLOTS, 0:n * P], stream[p, :, 0:n * P])\
                .then_inc(landed[p % RAW_SLOTS], 16)

        sp.dma_start(c1[:, :], const1).then_inc(loaded, 16)
        sp.dma_start(v1[:, :], vec1).then_inc(loaded, 16)
        for k in range(KT):
            sp.dma_start(x[:, k, ROW], xt[P * k:P * k + P, :]).then_inc(x_landed[k], 16)
            if k == 1:
                load_piece(0)
        for p in range(1, RAW_SLOTS):
            load_piece(p)
        sp.dma_start(distance, dist).then_inc(dist_landed, 16)
        if "layer0" in STAGES:
            sp.dma_start(x[:, :, 0:META], meta.rearrange("(k p) t -> p k t", p=P)).then_inc(meta_landed, 16)
            sp.dma_start(v2[:, :, :], vec2).then_inc(meta_landed, 16)
            sp.dma_start(c2[:, :], const2).then_inc(meta_landed, 16)

        def save_x(l):
            norms = 4 + 2 * l if "mix0" in STAGES else 2 * l
            sp.wait_ge(n_ready, KT * (norms + 1))
            sp.dma_start(saved_x.rearrange("(k p) t -> p k t", p=P), x[:, :, :]).then_inc(x_saved, 16)
            sp.wait_ge(x_saved, 16 * (l + 1))

        def restore_x(l, m):
            sp.wait_ge(mix_ready, KT * l + m + 1)
            sp.dma_start(x[:, m, :], saved_x[P * m:P * m + P, :]).then_inc(x_back[m], 16)

        also = {}
        for l in range(2):
            if f"layer{l}" in starts:
                first_piece = starts[f"layer{l}"]
                also[first_piece + RAW_SLOTS] = (save_x, l)
                for m in range(KT):
                    also[first_piece + BRANCHES + 2 * m + 7] = (restore_x, l, m)

        for p in range(RAW_SLOTS, pieces):
            sp.wait_ge(w_lo, p - RAW_SLOTS + 1)
            load_piece(p)
            if p in also:
                also[p][0](*also[p][1:])
            if p == starts.get("mix1", -9) + 3:
                sp.wait_ge(taken, starts["mix1"])
                sp.dma_start(lw[:, :, :], lru_w).then_inc(lru_landed, 16)
        for k in range(KT):
            if STAGES[-1] == "final":
                sp.wait_ge(x_final, k + 1)
            else:
                sp.wait_ge(taken, pieces - KT + k + 1)
            sp.dma_start(out[P * k:P * k + P, :], x[:, k, ROW]).then_inc(stored, 16)
        sp.wait_ge(stored, 16 * KT)

    @block.gpsimd
    def _(pool):
        assert pieces % W_SLOTS == 0 and RAW_SLOTS == W_SLOTS
        with nc.Fori(0, pieces, W_SLOTS, engines=(mybir.EngineType.Pool,)) as p:
            for slot in range(W_SLOTS):
                pool.wait_ge(w_hi, p + slot + 1)
                pool.tensor_tensor(wl[:, slot, :], raw[:, slot, :], wh[:, slot, :].bitcast(F32), ALU.subtract)\
                    .then_inc(w_lo, 1)


    @block.tensor
    def _(pe):
        c = Counts()
        at = {"piece": 0, "both": False, "block": 0}

        def product(job, hi, lo, cols, wait=None):
            p = at["piece"]
            pe.wait_ge(w_lo, p + 1)
            one = cols == SEQ
            slots = 4 if one and not shares(job) else 2
            if job >= slots:
                pe.wait_ge(taken, job if at["both"] else job - slots + 1)
            at["both"] = False
            n, last = pieces_of(p), None
            for b in range(n):
                if wait is not None:
                    pe.wait_ge(wait, c.next(wait))
                for i, (w, v) in enumerate(((wh, hi), (wh, lo), (wl, hi))):
                    for s in range(1 if one else 2):
                        o = acc[:, bank_of(job), :] if one else acc[:, 2 * pair_of(job) + s, 0:HALF]
                        r = v[:, b, ROW] if one else v[:, b, HALF * s:HALF * s + HALF]
                        last = pe.matmul(o, w[:, p % W_SLOTS, P * b:P * b + P], r,
                                         start=(b == 0 and i == 0), stop=(b == n - 1 and i == 2))
            last.then_inc(w_used, 1)
            at["piece"] = p + 1

        def square_sum(cols):
            pe.wait_ge(sq_added, c.next(sq_added, KT))
            if cols == SEQ:
                pe.matmul(aux[:, 0, :], ones, ssq[:, ROW], start=True, stop=True).then_inc(ss_full, 1)
            else:
                pe.matmul(aux[:, 0, 0:HALF], ones, ssq[:, 0:HALF], start=True, stop=True)
                pe.matmul(aux[:, 1, 0:HALF], ones, ssq[:, HALF:T], start=True, stop=True)\
                    .then_inc(ss_full, 1)

        def jobs(n, cols=SEQ, fresh=None, hi=nh, lo=nl):
            for i in range(n):
                product(at["piece"], hi, lo, cols, fresh if i == 0 else None)

        def mixer0():
            square_sum(SEQ)
            jobs(8, fresh=n_ready)
            pe.wait_ge(root_ready, c.next(root_ready))

            def v_by_token(pair):
                pe.wait_ge(taken, at["piece"])
                if pair >= 2:
                    pe.wait_ge(o_copied, pair - 1)
                for a in range(4):
                    mm = pe.transpose(acc[:, pair % 2, P * a:P * a + P], vs[:, pair, P * a:P * a + P], ident)
                mm.then_inc(vt_full, 1)

            def turn(u):
                h, i = divmod(u, 4)
                pe.wait_ge(p_ready, u + 1)
                if u >= 2:
                    pe.wait_ge(pt_ready, u - 1)
                for b in range(i + 1):
                    mm = pe.transpose(aux[:, 2 + u % 2, P * b:P * b + P], sm[:, u % 4, P * b:P * b + P], ident)
                mm.then_inc(pt_full, 1)

            def values(u):
                h, i = divmod(u, 4)
                po, pair = DH * (h % 2), h // 2
                pe.wait_ge(pt_ready, u + 1)
                if u % 8 == 0:
                    pe.wait_ge(vt_copied, pair + 1)
                for b in range(i + 1):
                    mm = pe.matmul(acc[po:po + DH, pair % 2, P * i:P * i + P],
                                   vt[:, b, DH * h:DH * h + DH], pt[:, u % 2, P * b:P * b + P],
                                   start=(b == 0), stop=(b == i))
                mm.then_inc(o_full, 1)

            jobs(3)
            v_by_token(0)
            for u in range(UNITS_A + 3):
                if u < UNITS_A:
                    h, i = divmod(u, 4)
                    po, w = DH * (h % 2), P * (i + 1)
                    if u == 0:
                        pe.wait_ge(taken, at["piece"])
                    if u >= 2:
                        pe.wait_ge(s_shift, u - 1)
                    pe.matmul(aux[:, u % 2, 0:w], qs[po:po + DH, h // 2, P * i:P * i + P],
                              ks[po:po + DH, h // 2, 0:w], start=True, stop=True).then_inc(s_full, 1)
                if 2 <= u < UNITS_A + 2:
                    turn(u - 2)
                if u >= 3:
                    values(u - 3)
                if u < UNITS_A - 8 and u % 8 in (1, 3, 5):
                    jobs(1)
                if u < UNITS_A - 8 and u % 8 == 7:
                    v_by_token(u // 8 + 1)
                if u == MEAN_AT:
                    pe.wait_ge(taken, at["piece"])
                    pe.wait_ge(conv_ready, c.next(conv_ready, 4))
                    for i in range(4):
                        mm = pe.matmul(acc[:, 2, :], ones, cv[:, i, :], start=(i == 0), stop=(i == 3))
                    mm.then_inc(mean_full, 1)
                if u == VAR_AT:
                    for i in range(4):
                        pe.wait_ge(ln_sq, c.next(ln_sq))
                        mm = pe.matmul(acc[:, 3, :], ones, zpad[:, i, 0:SEQ], start=(i == 0), stop=(i == 3))
                    mm.then_inc(var_full, 1)
            pe.wait_ge(y_ready, c.next(y_ready, 8))
            jobs(KT)

        def mixer1():
            square_sum(SEQ)
            jobs(KT, fresh=n_ready)
            pe.wait_ge(root_ready, c.next(root_ready))
            pe.wait_ge(lru_landed, 16)
            for h in range(KT):
                jobs(1)
                pe.wait_ge(xc_ready, h + 1)
                if h >= 2:
                    pe.wait_ge(ri_sig, h - 1)
                for g in range(2):
                    mm = pe.matmul(aux[:, 2 * (h % 2) + g, :], lw[:, LRU_HEADS * g + h, :], xc[:, h, :],
                                   start=True, stop=True)
                mm.then_inc(ri_full, 1)
            pe.wait_ge(ri_sig, KT)
            jobs(KT, fresh=y_ready)

        def mlp1():
            square_sum(SEQ)
            for n, (what, q) in enumerate(mlp_order()):
                if what == "up":
                    jobs(KT, fresh=n_ready if n == 0 else None)
                    if n == 0:
                        pe.wait_ge(root_ready, c.next(root_ready))
                else:
                    jobs(KT, fresh=h_ready, hi=hid_hi[:, q % 2], lo=hid_lo[:, q % 2])

        def rows_sum(n, count, which):
            pe.wait_ge(dsq_ready, c.next(dsq_ready))
            for s in range(2):
                mm = pe.matmul(aux[0:8, s, 0:HALF], const("rows")[:, 8 * n:8 * n + 8],
                               sqb[:, which % 2, HALF * s:HALF * s + HALF], start=(n == 0), stop=(n == count - 1))
            mm.then_inc(dsq_used if n < count - 1 else dsum_full, 1)

        def spread(n, pair):
            for s in range(2):
                mm = pe.matmul(aux[:, 2 * pair + s, 0:HALF], ident[0:8, n:n + 1].to_broadcast([8, P]),
                               rt[0:8, HALF * s:HALF * s + HALF], start=True, stop=True)
            return mm

        def layer(l):
            square_sum(T)
            jobs(2, T, fresh=n_ready)
            pe.wait_ge(root_ready, c.next(root_ready))
            pe.wait_ge(taken, at["piece"] - 1)
            for u in range(UNITS):
                mm = pe.transpose(aux[:, 2, 16 * u:16 * u + 16], ub[0:16, 0, first(u):first(u) + P], ident[0:16, 0:16])
            mm.then_inc(rates_full, 1)
            jobs(10, T)
            for n in range(6):
                rows_sum(n, 6, n)
            jobs(2, T)
            pe.wait_ge(dinv_ready, c.next(dinv_ready))
            pe.wait_ge(gained, c.next(gained, 6))
            tiles = [(ik[:, :], "turn_i", 0)] + [(iq[:, i, :], "turn_i", None) for i in range(4)] \
                + [(bq[:, i, :], "turn_a", 1 + i) for i in range(4)] + [(bk[:, :], "turn_a", 5)]
            for n, (t, turn, row) in enumerate(tiles):
                if n:
                    pe.wait_ge(rope_done, c.next(rope_done))
                for s in range(2):
                    mm = pe.matmul(aux[:, s, 0:HALF], const(turn), t[:, HALF * s:HALF * s + HALF],
                                   start=True, stop=True)
                if row is not None:
                    mm = spread(row, 1)
                mm.then_inc(rot_full, 1)
                jobs(1, T)
            pe.wait_ge(rope_done, c.next(rope_done))
            n = 0
            base = c.at(irelu)
            for j in range(1, 4):
                for h in range(IDX_HEADS):
                    if n >= 4:
                        pe.wait_ge(irelu, base + n - 3)
                    po, w = 64 * (h % 2), P * (j + 1)
                    pe.matmul(aux[:, n % 4, 0:w], iq[po:po + 64, h // 2, META + P * j:META + P * j + P],
                              ik[po:po + 64, META:META + w], start=True, stop=True).then_inc(is_full, 1)
                    n += 1
            pe.wait_ge(irelu, c.next(irelu, n))
            for u in range(UNITS):
                mm = pe.transpose(aux[:, u // 4, P * (u % 4):P * (u % 4) + P], bv[:, first(u):first(u) + P], ident)
            mm.then_inc(vtok_full, 1)
            pe.wait_ge(vtok_ready, c.next(vtok_ready))
            for n in range(8):
                rows_sum(n, 8, n)
            jobs(1, T)
            pe.wait_ge(dinv_ready, c.next(dinv_ready))
            base = c.at(lnormed)
            for n in range(8):
                if n >= 2:
                    pe.wait_ge(lnormed, base + n - 1)
                spread(n, n % 2).then_inc(lbc_full, 1)
                if n in (1, 3, 5):
                    jobs(1, T)
            pe.wait_ge(lnormed, c.next(lnormed, 8))
            pe.wait_ge(g_in, c.next(g_in))
            pe.matmul(aux[:, 0, 0:20], const("until"), gt[:, 1, :], start=True, stop=True)
            pe.matmul(aux[:, 0, 32:52], const("same"), gt[:, 1, :], start=True, stop=True).then_inc(gcol_full, 1)
            pe.wait_ge(g_in, c.next(g_in))
            pe.wait_ge(taken, at["piece"])
            attention()
            for u in range(UNITS):
                unit(u)
            pe.wait_ge(us_ready, c.next(us_ready))
            for n in range(4):
                rows_sum(n, 4, n)
            jobs(1, T)
            pe.wait_ge(dinv_ready, c.next(dinv_ready))
            base = c.at(onorm_ready)
            for n in range(4):
                if n >= 2:
                    pe.wait_ge(onorm_ready, base + n - 1)
                spread(n, n % 2).then_inc(lbc_full, 1)
            pe.wait_ge(onorm_ready, c.next(onorm_ready, 4))
            pe.wait_ge(o_ready, c.next(o_ready, 8))
            for m in range(KT):
                if m + 1 < KT:
                    jobs(1, T)
                branch(m)
            jobs(KT, T, fresh=mix_lo, hi=yh, lo=yl)
            square_sum(T)
            for n, (what, g) in enumerate(FFN_ORDER):
                a, b = FFN_THIRDS[g]
                if what == "up":
                    jobs(2 * (b - a), T, fresh=n_ready if n == 0 else None)
                    if n == 0:
                        pe.wait_ge(root_ready, c.next(root_ready))
                else:
                    jobs(KT, T, fresh=h_ready, hi=hid_hi[:, g % 2], lo=hid_lo[:, g % 2])

        def branch(m):
            p = at["piece"]
            pe.wait_ge(w_lo, p + 1)
            if m:
                pe.wait_ge(taken, p - 1 if m < KT - 1 else p)
            for g in range(2):
                for b in range(4 * g, 4 * g + 4):
                    for i, (w, v) in enumerate(((wh, oh), (wh, ol), (wl, oh))):
                        for s in range(2):
                            mm = pe.matmul(aux[:, 2 * g + s, 0:HALF], w[:, p % W_SLOTS, P * b:P * b + P],
                                           v[:, b, HALF * s:HALF * s + HALF],
                                           start=(b == 4 * g and i == 0), stop=(b == 4 * g + 3 and i == 2))
            mm.then_inc(w_used, 1)
            at["piece"] = p + 1

        def fill(blocks):
            p = at["piece"]
            if blocks and at["block"] == 0:
                pe.wait_ge(w_lo, p + 1)
                pe.wait_ge(taken, p)
            for _ in range(blocks):
                b = at["block"]
                for i, (w, v) in enumerate(((wh, nh), (wh, nl), (wl, nh))):
                    for s in range(2):
                        mm = pe.matmul(acc[:, s, 0:HALF], w[:, p % W_SLOTS, P * b:P * b + P],
                                       v[:, b, HALF * s:HALF * s + HALF],
                                       start=(b == 0 and i == 0), stop=(b == KT - 1 and i == 2))
                at["block"] = b + 1
            if at["block"] == KT:
                mm.then_inc(w_used, 1)
                at.update(piece=p + 1, block=0, both=True)

        def heads(bank, make):
            for h in range(A_HEADS):
                mm = make(bank[:, P * h:P * h + P], h)
            return mm

        def mm_(out, lhs, rhs, start=True, stop=True):
            return pe.matmul(out, lhs, rhs, start=start, stop=stop)

        def unit(u):
            cs = slice(first(u), first(u) + P)
            heads(aux[:, 0, :], lambda o, h: mm_(o, gt[:, 1, 4 * u + h:4 * u + h + 1].to_broadcast([P, P]), const("until")))\
                .then_inc(ugb_full, 1)
            heads(aux[:, 2, :], lambda o, h: mm_(o, dk[:, h, cs], dk[:, h, cs]))
            heads(acc[:, 2, :], lambda o, h: pe.transpose(o, dk[:, h, cs], ident))
            heads(acc[:, 3, :], lambda o, h: pe.transpose(o, dv[:, h, cs], ident)).then_inc(utok_full, 1)
            if u:
                pe.wait_ge(uo_done, c.next(uo_done))
            heads(aux[:, 1, :], lambda o, h: mm_(o, gt[:, 0, 4 * u + h:4 * u + h + 1].to_broadcast([P, P]), ident))
            heads(aux[:, 3, :], lambda o, h: mm_(o, dk[:, h, cs], dq[:, h, cs])).then_inc(ukq_full, 1)
            if at["block"]:
                fill(KT - 1 - at["block"])
            pe.wait_ge(ux_ready, c.next(ux_ready))
            heads(aux[:, 0, :], lambda o, h: pe.transpose(o, xit[:, h, :], ident)).then_inc(ux_full, 1)
            if at["block"]:
                fill(1)
            more = 1 if u < FILLED else 0
            pe.wait_ge(ux_copied, c.next(ux_copied))
            for n in range(1, LEVELS):
                pe.wait_ge(uct_ready, c.next(uct_ready))
                if n > 1:
                    pe.wait_ge(uxi_ready, c.next(uxi_ready))
                heads(aux[:, 0, :], lambda o, h: mm_(o, ct[:, h, :], xi[:, h, :])).then_inc(up1_full, 1)
                fill(more)
                if n > 1:
                    pe.wait_ge(uinv_ready, c.next(uinv_ready))
                pe.wait_ge(up1_ready, c.next(up1_ready))
                if n < LEVELS - 1:
                    heads(aux[:, 1, :], lambda o, h: mm_(o, xit[:, h, :], p1[:, h, :])).then_inc(uxi_full, 1)
                heads(aux[:, 2, :], lambda o, h: mm_(o, p1[:, h, :], xit[:, h, :])).then_inc(uz_full, 1)
                fill(more)
            pe.wait_ge(uinv_ready, c.next(uinv_ready))
            pe.wait_ge(utok_ready, c.next(utok_ready))
            heads(acc[:, 2, :], lambda o, h: mm_(o, kbg[:, h, :], xit[:, h, :])).then_inc(uw_full, 1)
            pe.wait_ge(uw_ready, c.next(uw_ready))
            pe.wait_ge(uq_ready, c.next(uq_ready))
            for cc in range(1 if u == 0 else 2):
                r = slice(64 * cc, 64 * cc + 64)
                pe.wait_ge(us_ready, c.next(us_ready))
                for h in range(A_HEADS):
                    o = aux[r, 0, P * h:P * h + P]
                    mm_(o, xit[:, h, r], vb[:, h, :], True, False)
                    mm = mm_(o, nwt[:, h, r], state_of(u, cc)[:, h, :], False, True)
                mm.then_inc(uv_full, 1)
                fill(more)
                pe.wait_ge(uv_ready, c.next(uv_ready))
                heads(aux[:, 1, :], lambda o, h: mm_(o, kg[r, h, :], vn[r, h, :])).then_inc(uso_full, 1)
                for h in range(A_HEADS):
                    o = aux[:, 3, P * h + 64 * cc:P * h + 64 * cc + 64]
                    mm_(o, state_of(u, cc)[:, h, :], qg[:, h, r], True, False)
                    mm = mm_(o, vn[r, h, :], qkt[r, h, r], False, True)
                if cc or u == 0:
                    mm.then_inc(uout_full, 1)
                if u and cc == 0:
                    fill(more)
            if u == UNITS - 1:
                pe.wait_ge(uo_done, c.next(uo_done))

        def attention():
            n, t = 0, 0
            shifted, turned, outs = c.at(bshift), c.at(bt_ready), c.at(bo_ready)
            for j in range(4):
                w = META + P * (j + 1)
                for h in range(B_HEADS):
                    if n >= 2:
                        pe.wait_ge(bshift, shifted + n - 1)
                    for s in range(2):
                        mm = pe.matmul(aux[:, 2 * (h % 2) + s, 0:w // 2], bq[:, h, META + P * j:META + P * j + P],
                                       bk[:, s * (w // 2):(s + 1) * (w // 2)], start=True, stop=True)
                    mm.then_inc(bs_full, 1)
                    n += 1
                pe.wait_ge(bp_ready, c.next(bp_ready, 4))
                for b in range(j + 3):
                    if b < j + 2:
                        rows = P if b else META
                        if t + b >= 2:
                            pe.wait_ge(bt_ready, turned + t + b - 1)
                        for h in range(B_HEADS):
                            mm = pe.transpose(acc[0:rows, (t + b) % 2, P * h:P * h + P],
                                              pb[:, h, first(b):first(b) + rows], ident)
                        mm.then_inc(bt_full, 1)
                    if b == 0:
                        if j >= 2:
                            pe.wait_ge(bo_ready, outs + j - 1)
                        continue
                    v, rows = b - 1, P if b > 1 else META
                    pe.wait_ge(bt_ready, turned + t + v + 1)
                    mm = pe.matmul(acc[:, 2 + j % 2, :], vtok[0:rows, v, :], sb_[0:rows, (t + v) % 2, 0:512],
                                   start=(v == 0), stop=(v == j + 1))
                t += j + 2
                mm.then_inc(bo_full, 1)
            pe.wait_ge(bshift, c.next(bshift, n))
            for h in range(B_HEADS):
                mm = pe.matmul(aux[0:META, 0, META * h:META * h + META], bq[:, h, 0:META], bk[:, 0:META],
                               start=True, stop=True)
            mm.then_inc(bs_full, 1)
            pe.wait_ge(bp_ready, c.next(bp_ready))
            c.next(bshift)
            c.next(bt_ready, t)
            pe.wait_ge(bt_ready, c.at(bt_ready))
            for h in range(B_HEADS):
                mm = pe.transpose(acc[0:META, 0, META * h:META * h + META], pb[0:META, h, 0:META], ident[0:META, 0:META])
            mm.then_inc(bt_full, 1)
            pe.wait_ge(bt_ready, c.next(bt_ready))
            pe.wait_ge(bo_ready, c.next(bo_ready, 4))
            pe.matmul(acc[:, 2, 0:4 * META], vtok[0:META, 0, :], sb_[0:META, 0, 0:4 * META],
                      start=True, stop=True).then_inc(bo_full, 1)
            pe.wait_ge(bo_ready, c.next(bo_ready))

        for stage in STAGES:
            if stage == "mix0":
                mixer0()
            if stage == "mix1":
                mixer1()
            if stage in ("mlp0", "mlp1"):
                mlp1()
            if stage == "final":
                square_sum(SEQ)
                pe.wait_ge(root_ready, c.next(root_ready))
            if stage in ("layer0", "layer1"):
                layer(int(stage[-1]))

    @block.scalar
    def _(act):
        c = Counts()
        at = {"piece": 0, "split": 0, "squared": False}

        def split(p):
            while at["split"] <= min(p, pieces - 1):
                q = at["split"]
                act.wait_ge(landed[q % RAW_SLOTS], 16 * (q // RAW_SLOTS + 1))
                if q >= W_SLOTS:
                    act.wait_ge(w_used, q - W_SLOTS + 1)
                n = pieces_of(q) * P
                act.activation(wh[:, q % W_SLOTS, 0:n], raw[:, q % RAW_SLOTS, 0:n], ACT.Copy)\
                    .then_inc(w_hi, 1)
                at["split"] = q + 1

        def job():
            p = at["piece"]
            split(p + AHEAD)
            at["piece"] = p + 1
            return p

        def square(k, s):
            if k >= 2:
                act.wait_ge(sq_added, c.at(sq_added) + k - 1)
            act.activation(sqb[:, k % 2, s], x[:, k, s], ACT.Square).then_inc(sq_ready, c.made(sq_ready))

        def last_jobs(cols, norm_next=True):
            for k in range(KT):
                p = job()
                if norm_next and k:
                    act.wait_ge(taken, p)
                    square(k - 1, ROW if cols == SEQ else slice(0, T))
            at["squared"] = norm_next

        def norm(gains, cols, first=False, after=None):
            split(at["piece"] + AHEAD)
            s = ROW if cols == SEQ else slice(0, T)

            def high(k):
                if gains is not None:
                    act.activation(nh[:, k, s], x[:, k, s], ACT.Copy, scale=gains(k)).then_inc(n_hi, c.made(n_hi))

            if at["squared"]:
                act.wait_ge(taken, at["piece"])
                square(KT - 1, s)
            if at["piece"]:
                act.wait_ge(w_used, at["piece"])
            for k in range(KT):
                if not at["squared"]:
                    if after is not None:
                        act.wait_ge(after, c.next(after))
                    elif first:
                        act.wait_ge(x_landed[k], 16)
                    else:
                        act.wait_ge(taken, at["piece"] - KT + k + 1)
                    square(k, s)
                high(k)
            at["squared"] = False
            c.next(sq_added, KT)
            root(cols)

        def root(cols):
            act.wait_ge(ss_full, c.next(ss_full))
            if cols == SEQ:
                act.activation(rt[:, ROW], aux[:, 0, :], ACT.Sqrt, scale=1.0 / D, bias=eps[:, 0:1])\
                    .then_inc(root_ready, c.made(root_ready))
            else:
                act.activation(rt[:, :].rearrange("p (s t) -> p s t", s=2), aux[:, 0:2, 0:HALF], ACT.Sqrt,
                               scale=1.0 / D, bias=eps[:, 0:1]).then_inc(root_ready, c.made(root_ready))

        def mixer0():
            norm(lambda k: vec("mix_norm", k), SEQ, first=True)
            for i in range(4):
                p = job()
                act.wait_ge(taken, p + 1)
                act.activation(sb_[:, i % 2, 0:SEQ], ub[:, i % 2, 0:SEQ], ACT.Sigmoid)\
                    .then_inc(sig_ready, c.made(sig_ready))
                job()
            def copy_v(pair):
                act.wait_ge(vt_full, c.next(vt_full))
                act.activation(vt[:, :, P * pair:P * pair + P], acc[:, pair % 2, :].rearrange("p (a d) -> p a d", a=4),
                               ACT.Copy).then_inc(vt_copied, c.made(vt_copied))

            def copy_probs(u):
                act.wait_ge(pt_full, u + 1)
                if u >= 2:
                    act.wait_ge(o_full, u - 1)
                w = P * (u % 4 + 1)
                act.activation(pt[:, u % 2, 0:w], aux[:, 2 + u % 2, 0:w], ACT.Copy).then_inc(pt_ready, c.made(pt_ready))

            def heads_out(pair):
                act.wait_ge(o_full, 8 * pair + 8)
                act.activation(qs[:, pair, :], acc[:, pair % 2, :], ACT.Copy).then_inc(o_copied, c.made(o_copied))

            def heads_high(pair):
                act.wait_ge(o_copied, pair + 1)
                if pair == 0:
                    act.wait_ge(w_used, at["piece"])
                act.activation(nh[:, 4 + pair, ROW], qs[:, pair, :], ACT.Copy).then_inc(y_hi, c.made(y_hi))

            for _ in range(3):
                job()
            copy_v(0)
            for u in range(UNITS_A + 4):
                if u < UNITS_A:
                    act.wait_ge(s_shift, u + 1)
                    w, b = P * (u % 4 + 1), u % 2
                    act.activation(sm[:, u % 4, 0:w], sm[:, u % 4, 0:w], ACT.Exp, bias=small[:, 1, b:b + 1],
                                   accum_out=small[:, 2, b:b + 1]).then_inc(s_exp, c.made(s_exp))
                if 2 <= u < UNITS_A + 2:
                    copy_probs(u - 2)
                if u >= 4 and (u - 4) % 8 == 7:
                    heads_out((u - 4) // 8)
                if u < UNITS_A - 8 and u % 8 in (1, 3, 5):
                    job()
                if u < UNITS_A - 8 and u % 8 == 7:
                    copy_v(u // 8 + 1)
                if u == CENTRE_AT:
                    for i in range(4):
                        act.wait_ge(cent_ready, c.next(cent_ready))
                        act.activation(zpad[:, i, 0:SEQ], cv[:, i, :], ACT.Square).then_inc(ln_sq, c.made(ln_sq))
                if u == ROOT_AT:
                    act.wait_ge(var_full, c.next(var_full))
                    act.activation(rt[:, 0:SEQ], acc[:, 3, :], ACT.Sqrt, scale=1.0 / CONV_CH, bias=eps[:, 0:1])\
                        .then_inc(ln_root, c.made(ln_root))
                if u == AFFINE_AT:
                    for i in range(4):
                        act.wait_ge(ln_scaled, c.next(ln_scaled))
                        act.activation(zpad[:, i, 0:SEQ], cv[:, i, :], ACT.Identity, scale=vec("ab_ln_g", i),
                                       bias=vec("ab_ln_b", i)).then_inc(act_seq, c.made(act_seq))
                        act.activation(cv[:, i, :], cv[:, i, :], ACT.Sigmoid, scale=vec("ab_ln_g", i),
                                       bias=vec("ab_ln_b", i)).then_inc(ln_act, c.made(ln_act))
                if u == UNITS_A - 1:
                    for pair in range(3):
                        heads_high(pair)
                    for i in range(4):
                        act.wait_ge(ln_out, c.next(ln_out))
                        act.activation(nh[:, i, ROW], zpad[:, i, 0:SEQ], ACT.Copy).then_inc(y_hi, c.made(y_hi))
            heads_high(3)
            last_jobs(SEQ, STAGES[-1] != "mix0")

        def mixer1():
            act.wait_ge(rate_in, 1)
            act.activation(c8[:, 1, :], c8[:, 0, :], ACT.Exp, scale=-1.0).then_inc(rate_ready, c.made(rate_ready))
            norm(lambda k: vec("mix_norm", 8 + k), SEQ)
            for _ in range(KT):
                job()
            act.wait_ge(rate_in, 2)
            for h in range(KT):
                job()
                act.wait_ge(g_ready, c.next(g_ready))
                act.activation(sb_[:, h % 2, 0:SEQ], sb_[:, h % 2, 0:SEQ], ACT.Sigmoid,
                               scale=2.0 * math.sqrt(2.0 / math.pi)).then_inc(gsig_ready, c.made(gsig_ready))
                act.wait_ge(ri_full, c.next(ri_full))
                act.activation(rb[:, h, :], aux[:, 2 * (h % 2), :], ACT.Sigmoid, bias=vec("c_b_r", h))\
                    .then_inc(act_seq, c.made(act_seq))
                done = c.mine()
                if h >= 2:
                    act.wait_ge(xc_gated, h - 1)
                act.activation(ub[:, h % 2, 0:SEQ], aux[:, 2 * (h % 2) + 1, :], ACT.Sigmoid, bias=vec("c_b_i", h))\
                    .then_inc(ri_sig, c.made(ri_sig))
                act.wait_ge(*done)
                act.activation(tb[:, h, :], rb[:, h, :], ACT.Tanh, scale=c8[:, 2, h:h + 1])\
                    .then_inc(tanh_ready, c.made(tanh_ready))
            for h in range(KT):
                act.activation(rb[:, h, :], rb[:, h, :], ACT.Exp, scale=c8[:, 3, h:h + 1])\
                    .then_inc(a_ready, c.made(a_ready))
            for h in range(KT):
                act.wait_ge(m_ready, c.next(m_ready))
                act.activation(tb[:, h, :], tb[:, h, :], ACT.Sqrt).then_inc(mult_ready, c.made(mult_ready))
            act.wait_ge(w_used, at["piece"])
            for h in range(KT):
                act.wait_ge(yc_ready, c.next(yc_ready))
                act.activation(nh[:, h, ROW], xc[:, h, :], ACT.Copy).then_inc(y_hi, c.made(y_hi))
            last_jobs(SEQ, STAGES[-1] != "mix1")

        def mlp1(layer):
            norm(lambda k: vec("mlp_norm", 8 * layer + k), SEQ)
            for what, q in mlp_order():
                if (what, q) == ("down", QUARTERS - 1):
                    last_jobs(SEQ, STAGES[-1] != f"mlp{layer}")
                    continue
                for m in range(KT):
                    p = job()
                    if what == "up":
                        act.wait_ge(h_sq, c.next(h_sq))
                        act.activation(hid_hi[:, q % 2, m, ROW], sb_[:, m % 2, 0:SEQ], ACT.Copy)\
                            .then_inc(h_hi, c.made(h_hi))

        def square_rows(tiles, gains=None):
            base = c.at(dsq_used)
            for n, (t, ready) in enumerate(tiles):
                if ready is not None:
                    act.wait_ge(*ready)
                if n >= 2:
                    act.wait_ge(dsq_used, base + n - 1)
                act.activation(sqb[:, n % 2, :], t, ACT.Square).then_inc(dsq_ready, c.made(dsq_ready))
                if gains is not None:
                    act.activation(t, t, ACT.Copy, scale=gains[n]).then_inc(gained, c.made(gained))
            c.next(dsq_used, len(tiles) - 1)

        def row_roots(factor):
            act.wait_ge(dsum_full, c.next(dsum_full))
            act.activation(wide(rt[0:8, :]), aux[0:8, 0:2, 0:HALF], ACT.Sqrt, scale=factor, bias=eps[0:8, 0:1])\
                .then_inc(droot_ready, c.made(droot_ready))

        def layer(l):
            def vec(name, n=0, count=1):
                return vec2_(l, name, n, count)

            def gate_tile(m, p):
                act.wait_ge(taken, p + 1)
                act.activation(x[:, m, :], x[:, m, :], ACT.Sigmoid, bias=vec("b_gate_2", m))\
                    .then_inc(gate_kept, c.made(gate_kept))

            if l == 0:
                act.wait_ge(meta_landed, 48)
            norm(lambda k: vec("norm_mix_2", k), T, after=x_final if l == 0 else None)
            p0 = at["piece"]
            for _ in range(12):
                job()
            tiles = [(ik[:, :], (taken, p0 + 2))] + [(bq[:, i, :], (taken, p0 + 7 + i)) for i in range(4)] \
                + [(bk[:, :], (taken, p0 + 11))]
            square_rows(tiles, [vec("kidx_norm_2")] + [vec("q_norm_2")] * 4 + [vec("k_norm_2")])
            row_roots(1.0 / P)
            act.wait_ge(abe_in, c.next(abe_in))
            act.activation(gt[:, 4, :], gt[:, 3, :], ACT.Exp, scale=-1.0).then_inc(act_seq, c.made(act_seq))
            act.activation(gt[:, 9, 0:4], vec("a_log_2", 0, 4), ACT.Exp).then_inc(act_seq, c.made(act_seq))
            act.activation(gt[:, 0, :].rearrange("p (u h) -> p u h", h=4), abt[:, :, 4:8], ACT.Sigmoid)\
                .then_inc(abe_out, c.made(abe_out))
            for n in range(12):
                job()
                t = ((dk, dq, dv)[n % 3])[:, n // 3, :]
                act.wait_ge(silu_in, c.next(silu_in))
                if n >= 2:
                    act.wait_ge(silu_out, c.at(silu_out) + n - 1)
                act.activation(sb_[:, n % 2, :], t, ACT.Sigmoid).then_inc(csig, c.made(csig))
            n = 0
            base = c.at(iscore)
            for j in range(1, 4):
                for h in range(IDX_HEADS):
                    w = P * (j + 1)
                    act.wait_ge(is_full, c.next(is_full))
                    if n >= 2:
                        act.wait_ge(iscore, base + n - 1)
                    act.activation(sqb[:, n % 2, 0:w], aux[:, n % 4, 0:w], ACT.Relu).then_inc(irelu, c.made(irelu))
                    n += 1
            c.next(iscore, n)
            c.next(silu_out, 12)
            act.wait_ge(vtok_full, c.next(vtok_full))
            act.activation(vtok[:, 0:4, :], aux[:, 0, :].rearrange("p (u d) -> p u d", u=4), ACT.Copy)\
                .then_inc(act_seq, c.made(act_seq))
            act.activation(vtok[:, 4, :], aux[:, 1, 0:P], ACT.Copy).then_inc(vtok_ready, c.made(vtok_ready))
            act.wait_ge(silu_out, c.at(silu_out))
            act.wait_ge(iscore, c.at(iscore))
            square_rows([(dq[:, h, :], None) for h in range(4)] + [(dk[:, h, :], None) for h in range(4)])
            row_roots(1.0)
            for m in range(TOP_GATES):
                gate_tile(m, job())
            act.wait_ge(g_in, c.next(g_in, 2))
            act.activation(gt[:, 5, :], gt[:, 3, :], ACT.Exp).then_inc(act_seq, c.made(act_seq))
            act.activation(gt[:, 6, :], gt[:, 4, :], ACT.Exp).then_inc(abe_out, c.made(abe_out))
            attention()
            for u in range(UNITS):
                unit(u, gate_tile)
            c.next(silu_out, A_HEADS)
            c.next(uo_done)
            square_rows([(dq[:, h, :], (uo_done, c.at(uo_done))) for h in range(4)])
            row_roots(1.0 / P)

            def second_gate(m, p):
                act.wait_ge(taken, p + 1)
                act.activation(sb_[:, m % 2, :], ub[:, m % 2, :], ACT.Sigmoid, bias=vec("b_gate_2", KT + m))\
                    .then_inc(gate_sig, c.made(gate_sig))

            p = job()
            for h in range(4):
                act.wait_ge(oz_ready, c.next(oz_ready))
                act.activation(oh[:, h, :], dq[:, h, :], ACT.Copy).then_inc(o_hi, c.made(o_hi))
            for h in range(4):
                act.activation(oh[:, 4 + h, :], ob[:, h, :], ACT.Copy).then_inc(o_hi, c.made(o_hi))
            second_gate(0, p)
            for m in range(KT):
                if m + 1 < KT:
                    second_gate(m + 1, job())
                job()
                act.wait_ge(mix_ready, c.next(mix_ready))
                act.activation(yh[:, m, :], sqb[:, 0, :], ACT.Copy).then_inc(mix_hi, c.made(mix_hi))
            last_jobs(T)
            norm(lambda k: vec("norm_ffn_2", k), T)
            for what, g in FFN_ORDER:
                a, b = FFN_THIRDS[g]
                if (what, g) == FFN_ORDER[-1]:
                    last_jobs(T, STAGES[-1] != f"layer{l}")
                    continue
                if what == "down":
                    for _ in range(KT):
                        job()
                    continue
                for i in range(a, b):
                    job()
                    act.wait_ge(silu_in, c.next(silu_in))
                    act.activation(sqb[:, i % 2, :], sb_[:, i % 2, :], ACT.Sigmoid).then_inc(csig, c.made(csig))
                    job()
                    act.wait_ge(h_sq, c.next(h_sq))
                    act.activation(hid_hi[:, g % 2, i - a, :], sb_[:, i % 2, :], ACT.Copy).then_inc(h_hi, c.made(h_hi))

        def flat(t):
            return t[:, :, :].rearrange("p h i -> p (h i)")

        def fill_sigmoid(f, gate_tile):
            p = at["filled"] + f
            if f >= A_HEADS:
                gate_tile(TOP_GATES + f - A_HEADS, p)
                return
            act.wait_ge(taken, p + 1)
            if f >= 2:
                act.wait_ge(silu_out, c.at(silu_out) + f - 1)
            act.activation(sb_[:, f % 2, :], dz[:, f, :], ACT.Sigmoid).then_inc(csig, c.made(csig))

        def unit(u, gate_tile):
            act.wait_ge(ugb_full, c.next(ugb_full))
            if u:
                act.wait_ge(uo_done, c.next(uo_done))
            act.activation(flat(egr), aux[:, 0, :], ACT.Exp).then_inc(egr_ready, c.made(egr_ready))
            act.wait_ge(udt, c.next(udt))
            act.activation(flat(dt), flat(dt), ACT.Exp).then_inc(udt_exp, c.made(udt_exp))
            act.wait_ge(ux_full, c.next(ux_full))
            act.activation(flat(xi), aux[:, 0, :], ACT.Copy).then_inc(ux_copied, c.made(ux_copied))
            for n in range(1, LEVELS):
                act.wait_ge(up1_full, c.next(up1_full))
                act.activation(flat(p1), aux[:, 0, :], ACT.Copy).then_inc(up1_ready, c.made(up1_ready))
                if n == 1 and 0 < u <= FILLED:
                    fill_sigmoid(2 * u - 1, gate_tile)
                if n == LEVELS - 1 and u < FILLED:
                    fill_sigmoid(2 * u, gate_tile)
                if n in (1, LEVELS - 1) and u < FILLED:
                    p = job()
                    if u == 0 and n == 1:
                        at["filled"] = p
            act.wait_ge(uw_full, c.next(uw_full))
            act.activation(flat(nwt), acc[:, 2, :], ACT.Copy, scale=-1.0).then_inc(uw_ready, c.made(uw_ready))
            for cc in range(1 if u == 0 else 2):
                r = slice(64 * cc, 64 * cc + 64)
                act.wait_ge(uv_full, c.next(uv_full))
                act.activation(vn[r, :, :].rearrange("p h i -> p (h i)"), aux[r, 0, :], ACT.Copy)\
                    .then_inc(uv_ready, c.made(uv_ready))

        def attention():
            t = 0
            for j in range(4):
                w = META + P * (j + 1)
                for h in range(B_HEADS):
                    act.wait_ge(bshift, c.next(bshift))
                    act.activation(pb[:, h, 0:w], pb[:, h, 0:w], ACT.Exp, scale=P ** -0.5, bias=row4[:, 1, h:h + 1],
                                   accum_out=row4[:, 2, h:h + 1]).then_inc(bexp, c.made(bexp))
                for b in range(j + 2):
                    rows = P if b else META
                    act.wait_ge(bt_full, c.next(bt_full))
                    act.activation(sb_[0:rows, t % 2, 0:512], acc[0:rows, t % 2, :], ACT.Copy)\
                        .then_inc(bt_ready, c.made(bt_ready))
                    t += 1
                act.wait_ge(bo_full, c.next(bo_full))
                act.activation(ob[:, :, META + P * j:META + P * j + P],
                               acc[:, 2 + j % 2, :].rearrange("p (h q) -> p h q", h=4), ACT.Copy)\
                    .then_inc(bo_ready, c.made(bo_ready))
            act.wait_ge(bshift, c.next(bshift))
            act.activation(pb[0:META, :, 0:META], pb[0:META, :, 0:META], ACT.Exp, scale=P ** -0.5)\
                .then_inc(bexp, c.made(bexp))
            act.wait_ge(bt_full, c.next(bt_full))
            act.activation(sb_[0:META, 0, 0:4 * META], acc[0:META, 0, 0:4 * META], ACT.Copy)\
                .then_inc(bt_ready, c.made(bt_ready))
            act.wait_ge(bo_full, c.next(bo_full))
            act.activation(ob[:, :, 0:META], acc[:, 2, 0:4 * META].rearrange("p (h q) -> p h q", h=4), ACT.Copy)\
                .then_inc(bo_ready, c.made(bo_ready))

        act.wait_ge(loaded, 32)
        act.wait_ge(pad_clear, 1)
        for stage in STAGES:
            if stage == "mix0":
                mixer0()
            if stage == "mix1":
                mixer1()
            if stage in ("mlp0", "mlp1"):
                mlp1(int(stage[-1]))
            if stage == "final":
                norm(None, SEQ)
            if stage in ("layer0", "layer1"):
                layer(int(stage[-1]))

    @block.vector
    def _(dve):
        c = Counts()
        at = {"piece": 0, "squared": False}

        def step(i):
            i.then_inc(dve_seq, c.made(dve_seq))
            return c.mine()

        def full():
            p = at["piece"]
            dve.wait_ge(w_used, p + 1)
            at["piece"] = p + 1
            return acc[:, bank_of(p), :] if p < starts.get("layer0", pieces) else acc[:, 2 * pair_of(p):2 * pair_of(p) + 2, 0:HALF]

        def add_square(k, s):
            dve.wait_ge(sq_ready, c.next(sq_ready))
            if k == 0:
                dve.tensor_copy(ssq[:, s], sqb[:, 0, s]).then_inc(sq_added, c.made(sq_added))
            else:
                dve.wait_ge(sq_added, c.at(sq_added))
                dve.tensor_tensor(ssq[:, s], ssq[:, s], sqb[:, k % 2, s], ALU.add)\
                    .then_inc(sq_added, c.made(sq_added))

        def norm(gains, cols):
            s = ROW if cols == SEQ else slice(0, T)
            if at["squared"]:
                add_square(KT - 1, s)
            for k in range(KT):
                if not at["squared"]:
                    add_square(k, s)
                if gains is not None:
                    dve.wait_ge(n_hi, c.next(n_hi))
                    dve.scalar_tensor_tensor(nl[:, k, s], x[:, k, s], gains(k), nh[:, k, s].bitcast(F32),
                                             ALU.mult, ALU.subtract).then_inc(n_ready, c.made(n_ready))
            at["squared"] = False
            dve.wait_ge(root_ready, c.next(root_ready))
            dve.reciprocal(scale[:, s], rt[:, s]).then_inc(scale_ready, c.made(scale_ready))
            dve.wait_ge(*c.mine())

        def mixer0():
            norm(lambda k: vec("mix_norm", k), SEQ)
            taps = [(j, i) for two in ((0, 1), (2, 3)) for j in range(CONV_W) for i in two]
            latest = {}

            def convolve(n):
                for _ in range(min(n, len(taps))):
                    j, i = taps.pop(0)
                    dve.wait_ge(*latest[i])
                    w = vec("ab_conv_w", CONV_W * i + j)
                    if j == 0:
                        t = dve.tensor_scalar(cv[:, i, :], zpad[:, i, 0:SEQ], w, None, ALU.mult)
                    else:
                        t = dve.scalar_tensor_tensor(cv[:, i, :], zpad[:, i, j:j + SEQ], w, cv[:, i, :],
                                                     ALU.mult, ALU.add)
                    if j < CONV_W - 1:
                        latest[i] = step(t)
                    else:
                        t.then_inc(conv_ready, c.made(conv_ready))

            for i in range(4):
                a = full()
                if i >= 2:
                    dve.wait_ge(sig_ready, i - 1)
                dve.tensor_tensor(ub[:, i % 2, 0:SEQ], a, scale[:, ROW], ALU.mult).then_inc(taken, c.made(taken))
                a = full()
                dve.tensor_tensor(cv[:, i, :], a, scale[:, ROW], ALU.mult).then_inc(taken, c.made(taken))
                mine = c.mine()
                dve.wait_ge(sig_ready, i + 1)
                dve.wait_ge(*mine)
                latest[i] = step(dve.tensor_tensor(zpad[:, i, CONV_W - 1:], cv[:, i, :], sb_[:, i % 2, 0:SEQ], ALU.mult))
                if i:
                    convolve(15)
            c.next(sig_ready, 4)

            def project(n):
                a = full()
                t = (qs, ks, vs)[n % 3][:, n // 3, :]
                if n % 3 == 0:
                    dve.scalar_tensor_tensor(t, a, DH ** -0.5, scale[:, ROW], ALU.mult, ALU.mult)\
                        .then_inc(taken, c.made(taken))
                else:
                    dve.tensor_tensor(t, a, scale[:, ROW], ALU.mult).then_inc(taken, c.made(taken))

            for n in range(3):
                project(n)
                convolve(8)

            def normalise(u):
                dve.wait_ge(s_exp, u + 1)
                w, b = P * (u % 4 + 1), u % 2
                dve.wait_ge(*step(dve.reciprocal(small[:, 3, b:b + 1], small[:, 2, b:b + 1])))
                dve.tensor_scalar(sm[:, u % 4, 0:w], sm[:, u % 4, 0:w], small[:, 3, b:b + 1], None, ALU.mult)\
                    .then_inc(p_ready, c.made(p_ready))

            def low(tile, src):
                dve.wait_ge(y_hi, c.next(y_hi))
                dve.tensor_tensor(nl[:, tile, ROW], src, nh[:, tile, ROW].bitcast(F32), ALU.subtract)\
                    .then_inc(y_ready, c.made(y_ready))

            dve.wait_ge(dist_landed, 16)
            for u in range(UNITS_A + 1):
                if u < UNITS_A:
                    h, i = divmod(u, 4)
                    w, b = P * (i + 1), u % 2
                    if i == 0:
                        dve.wait_ge(*step(dve.tensor_scalar(bias[:, h % 2, :], distance,
                                                            2.0 ** (-8.0 * (h + 1) / HEADS), None, ALU.mult)))
                    dve.wait_ge(s_full, u + 1)
                    if u >= 4:
                        dve.wait_ge(pt_full, u - 3)
                    dve.wait_ge(*step(dve.tensor_tensor_reduce(
                        sm[:, u % 4, 0:w], aux[:, b, 0:w], bias[:, h % 2, SEQ - w:SEQ], 1.0, -3e38,
                        ALU.add, ALU.max, small[:, 0, b:b + 1])))
                    dve.tensor_scalar(small[:, 1, b:b + 1], small[:, 0, b:b + 1], -1.0, None, ALU.mult)\
                        .then_inc(s_shift, c.made(s_shift))
                if u >= 1:
                    normalise(u - 1)
                if u < UNITS_A - 8 and u % 8 in (2, 4, 6):
                    project(3 * (u // 8 + 1) + u % 8 // 2 - 1)
                convolve(3)
                if u == CENTRE_AT:
                    assert not taps
                    dve.wait_ge(mean_full, c.next(mean_full))
                    for i in range(4):
                        dve.scalar_tensor_tensor(cv[:, i, :], acc[:, 2, :], -1.0 / CONV_CH, cv[:, i, :], ALU.mult, ALU.add)\
                            .then_inc(cent_ready, c.made(cent_ready))
                if u == INV_AT:
                    dve.wait_ge(ln_root, c.next(ln_root))
                    dve.wait_ge(*step(dve.reciprocal(ub[:, 0, 0:SEQ], rt[:, 0:SEQ])))
                if u == SCALE_AT:
                    for i in range(4):
                        dve.tensor_tensor(cv[:, i, :], cv[:, i, :], ub[:, 0, 0:SEQ], ALU.mult)\
                            .then_inc(ln_scaled, c.made(ln_scaled))
                if u == UNITS_A - 1:
                    for i in range(4):
                        dve.wait_ge(ln_act, c.next(ln_act))
                        dve.tensor_tensor(zpad[:, i, 0:SEQ], zpad[:, i, 0:SEQ], cv[:, i, :], ALU.mult)\
                            .then_inc(ln_out, c.made(ln_out))
            for pair in range(3):
                low(4 + pair, qs[:, pair, :])
            for i in range(4):
                low(i, zpad[:, i, 0:SEQ])
            low(7, qs[:, 3, :])
            add_to_x(norm_next=STAGES[-1] != "mix0")

        written = {}

        def add_to_x(cols=SEQ, back=0, norm_next=True):
            for m in range(KT):
                a = full()
                if back:
                    dve.wait_ge(x_back[m], 16 * back)
                if m in written:
                    dve.wait_ge(*written[m])
                xm = x[:, m, ROW] if cols == SEQ else wide(x[:, m, :])
                dve.tensor_tensor(xm, xm, a, ALU.add).then_inc(taken, c.made(taken))
                written[m] = c.mine()
                if norm_next and m:
                    add_square(m - 1, ROW if cols == SEQ else slice(0, T))
            at["squared"] = norm_next

        def log1p(e, tmp, sum_):
            d, s, s2 = tmp
            dve.wait_ge(*step(dve.tensor_scalar(d, e, 2.0, None, ALU.add)))
            dve.wait_ge(*step(dve.reciprocal(d, d)))
            dve.wait_ge(*step(dve.tensor_tensor(s, e, d, ALU.mult)))
            dve.wait_ge(*step(dve.tensor_tensor(s2, s, s, ALU.mult)))
            dve.wait_ge(*step(dve.tensor_scalar(sum_, s2, 1.0 / 17.0, None, ALU.mult)))
            for n in (15, 13, 11, 9, 7, 5, 3):
                dve.wait_ge(*step(dve.scalar_tensor_tensor(sum_, sum_, 1.0 / n, s2, ALU.add, ALU.mult)))
            dve.wait_ge(*step(dve.scalar_tensor_tensor(sum_, sum_, 1.0, s, ALU.add, ALU.mult)))
            dve.wait_ge(*step(dve.tensor_scalar(sum_, sum_, 2.0, None, ALU.mult)))

        def mixer1():
            lam = v1[:, V1["c_lambda"][0]:V1["c_lambda"][1]]
            dve.wait_ge(*step(dve.tensor_scalar(c8[:, 2, :], lam, -1.0, 0.0, ALU.mult, ALU.max)))
            dve.wait_ge(*step(dve.tensor_scalar(c8[:, 0, :], lam, -1.0, None, ALU.mult)))
            dve.tensor_tensor(c8[:, 0, :], c8[:, 0, :], lam, ALU.max).then_inc(rate_in, c.made(rate_in))
            dve.wait_ge(rate_ready, c.next(rate_ready))
            log1p(c8[:, 1, :], (c8[:, 3, :], c8[:, 4, :], c8[:, 5, :]), c8[:, 0, :])
            dve.wait_ge(*step(dve.tensor_tensor(c8[:, 2, :], c8[:, 2, :], c8[:, 0, :], ALU.add)))
            dve.wait_ge(*step(dve.tensor_scalar(c8[:, 2, :], c8[:, 2, :], 8.0, None, ALU.mult)))
            dve.tensor_scalar(c8[:, 3, :], c8[:, 2, :], -1.0, None, ALU.mult).then_inc(rate_in, c.made(rate_in))
            norm(lambda k: vec("mix_norm", 8 + k), SEQ)
            for h in range(KT):
                a = full()
                dve.tensor_tensor(ub[:, h % 2, 0:SEQ], a, scale[:, ROW], ALU.mult).then_inc(taken, c.made(taken))
                for j in range(LRU_W):
                    w = vec("c_conv_w", LRU_W * h + j)
                    src = ubp[:, h % 2, PAD - LRU_W + 1 + j:PAD - LRU_W + 1 + j + SEQ]
                    dve.wait_ge(*c.mine())
                    if j == 0:
                        step(dve.tensor_scalar(xc[:, h, :], src, w, vec("c_conv_b", h),
                                               ALU.mult, ALU.add))
                    else:
                        t = dve.scalar_tensor_tensor(xc[:, h, :], src, w, xc[:, h, :],
                                                     ALU.mult, ALU.add)
                        t.then_inc(xc_ready if j == LRU_W - 1 else dve_seq,
                                   c.made(xc_ready if j == LRU_W - 1 else dve_seq))
            for h in range(KT):
                a = full()
                s = sb_[:, h % 2, 0:SEQ]
                dve.tensor_tensor(gb[:, h, :], a, scale[:, ROW], ALU.mult).then_inc(taken, c.made(taken))
                dve.wait_ge(*c.mine())
                dve.wait_ge(*step(dve.tensor_tensor(s, gb[:, h, :], gb[:, h, :], ALU.mult)))
                dve.wait_ge(*step(dve.tensor_scalar(s, s, 0.044715, 1.0, ALU.mult, ALU.add)))
                dve.tensor_tensor(s, s, gb[:, h, :], ALU.mult).then_inc(g_ready, c.made(g_ready))
                dve.wait_ge(ri_sig, c.next(ri_sig))
                dve.tensor_tensor(xc[:, h, :], xc[:, h, :], ub[:, h % 2, 0:SEQ], ALU.mult)\
                    .then_inc(xc_gated, c.made(xc_gated))
                dve.wait_ge(gsig_ready, c.next(gsig_ready))
                step(dve.tensor_tensor(gb[:, h, :], gb[:, h, :], s, ALU.mult))
            for h in range(KT):
                dve.wait_ge(a_ready, c.next(a_ready))
                dve.wait_ge(*step(dve.tensor_tensor(ub[:, h % 2, 0:SEQ], rb[:, h, :], rb[:, h, :], ALU.mult)))
                dve.scalar_tensor_tensor(tb[:, h, :], ub[:, h % 2, 0:SEQ], 1.0, tb[:, h, :], ALU.add, ALU.mult)\
                    .then_inc(m_ready, c.made(m_ready))

            def y_low(h):
                dve.wait_ge(y_hi, c.next(y_hi))
                dve.tensor_tensor(nl[:, h, ROW], xc[:, h, :], nh[:, h, ROW].bitcast(F32), ALU.subtract)\
                    .then_inc(y_ready, c.made(y_ready))

            for h in range(KT):
                dve.wait_ge(mult_ready, c.next(mult_ready))
                dve.wait_ge(*step(dve.tensor_tensor(xc[:, h, :], xc[:, h, :], tb[:, h, :], ALU.mult)))
                dve.wait_ge(*step(dve.tensor_tensor_scan(tb[:, h, :], rb[:, h, :], xc[:, h, :], 0.0,
                                                         ALU.mult, ALU.add)))
                dve.tensor_tensor(xc[:, h, :], tb[:, h, :], gb[:, h, :], ALU.mult).then_inc(yc_ready, c.made(yc_ready))
                if h:
                    y_low(h - 1)
            y_low(KT - 1)
            add_to_x(norm_next=STAGES[-1] != "mix1")

        def mlp1(layer):
            norm(lambda k: vec("mlp_norm", 8 * layer + k), SEQ)
            waiting = []

            def low():
                q, m = waiting.pop(0)
                dve.wait_ge(h_hi, c.next(h_hi))
                dve.tensor_tensor(hid_lo[:, q % 2, m, ROW], sb_[:, m % 2, 0:SEQ],
                                  hid_hi[:, q % 2, m, ROW].bitcast(F32), ALU.subtract)\
                    .then_inc(h_ready, c.made(h_ready))

            for what, q in mlp_order():
                if what == "down":
                    add_to_x(norm_next=q == QUARTERS - 1 and STAGES[-1] != f"mlp{layer}")
                    continue
                for m in range(KT):
                    a = full()
                    u = ub[:, m % 2, 0:SEQ]
                    dve.scalar_tensor_tensor(u, a, 0.0, scale[:, ROW], ALU.max, ALU.mult)\
                        .then_inc(taken, c.made(taken))
                    if waiting:
                        low()
                    dve.wait_ge(taken, c.at(taken))
                    dve.tensor_tensor(sb_[:, m % 2, 0:SEQ], u, u, ALU.mult).then_inc(h_sq, c.made(h_sq))
                    waiting.append((q, m))
                low()

        def row_scales():
            dve.wait_ge(droot_ready, c.next(droot_ready))
            dve.reciprocal(rt[0:8, :], rt[0:8, :]).then_inc(dinv_ready, c.made(dinv_ready))

        def layer(l):
            def vec(name, n=0, count=1):
                return vec2_(l, name, n, count)

            norm(lambda k: vec("norm_mix_2", k), T)
            wscale = wide(scale[:, :])
            a = full()
            dve.tensor_tensor(wide(ub[0:16, 0, :]), a[0:16], wide(scale[0:16, :]), ALU.mult)\
                .then_inc(taken, c.made(taken))
            for t in [ik[:, :]] + [iq[:, i, :] for i in range(4)] + [bq[:, i, :] for i in range(4)] \
                    + [bk[:, :], bv[:, :]]:
                a = full()
                dve.tensor_tensor(wide(t), a, wscale, ALU.mult).then_inc(taken, c.made(taken))
            dve.wait_ge(rates_full, c.next(rates_full))
            dve.wait_ge(*step(dve.tensor_copy(abt[:, :, :], aux[:, 2, 0:16 * UNITS].rearrange("p (u n) -> p u n", u=UNITS))))
            step(dve.tensor_scalar(abt[:, :, 8:16], abt[:, :, 8:16], (IDX_HEADS * 64) ** -0.5, None, ALU.mult))

            def by_unit(n):
                return gt[:, n, :].rearrange("p (u h) -> p u h", h=4)

            def all_units(a):
                return a.rearrange("p (o h) -> p o h", o=1).to_broadcast([P, UNITS, 4])

            dve.wait_ge(*step(dve.tensor_tensor(by_unit(2), abt[:, :, 0:4], all_units(vec("dt_bias_2", 0, 4)), ALU.add)))
            dve.wait_ge(*step(dve.tensor_scalar(gt[:, 3, :], gt[:, 2, :], -1.0, None, ALU.mult)))
            dve.tensor_tensor(gt[:, 3, :], gt[:, 3, :], gt[:, 2, :], ALU.max).then_inc(abe_in, c.made(abe_in))
            row_scales()
            dve.wait_ge(abe_out, c.next(abe_out))
            log1p(gt[:, 4, :], (gt[:, 5, :], gt[:, 6, :], gt[:, 7, :]), gt[:, 8, :])
            dve.wait_ge(*step(dve.scalar_tensor_tensor(gt[:, 2, :], gt[:, 2, :], 0.0, gt[:, 8, :], ALU.max, ALU.add)))
            dve.wait_ge(*step(dve.scalar_tensor_tensor(by_unit(1), by_unit(2), -1.0, all_units(gt[:, 9, 0:4]),
                                                       ALU.mult, ALU.mult)))
            is_meta = const("is_meta")[:, 0:1]
            step(dve.tensor_scalar(gt[:, 1, 0:4], gt[:, 1, 0:4], is_meta, None, ALU.mult))
            dve.tensor_scalar(gt[:, 0, 0:4], gt[:, 0, 0:4], is_meta, None, ALU.mult).then_inc(g_in, c.made(g_in))

            pending = []

            def silu():
                t, b = pending.pop(0)
                dve.wait_ge(csig, c.next(csig))
                dve.tensor_tensor(t, t, sb_[:, b, :], ALU.mult).then_inc(silu_out, c.made(silu_out))

            def delta_tile(n):
                a = full()
                t = ((dk, dq, dv)[n % 3])[:, n // 3, :]
                tile = (4, 0, 8)[n % 3] + n // 3
                dve.tensor_tensor(wide(ub[:, n % 2, :]), a, wscale, ALU.mult).then_inc(taken, c.made(taken))
                for j in range(4):
                    w = vec("conv_a_2", 4 * tile + j)
                    src = ubp[:, n % 2, PAD - 3 + j:PAD - 3 + j + T]
                    dve.wait_ge(*c.mine())
                    if j == 0:
                        step(dve.tensor_scalar(t, src, w, None, ALU.mult))
                    else:
                        s = silu_in if j == 3 else dve_seq
                        dve.scalar_tensor_tensor(t, src, w, t, ALU.mult, ALU.add).then_inc(s, c.made(s))
                pending.append((t, n % 2))
                if len(pending) > 1:
                    silu()

            delta_tile(0)
            delta_tile(1)
            tiles = [(ik[:, :], "i", 0)] + [(iq[:, i, :], "i", None) for i in range(4)] \
                + [(bq[:, i, :], "a", 1 + i) for i in range(4)] + [(bk[:, :], "a", 5)]
            for n, (t, which, row) in enumerate(tiles):
                dve.wait_ge(rot_full, c.next(rot_full))
                step(dve.tensor_tensor(wide(ssq[:, :]), aux[:, 0:2, 0:HALF], wide(const("sin_" + which)), ALU.mult))
                dve.wait_ge(*step(dve.tensor_tensor(t, t, const("cos_" + which), ALU.mult)))
                i = dve.tensor_tensor(t, t, ssq[:, :], ALU.add)
                if row is not None:
                    dve.wait_ge(*step(i))
                    i = dve.tensor_tensor(wide(t), wide(t), aux[:, 2:4, 0:HALF], ALU.mult)
                i.then_inc(rope_done, c.made(rope_done))
                delta_tile(2 + n)
            silu()
            n = 0
            latest = {}
            for j in range(1, 4):
                for h in range(IDX_HEADS):
                    w = P * (j + 1)
                    iw, s = abt[:, j + 1, 8 + h:9 + h], score[:, j - 1, 0:w]
                    dve.wait_ge(irelu, c.next(irelu))
                    if h == 0:
                        dve.tensor_scalar(s, sqb[:, n % 2, 0:w], iw, None, ALU.mult).then_inc(iscore, c.made(iscore))
                    else:
                        dve.wait_ge(iscore, c.at(iscore))
                        dve.scalar_tensor_tensor(s, sqb[:, n % 2, 0:w], iw, s, ALU.mult, ALU.add)\
                            .then_inc(iscore, c.made(iscore))
                    n += 1

            def gate_tile(m):
                a = full()
                dve.tensor_tensor(wide(x[:, m, :]), a, wscale, ALU.mult).then_inc(taken, c.made(taken))

            def l2_scale(n):
                t = dq[:, n, :] if n < 4 else dk[:, n - 4, :]
                dve.wait_ge(lbc_full, c.next(lbc_full))
                b = aux[:, 2 * (n % 2):2 * (n % 2) + 2, 0:HALF]
                dve.scalar_tensor_tensor(wide(t), wide(t), P ** -0.5 if n < 4 else 1.0, b, ALU.mult, ALU.mult)\
                    .then_inc(lnormed, c.made(lnormed))

            def decay_sums():
                dve.wait_ge(gcol_full, c.next(gcol_full))
                dve.wait_ge(*step(dve.tensor_copy(gt[:, 3, :], aux[:, 0, 0:20])))
                dve.tensor_tensor(gt[:, 4, :], aux[:, 0, 32:52], gt[:, 3, :], ALU.subtract).then_inc(g_in, c.made(g_in))

            def between(round_):
                if round_ == 0:
                    dve.wait_ge(x_saved, 16 * (l + 1))
                if round_ == 3:
                    row_scales()
                if round_ in (5, 7, 9, 11):
                    m = (round_ - 5) // 2
                    gate_tile(m)
                    l2_scale(2 * m)
                    l2_scale(2 * m + 1)
                if round_ == 12:
                    decay_sums()

            top_keys(between)
            dve.wait_ge(abe_out, c.next(abe_out))
            dve.wait_ge(*step(dve.tensor_tensor(gt[:, 7, :], gt[:, 0, :], gt[:, 5, :], ALU.mult)))
            attention()
            dve.memset(state[:, :, :], 0.0).then_inc(us_ready, c.made(us_ready))
            filled = []

            def fill_result():
                f = len(filled)
                if f >= A_HEADS:
                    gate_tile(TOP_GATES + f - A_HEADS)
                else:
                    a = full()
                    dve.tensor_tensor(wide(dz[:, f, :]), a, wscale, ALU.mult).then_inc(taken, c.made(taken))
                    pending.append((dz[:, f, :], f % 2))
                filled.append(f)

            for u in range(UNITS):
                unit(u, fill_result, lambda: silu() if pending else None)
            row_scales()
            for h in range(4):
                dve.wait_ge(lbc_full, c.next(lbc_full))
                b = aux[:, 2 * (h % 2):2 * (h % 2) + 2, 0:HALF]
                dve.scalar_tensor_tensor(wide(dq[:, h, :]), wide(dq[:, h, :]), vec("a_out_norm_2"), b,
                                         ALU.mult, ALU.mult).then_inc(onorm_ready, c.made(onorm_ready))
                dve.wait_ge(*c.mine())
                dve.tensor_tensor(dq[:, h, :], dq[:, h, :], dz[:, h, :], ALU.mult).then_inc(oz_ready, c.made(oz_ready))
            for k in range(8):
                dve.wait_ge(o_hi, c.next(o_hi))
                src = dq[:, k, :] if k < 4 else ob[:, k - 4, :]
                dve.tensor_tensor(ol[:, k, :], src, oh[:, k, :].bitcast(F32), ALU.subtract)\
                    .then_inc(o_ready, c.made(o_ready))
            dve.wait_ge(gate_kept, c.next(gate_kept, KT))

            def second_gate(m):
                a = full()
                dve.tensor_tensor(wide(ub[:, m % 2, :]), a, wscale, ALU.mult).then_inc(taken, c.made(taken))

            second_gate(0)
            for m in range(KT):
                if m + 1 < KT:
                    second_gate(m + 1)
                if m:
                    mixed_low(m - 1)
                full()
                dve.wait_ge(gate_sig, c.next(gate_sig))
                if m:
                    dve.wait_ge(mix_lo, c.at(mix_lo))
                step(dve.tensor_tensor(wide(sqb[:, 0, :]), aux[:, 0:2, 0:HALF], wide(x[:, m, :]), ALU.mult))
                dve.tensor_tensor(wide(sqb[:, 1, :]), aux[:, 2:4, 0:HALF], wide(sb_[:, m % 2, :]), ALU.mult)\
                    .then_inc(taken, c.made(taken))
                dve.wait_ge(*c.mine())
                dve.tensor_tensor(sqb[:, 0, :], sqb[:, 0, :], sqb[:, 1, :], ALU.add)\
                    .then_inc(mix_ready, c.made(mix_ready))
            mixed_low(KT - 1)
            add_to_x(T, l + 1)
            norm(lambda k: vec("norm_ffn_2", k), T)
            waiting = []

            def low():
                g, i, b = waiting.pop(0)
                dve.wait_ge(h_hi, c.next(h_hi))
                dve.tensor_tensor(hid_lo[:, g % 2, i, :], sb_[:, b, :], hid_hi[:, g % 2, i, :].bitcast(F32),
                                  ALU.subtract).then_inc(h_ready, c.made(h_ready))

            for what, g in FFN_ORDER:
                if what == "down":
                    add_to_x(T, norm_next=(what, g) == FFN_ORDER[-1] and STAGES[-1] != f"layer{l}")
                    continue
                for i in range(*FFN_THIRDS[g]):
                    b = i % 2
                    a = full()
                    dve.tensor_tensor(wide(ub[:, b, :]), a, wscale, ALU.mult).then_inc(taken, c.made(taken))
                    if waiting:
                        low()
                    for j in range(3):
                        w = vec("conv_ffn_2", 3 * i + j)
                        src = ubp[:, b, PAD - 2 + j:PAD - 2 + j + T]
                        dve.wait_ge(*c.mine())
                        if j == 0:
                            step(dve.tensor_scalar(sb_[:, b, :], src, w, None, ALU.mult))
                        else:
                            s = silu_in if j == 2 else dve_seq
                            dve.scalar_tensor_tensor(sb_[:, b, :], src, w, sb_[:, b, :], ALU.mult, ALU.add)\
                                .then_inc(s, c.made(s))
                    a = full()
                    dve.wait_ge(silu_in, c.at(silu_in))
                    dve.tensor_tensor(wide(ub[:, b, :]), a, wscale, ALU.mult).then_inc(taken, c.made(taken))
                    dve.wait_ge(csig, c.next(csig))
                    dve.wait_ge(*step(dve.tensor_tensor(sb_[:, b, :], sb_[:, b, :], sqb[:, b, :], ALU.mult)))
                    dve.tensor_tensor(sb_[:, b, :], sb_[:, b, :], ub[:, b, :], ALU.mult).then_inc(h_sq, c.made(h_sq))
                    waiting.append((g, i - FFN_THIRDS[g][0], b))
                low()

        def mixed_low(m):
            dve.wait_ge(mix_hi, c.next(mix_hi))
            dve.tensor_tensor(yl[:, m, :], sqb[:, 0, :], yh[:, m, :].bitcast(F32), ALU.subtract)\
                .then_inc(mix_lo, c.made(mix_lo))

        def top_keys(between):
            latest = {}
            dve.wait_ge(iscore, c.at(iscore))
            for j in range(1, 4):
                latest[j] = step(dve.memset(score[0:64, j - 1, P * j + 64:P * j + P], -BIG))
            for round_ in range(TOPK // 8):
                between(round_)
                for j in range(1, 4):
                    s = score[:, j - 1, 0:P * (j + 1)]
                    dve.wait_ge(*latest[j])
                    latest[j] = step(dve.max(best[:, j - 1, :], s))
                for j in range(1, 4):
                    s = score[:, j - 1, 0:P * (j + 1)]
                    dve.wait_ge(*latest[j])
                    latest[j] = step(dve.match_replace(s, best[:, j - 1, :], s, MARK))
            for j in range(4):
                o = SEL_AT[j]
                step(dve.memset(selb[:, o:o + META], 0.0))
                if j == 0:
                    step(dve.tensor_copy(selb[:, o + META:SEL_AT[1]], const("ahead")))
                else:
                    dve.wait_ge(*latest[j])
                    step(dve.tensor_scalar(selb[:, o + META:SEL_AT[j + 1]], score[:, j - 1, 0:P * (j + 1)], MARK, -BIG,
                                           ALU.not_equal, ALU.mult))
            dve.wait_ge(*c.mine())

        def per_head(a):
            return a.rearrange("p (o i) -> p o i", o=1).to_broadcast([P, A_HEADS, P])

        def per_token(n, u):
            return gt[:, n, 4 * u:4 * u + 4].rearrange("p (h o) -> p h o", o=1).to_broadcast([P, A_HEADS, P])

        def by_head(bank):
            return bank.rearrange("p (h i) -> p h i", h=A_HEADS)

        def unit(u, fill_result, silu):
            cs = slice(first(u), first(u) + P)
            dve.wait_ge(egr_ready, c.next(egr_ready))
            for h in range(A_HEADS):
                i = dve.tensor_scalar(dt[:, h, :], aux[:, 0, P * h:P * h + P], gt[:, 3, 4 * u + h:4 * u + h + 1], 0.0,
                                      ALU.subtract, ALU.min)
                s = udt if h == A_HEADS - 1 else dve_seq
                i.then_inc(s, c.made(s))
            dve.wait_ge(ukq_full, c.next(ukq_full))
            dve.wait_ge(*step(dve.tensor_copy(mt[:, :, :], by_head(aux[:, 2, :]))))
            dve.wait_ge(*step(dve.tensor_tensor(mt[:, :, :], mt[:, :, :], by_head(aux[:, 1, :]), ALU.mult)))
            dve.wait_ge(udt_exp, c.next(udt_exp))
            dve.wait_ge(*step(dve.tensor_tensor(mt[:, :, :], mt[:, :, :], dt[:, :, :], ALU.mult)))
            dve.wait_ge(*step(dve.tensor_tensor(xit[:, :, :], mt[:, :, :], per_head(const("join_0")), ALU.mult)))
            dve.tensor_tensor(xit[:, :, :], per_head(ident), xit[:, :, :], ALU.subtract).then_inc(ux_ready, c.made(ux_ready))
            dve.wait_ge(*c.mine())
            dve.tensor_tensor(ct[:, :, :], mt[:, :, :], per_head(const("join_1")), ALU.mult)\
                .then_inc(uct_ready, c.made(uct_ready))

            def token_side():
                dve.wait_ge(utok_full, c.next(utok_full))
                step(dve.tensor_tensor(kbg[:, :, :], by_head(acc[:, 2, :]), per_token(7, u), ALU.mult))
                step(dve.tensor_tensor(kg[:, :, :], by_head(acc[:, 2, :]), per_token(6, u), ALU.mult))
                dve.tensor_tensor(vb[:, :, :], by_head(acc[:, 3, :]), per_token(0, u), ALU.mult)\
                    .then_inc(utok_ready, c.made(utok_ready))

            def query_side():
                dve.wait_ge(*step(dve.tensor_tensor(dt[:, :, :], dt[:, :, :], per_head(const("until")), ALU.mult)))
                step(dve.tensor_tensor(qkt[:, :, :], by_head(aux[:, 3, :]), dt[:, :, :], ALU.mult))
                dve.tensor_tensor(qg[:, :, :], dq[:, :, cs], egr[:, :, :], ALU.mult).then_inc(uq_ready, c.made(uq_ready))

            for n in range(1, LEVELS):
                if (n == 1 and 0 < u <= FILLED) or (n == LEVELS - 1 and u < FILLED):
                    fill_result()
                if n == 2:
                    silu()
                if n < LEVELS - 1:
                    dve.wait_ge(up1_full, c.next(up1_full))
                    dve.tensor_tensor(ct[:, :, :], mt[:, :, :], per_head(const(f"join_{n + 1}")), ALU.mult)\
                        .then_inc(uct_ready, c.made(uct_ready))
                    dve.wait_ge(uxi_full, c.next(uxi_full))
                    dve.tensor_tensor(xi[:, :, :], xi[:, :, :], by_head(aux[:, 1, :]), ALU.subtract)\
                        .then_inc(uxi_ready, c.made(uxi_ready))
                else:
                    c.next(up1_full)
                dve.wait_ge(uz_full, c.next(uz_full))
                dve.tensor_tensor(xit[:, :, :], xit[:, :, :], by_head(aux[:, 2, :]), ALU.subtract)\
                    .then_inc(uinv_ready, c.made(uinv_ready))
                if n == 1:
                    token_side()
                if n == 2:
                    query_side()
                dve.wait_ge(uinv_ready, c.at(uinv_ready))
            chunks = 1 if u == 0 else 2
            silu()
            for cc in range(chunks):
                dve.wait_ge(uso_full, c.next(uso_full))
                for h in range(A_HEADS):
                    i = dve.scalar_tensor_tensor(state_of(u, cc + 1)[:, h, :], state_of(u, cc)[:, h, :], egr[:, h, 64 * cc + 63:64 * cc + 64],
                                                 aux[:, 1, P * h:P * h + P], ALU.mult, ALU.add)
                    s = us_ready if h == A_HEADS - 1 else dve_seq
                    i.then_inc(s, c.made(s))
                dve.wait_ge(*c.mine())
            n = P if u else META
            dve.wait_ge(uout_full, c.next(uout_full))
            dve.tensor_copy(dq[:, :, first(u):first(u) + n], by_head(aux[:, 3, :])[:, :, 0:n])\
                .then_inc(uo_done, c.made(uo_done))
            dve.wait_ge(*c.mine())

        def attention():
            def shift(j, h):
                w, o = META + P * (j + 1), SEL_AT[j]
                dve.wait_ge(bs_full, c.next(bs_full))
                dve.wait_ge(*step(dve.tensor_tensor_reduce(
                    pb[:, h, 0:w].rearrange("p (s t) -> p s t", s=2), aux[:, 2 * (h % 2):2 * (h % 2) + 2, 0:w // 2],
                    selb[:, o:o + w].rearrange("p (s t) -> p s t", s=2), 1.0, MARK, ALU.add, ALU.max,
                    row4[:, 0, h:h + 1])))
                dve.tensor_scalar(row4[:, 1, h:h + 1], row4[:, 0, h:h + 1], -P ** -0.5, None, ALU.mult)\
                    .then_inc(bshift, c.made(bshift))

            def normalise(j, h):
                w = META + P * (j + 1)
                dve.wait_ge(bexp, c.next(bexp))
                dve.wait_ge(*step(dve.reciprocal(row4[:, 3, h:h + 1], row4[:, 2, h:h + 1])))
                dve.tensor_scalar(pb[:, h, 0:w], pb[:, h, 0:w], row4[:, 3, h:h + 1], None, ALU.mult)\
                    .then_inc(bp_ready, c.made(bp_ready))

            for j in range(4):
                if j:
                    dve.wait_ge(bt_full, c.next(bt_full, j + 1))
                for h in range(B_HEADS):
                    shift(j, h)
                    if h:
                        normalise(j, h - 1)
                normalise(j, B_HEADS - 1)
            dve.wait_ge(bt_full, c.next(bt_full, 5))
            dve.wait_ge(bs_full, c.next(bs_full))
            s = aux[0:META, 0, 0:4 * META].rearrange("p (h k) -> p h k", h=4)
            pm = pb[0:META, :, 0:META]

            def bc(n):
                return row4[0:META, n, :].rearrange("p (h o) -> p h o", o=1).to_broadcast([META, 4, META])

            dve.wait_ge(*step(dve.tensor_reduce(row4[0:META, 0, :], s, AX.X, ALU.max)))
            dve.tensor_tensor(pm, s, bc(0), ALU.subtract).then_inc(bshift, c.made(bshift))
            dve.wait_ge(bexp, c.next(bexp))
            dve.wait_ge(*step(dve.tensor_reduce(row4[0:META, 2, :], pm, AX.X, ALU.add)))
            dve.wait_ge(*step(dve.reciprocal(row4[0:META, 3, :], row4[0:META, 2, :])))
            dve.tensor_tensor(pm, pm, bc(3), ALU.mult).then_inc(bp_ready, c.made(bp_ready))
            c.next(bt_full)

        step(dve.memset(ubp[:, :, 0:PAD], 0.0))
        dve.memset(eps[:, :], EPS).then_inc(dve_seq, c.made(dve_seq))
        dve.memset(zpad[:, :, 0:CONV_W - 1], 0.0).then_inc(pad_clear, c.made(pad_clear))
        dve.wait_ge(*c.mine())
        dve.wait_ge(loaded, 32)
        for stage in STAGES:
            if stage == "mix0":
                mixer0()
            if stage == "mix1":
                mixer1()
            if stage in ("mlp0", "mlp1"):
                mlp1(int(stage[-1]))
            if stage == "final":
                norm(None, SEQ)
                for k in range(KT):
                    dve.scalar_tensor_tensor(x[:, k, ROW], x[:, k, ROW], vec("final_norm", k), scale[:, ROW],
                                             ALU.mult, ALU.mult).then_inc(x_final, c.made(x_final))
            elif stage in ("layer0", "layer1"):
                layer(int(stage[-1]))

    block.__exit__(None, None, None)


def distances(np):
    p = np.arange(P)[:, None]
    s = np.arange(SEQ)[None, :] - (SEQ - P)
    return np.where(s <= p, s - p, -BIG).astype(np.float32)


def tables1(np):
    return np.concatenate([np.eye(P), np.ones((P, P))], axis=1).astype(np.float32)


def tables2(np):
    f32 = np.float32
    p, i = np.arange(P)[:, None], np.arange(P)[None, :]
    parts = {}
    for name, dim in (("a", P), ("i", 64)):
        half = dim // 2
        inv = (f32(1.0) / (f32(10000.0) ** (np.arange(0, dim, 2, dtype=f32) / f32(dim)))).astype(f32)
        angle = (np.arange(T, dtype=f32)[:, None] * inv[None, :]).astype(f32)[:, np.arange(P) % half].T
        parts["cos_" + name], parts["sin_" + name] = np.cos(angle), np.sin(angle)
        low = (i % dim) < half
        parts["turn_" + name] = np.where(low & (p == i + half), -1.0, 0.0) + np.where(~low & (p == i - half), 1.0, 0.0)
    same = p // CHUNK == i // CHUNK
    parts["until"], parts["same"] = same & (p <= i), same
    parts["ahead"] = np.where(i // CHUNK > p // CHUNK, -BIG, 0.0)
    for n in range(LEVELS):
        b = 2 ** n
        parts[f"join_{n}"] = ((i // b) % 2 == 1) & (p // b == i // b - 1)
    parts["rows"] = np.tile((np.arange(64) // 8 == np.arange(64) % 8)[None, :], (P, 1))
    parts["is_meta"] = np.tile(p < META, (1, 8))
    return np.concatenate([parts[name].astype(f32) for name, _ in CONST2], axis=1)


def tile_columns(a):
    return a.reshape(-1, P).T


def kernel(**inputs):
    import numpy as np
    import concourse.bacc as bacc
    from concourse.bass_utils import run_bass_kernel_spmd

    a = {name: np.asarray(v) for name, v in inputs.items()}
    weights = dict(a)
    weights["w_branch_2"] = np.concatenate([a["w_branch_a_2"], a["w_branch_b_2"]], axis=1)

    def piece(name, layer, parts):
        out = np.zeros((P, KT * P), np.float32)
        w = weights[name][layer]
        for b, (r, col, n) in enumerate(parts):
            rows = w[r:r + P]
            if col == "ab_iw":
                out[:, P * b:P * b + 8] = rows[:, AA:AA + 8]
                out[:, P * b + 8:P * b + 16] = rows[:, IW:IW + 8]
            elif col == "ik_twice":
                out[:, P * b:P * b + 64] = rows[:, IK:IK + 64]
                out[:, P * b + 64:P * b + 128] = rows[:, IK:IK + 64]
            else:
                out[:, P * b:P * b + n] = rows[:, col:col + n]
        return out

    plan, _ = weight_plan()
    stream = np.stack([piece(*p) for p in plan])
    v1 = [tile_columns(a["mix_norm"]), tile_columns(a["mlp_norm"]), tile_columns(a["final_norm"]),
          a["ab_conv_w"][0].reshape(CONV_W, 4, P).transpose(2, 1, 0).reshape(P, -1),
          tile_columns(a["ab_ln_g"]), tile_columns(a["ab_ln_b"]),
          a["c_conv_w"][0].reshape(LRU_W, KT, P).transpose(2, 1, 0).reshape(P, -1),
          tile_columns(a["c_conv_b"]), tile_columns(a["c_b_r"]), tile_columns(a["c_b_i"]),
          tile_columns(a["c_lambda"])]
    def by_tile(w, taps):
        return w.reshape(taps, -1, P).transpose(2, 1, 0).reshape(P, -1)

    def all_rows(v):
        return np.repeat(v[None, :], P, axis=0)

    v2 = [np.concatenate([
        tile_columns(a["norm_mix_2"][l]), tile_columns(a["norm_ffn_2"][l]), by_tile(a["conv_a_2"][l], 4),
        all_rows(a["a_log_2"][l]), all_rows(a["dt_bias_2"][l]), tile_columns(a["a_out_norm_2"][l]),
        tile_columns(a["q_norm_2"][l]), tile_columns(a["k_norm_2"][l]),
        np.concatenate([a["kidx_norm_2"][l]] * 2)[:, None],
        tile_columns(a["b_gate_2"][l]), by_tile(a["conv_ffn_2"][l], 3)], axis=1) for l in range(2)]
    arrays = {
        "vec2": np.stack(v2, axis=1), "const2": tables2(np), "dist": distances(np),
        "meta": a["meta_tokens_2"].T,
        "stream": stream,
        "xt": a["x"][0].T,
        "vec1": np.concatenate(v1, axis=1),
        "const1": tables1(np),
        "lru_w": np.concatenate([a["c_w_r"][0], a["c_w_i"][0]]).transpose(1, 0, 2),
    }
    arrays = {f"in_{n}": np.ascontiguousarray(v) for n, v in arrays.items()}
    nc = bacc.Bacc("TRN2", target_bir_lowering=False, num_devices=1)
    dram = {n[3:]: nc.dram_tensor(n, v.shape, mybir.dt.from_np(v.dtype), kind="ExternalInput").ap()
            for n, v in arrays.items()}
    out = nc.dram_tensor("out_dram", (D, SEQ), F32, kind="ExternalOutput").ap()
    saved_x = nc.dram_tensor("saved_x", (D, T), F32, kind="Internal").ap()
    build(nc, out=out, saved_x=saved_x, **dram)
    r = run_bass_kernel_spmd(nc, [arrays], core_ids=[0])
    return r.results[0]["out_dram"].T[None]
```
